# Optimizing a Trainium2 kernel written in Bass

```python
import math
import jax, jax.numpy as jnp
from jax import lax
import numpy as np

D_MODEL = 1024
BATCH = 1
SEQ = 256
DEPTH = 2
DEC_BATCH = 8
DEC_SEQ = 1
PAST_LEN = 2048
PAGE_SIZE = 128

GLA_HEADS = 4
GLA_DK = D_MODEL // 2 // GLA_HEADS
GLA_DV = D_MODEL // GLA_HEADS
GLA_RANK = 16
GLA_NORMALIZER = 16.0
GLA_CHUNK = 64
ATT_HEADS = 16
ATT_KV_HEADS = 4
ATT_DH = D_MODEL // ATT_HEADS
IDX_HEADS = 8
IDX_DH = 64
TOPK_MAX = 256
ATT_QBLK = 32
N_BUCKETS = 32
MAX_DISTANCE = 128
N_EXPERTS = 64
TOP_K = 8
N_GROUPS = 8
TOPK_GROUPS = 4
EXPERT_FF = 256
SHARED_FF = 256
ROUTE_SCALE = 2.5
MOE_BLK = 128
EPS = 1e-6

N_GLA_LAYERS = (DEPTH + 1) // 2
N_DSA_LAYERS = DEPTH // 2

kernel_name = 'gla_dsa_moe_hybrid_step'

def rms_norm(x, g):
    xf = x.astype(jnp.float32)
    y = xf * lax.rsqrt(jnp.mean(xf * xf, axis=-1, keepdims=True) + EPS)
    return (y * g.astype(jnp.float32)).astype(x.dtype)

def layer_norm(x, g, b):
    xf = x.astype(jnp.float32)
    mu = jnp.mean(xf, axis=-1, keepdims=True)
    var = jnp.mean(jnp.square(xf - mu), axis=-1, keepdims=True)
    return ((xf - mu) * lax.rsqrt(var + EPS) * g + b).astype(x.dtype)

def ada_mod(c, w, b):
    return jnp.split(jax.nn.silu(c) @ w + b, 6, axis=-1)

def modulate(x, g, shift, scale):
    return rms_norm(x, g) * (1 + scale[:, None, :]) + shift[:, None, :]

def t5_bucket(dist):
    dist = jnp.maximum(dist, 0)
    max_exact = N_BUCKETS // 2
    ratio = jnp.log(jnp.maximum(dist, max_exact).astype(jnp.float32) / max_exact) / math.log(MAX_DISTANCE / max_exact)
    large = jnp.minimum(max_exact + (ratio * (N_BUCKETS - max_exact)).astype(jnp.int32), N_BUCKETS - 1)
    return jnp.where(dist < max_exact, dist, large)

def gla_project(h, w_in, w_g2, b_g2):
    B, T = h.shape[:2]
    hk, hv = GLA_HEADS * GLA_DK, GLA_HEADS * GLA_DV
    q, k, v, r, g1 = jnp.split(h @ w_in, [hk, 2 * hk, 2 * hk + hv, 2 * hk + 2 * hv], axis=-1)
    log_a = jax.nn.log_sigmoid((g1 @ w_g2 + b_g2).astype(jnp.float32)) / GLA_NORMALIZER
    heads = lambda a, d: a.reshape(B, T, GLA_HEADS, d)
    return (heads(q, GLA_DK) * GLA_DK ** -0.5, heads(k, GLA_DK), heads(v, GLA_DV), r,
            heads(log_a, GLA_DK))

def gla_chunked(q, k, v, log_a):
    B, T = q.shape[:2]
    C = GLA_CHUNK
    nc = T // C

    def chunks(a):
        return a.astype(jnp.float32).reshape(B, nc, C, GLA_HEADS, -1).transpose(1, 0, 3, 2, 4)

    tri = jnp.tril(jnp.ones((C, C), dtype=bool))[:, :, None]

    def step(S, inp):
        qc, kc, vc, gc = inp
        b = jnp.cumsum(gc, axis=2)
        decay = jnp.exp(jnp.where(tri, b[:, :, :, None, :] - b[:, :, None, :, :], -jnp.inf))
        att = jnp.einsum('bhtd,bhsd,bhtsd->bhts', qc, kc, decay)
        o = jnp.einsum('bhts,bhsv->bhtv', att, vc) + jnp.einsum('bhtd,bhdv->bhtv', qc * jnp.exp(b), S)
        b_end = b[:, :, -1:, :]
        S = jnp.exp(b_end[:, :, 0, :, None]) * S + jnp.einsum('bhsd,bhsv->bhdv', kc * jnp.exp(b_end - b), vc)
        return S, o

    S0 = jnp.zeros((B, GLA_HEADS, GLA_DK, GLA_DV), jnp.float32)
    S, o = lax.scan(step, S0, (chunks(q), chunks(k), chunks(v), chunks(log_a)))
    return o.transpose(1, 0, 3, 2, 4).reshape(B, T, GLA_HEADS, GLA_DV), S

def gla_recurrent(q, k, v, log_a, S0):
    def step(S, inp):
        qt, kt, vt, gt = inp
        S = jnp.exp(gt)[..., None] * S + kt[..., :, None] * vt[..., None, :]
        return S, jnp.einsum('bhd,bhdv->bhv', qt, S)

    xs = tuple(a.astype(jnp.float32).swapaxes(0, 1) for a in (q, k, v, log_a))
    S, o = lax.scan(step, S0.astype(jnp.float32), xs)
    return o.swapaxes(0, 1), S

def gla_mixer(h, state, w_in, w_g2, b_g2, gnorm, w_out):
    B, T = h.shape[:2]
    q, k, v, r, log_a = gla_project(h, w_in, w_g2, b_g2)
    if state is None:
        o, S = gla_chunked(q, k, v, log_a)
    else:
        o, S = gla_recurrent(q, k, v, log_a, state)
    o = rms_norm(o.astype(h.dtype), gnorm).reshape(B, T, GLA_HEADS * GLA_DV) * jax.nn.silu(r)
    return o @ w_out, S

def dsa_project(h, w_in, ln_g, ln_b):
    B, T = h.shape[:2]
    nq, nkv, nqi = ATT_HEADS * ATT_DH, ATT_KV_HEADS * ATT_DH, IDX_HEADS * IDX_DH
    cuts = [nq, nq + nkv, nq + 2 * nkv, nq + 2 * nkv + nqi, nq + 2 * nkv + nqi + IDX_DH]
    q, k, v, qi, ki, wi = jnp.split(h @ w_in, cuts, axis=-1)
    return (q.reshape(B, T, ATT_HEADS, ATT_DH), k.reshape(B, T, ATT_KV_HEADS, ATT_DH),
            v.reshape(B, T, ATT_KV_HEADS, ATT_DH), qi.reshape(B, T, IDX_HEADS, IDX_DH),
            layer_norm(ki, ln_g, ln_b), wi)

def indexer_scores(qi, wi, ki):
    logits = jnp.einsum('bthd,bsd->bths', qi, ki).astype(jnp.float32) * IDX_DH ** -0.5
    return jnp.einsum('bths,bth->bts', jax.nn.relu(logits), wi.astype(jnp.float32) * IDX_HEADS ** -0.5)

def sparse_attend(q, k_sel, v_sel, valid, dist, rel_bias):
    B, Tq = q.shape[:2]
    G = ATT_HEADS // ATT_KV_HEADS
    qg = q.reshape(B, Tq, ATT_KV_HEADS, G, ATT_DH)
    logits = jnp.einsum('btkgd,btskd->btkgs', qg, k_sel).astype(jnp.float32) * ATT_DH ** -0.5
    bias = rel_bias[t5_bucket(dist)].astype(jnp.float32)
    bias = bias.reshape(B, Tq, -1, ATT_KV_HEADS, G).transpose(0, 1, 3, 4, 2)
    logits = jnp.where(valid[:, :, None, None, :], logits + bias, -jnp.inf)
    p = jax.nn.softmax(logits, axis=-1).astype(v_sel.dtype)
    o = jnp.einsum('btkgs,btskd->btkgd', p, v_sel)
    return o.reshape(B, Tq, ATT_HEADS * ATT_DH)

def dsa_mixer_prompt(h, rel_bias, w_in, ln_g, ln_b, w_out):
    q, k, v, qi, ki, wi = dsa_project(h, w_in, ln_g, ln_b)
    B, T = h.shape[:2]
    topk = min(TOPK_MAX, T // 4)
    n_blk = T // ATT_QBLK
    pos_k = jnp.arange(T)
    bidx = jnp.arange(B)[:, None, None]

    def block(i):
        t0 = i * ATT_QBLK
        sl = lambda a: lax.dynamic_slice_in_dim(a, t0, ATT_QBLK, axis=1)
        pos_q = t0 + jnp.arange(ATT_QBLK)
        causal = (pos_k[None, :] <= pos_q[:, None])[None]
        sc = jnp.where(causal, indexer_scores(sl(qi), sl(wi), ki), -jnp.inf)
        _, idx = lax.top_k(sc, topk)
        return sparse_attend(sl(q), k[bidx, idx], v[bidx, idx], idx <= pos_q[None, :, None],
                             pos_q[None, :, None] - idx, rel_bias)

    o = lax.map(block, jnp.arange(n_blk))
    o = jnp.swapaxes(o, 0, 1).reshape(B, T, ATT_HEADS * ATT_DH)
    return o @ w_out, (k, v, ki)

def dsa_mixer_sample(h, cache_k, cache_v, cache_ki, page_table, rel_bias, w_in, ln_g, ln_b, w_out):
    q, k, v, qi, ki, wi = dsa_project(h, w_in, ln_g, ln_b)
    B, T = h.shape[:2]
    past = page_table.shape[1] * PAGE_SIZE
    L = past + T
    topk = min(TOPK_MAX, L // 4)
    ki_past = cache_ki[page_table].reshape(B, past, IDX_DH)
    ki_all = jnp.concatenate([ki_past, ki.astype(ki_past.dtype)], axis=1)
    pos_q = past + jnp.arange(T)
    pos_k = jnp.arange(L)
    causal = (pos_k[None, :] <= pos_q[:, None])[None]
    sc = jnp.where(causal, indexer_scores(qi, wi, ki_all), -jnp.inf)
    _, idx = lax.top_k(sc, topk)
    bidx = jnp.arange(B)[:, None, None]
    pidx = jnp.minimum(idx, past - 1)
    phys = page_table[bidx, pidx // PAGE_SIZE] * PAGE_SIZE + pidx % PAGE_SIZE
    nidx = jnp.clip(idx - past, 0, T - 1)
    in_past = (idx < past)[..., None, None]
    k_sel = jnp.where(in_past, cache_k.reshape(-1, ATT_KV_HEADS, ATT_DH)[phys], k[bidx, nidx])
    v_sel = jnp.where(in_past, cache_v.reshape(-1, ATT_KV_HEADS, ATT_DH)[phys], v[bidx, nidx])
    o = sparse_attend(q, k_sel, v_sel, idx <= pos_q[None, :, None], pos_q[None, :, None] - idx, rel_bias)
    return o @ w_out, (k, v, ki)

def swiglu(x, w_g, w_u, w_d):
    return (jax.nn.silu(x @ w_g) * (x @ w_u)) @ w_d

def routed_experts(x, eidx, wsel, w_gate, w_up, w_down):
    N = x.shape[0]
    A = N * TOP_K
    e_flat = eidx.reshape(A)
    tok_flat = jnp.arange(A, dtype=jnp.int32) // TOP_K
    w_flat = wsel.reshape(A)
    order = jnp.argsort(e_flat)
    e_s, tok_s, w_s = e_flat[order], tok_flat[order], w_flat[order]
    counts = jnp.zeros((N_EXPERTS,), jnp.int32).at[e_flat].add(1)
    start = jnp.cumsum(counts) - counts
    padded = (counts + MOE_BLK - 1) // MOE_BLK * MOE_BLK
    pad_end = jnp.cumsum(padded)
    pad_start = pad_end - padded
    dest = pad_start[e_s] + (jnp.arange(A, dtype=jnp.int32) - start[e_s])
    n_blocks = (A + N_EXPERTS * (MOE_BLK - 1) + MOE_BLK - 1) // MOE_BLK
    P = n_blocks * MOE_BLK
    row_tok = jnp.zeros((P,), jnp.int32).at[dest].set(tok_s)
    row_w = jnp.zeros((P,), x.dtype).at[dest].set(w_s)
    blk_expert = jnp.minimum(jnp.searchsorted(pad_end, jnp.arange(n_blocks) * MOE_BLK, side='right'),
                             N_EXPERTS - 1)

    def body(y, inp):
        e, toks, wr = inp
        out = swiglu(x[toks], w_gate[e], w_up[e], w_down[e]) * wr[:, None]
        return y.at[toks].add(out), None

    y, _ = lax.scan(body, jnp.zeros_like(x),
                    (blk_expert, row_tok.reshape(n_blocks, MOE_BLK), row_w.reshape(n_blocks, MOE_BLK)))
    return y

def moe_ffn(h, w_router, router_bias, w_gate, w_up, w_down, ws_gate, ws_up, ws_down):
    shp = h.shape
    x = h.reshape(-1, shp[-1])
    N = x.shape[0]
    s = jax.nn.sigmoid((x @ w_router).astype(jnp.float32))
    sel = s + router_bias.astype(jnp.float32)
    grp_score = lax.top_k(sel.reshape(N, N_GROUPS, -1), 2)[0].sum(-1)
    _, gidx = lax.top_k(grp_score, TOPK_GROUPS)
    gmask = jnp.any(gidx[..., None] == jnp.arange(N_GROUPS), axis=1)
    emask = jnp.repeat(gmask, N_EXPERTS // N_GROUPS, axis=-1)
    _, eidx = lax.top_k(jnp.where(emask, sel, -jnp.inf), TOP_K)
    wsel = jnp.take_along_axis(s, eidx, axis=-1)
    wsel = wsel / jnp.sum(wsel, axis=-1, keepdims=True) * ROUTE_SCALE
    y = routed_experts(x, eidx, wsel.astype(x.dtype), w_gate, w_up, w_down) + swiglu(x, ws_gate, ws_up, ws_down)
    return y.reshape(shp)

def setup_inputs(seed: int = 0) -> dict:
    key = jax.random.key(seed)
    ks = iter(jax.random.split(key, 48))
    nrm = lambda shape, scale: jax.random.normal(next(ks), shape, jnp.float32) * scale
    n_pages = PAST_LEN // PAGE_SIZE
    n_phys = (DEC_BATCH * n_pages * 5 + 3) // 4
    D = D_MODEL
    hk, hv = GLA_HEADS * GLA_DK, GLA_HEADS * GLA_DV
    gla_in = 2 * hk + 2 * hv + GLA_RANK
    dsa_in = ATT_HEADS * ATT_DH + 2 * ATT_KV_HEADS * ATT_DH + IDX_HEADS * IDX_DH + IDX_DH + IDX_HEADS
    page_table = jax.random.permutation(next(ks), n_phys)[:DEC_BATCH * n_pages]
    page_table = page_table.reshape(DEC_BATCH, n_pages).astype(jnp.int32)
    return {
        'x_prompt': nrm((BATCH, SEQ, D), 1.0),
        'x_sample': nrm((DEC_BATCH, DEC_SEQ, D), 1.0),
        'c_prompt': nrm((BATCH, D), 1.0),
        'c_sample': nrm((DEC_BATCH, D), 1.0),
        'state_gla': nrm((N_GLA_LAYERS, DEC_BATCH, GLA_HEADS, GLA_DK, GLA_DV), 0.5),
        'cache_k': nrm((N_DSA_LAYERS, n_phys, PAGE_SIZE, ATT_KV_HEADS, ATT_DH), 1.0),
        'cache_v': nrm((N_DSA_LAYERS, n_phys, PAGE_SIZE, ATT_KV_HEADS, ATT_DH), 1.0),
        'cache_idx_k': nrm((N_DSA_LAYERS, n_phys, PAGE_SIZE, IDX_DH), 1.0),
        'page_table': page_table,
        'rel_bias': nrm((N_BUCKETS, ATT_HEADS), 0.5),
        'w_ada': nrm((DEPTH, D, 6 * D), 0.5 * D ** -0.5),
        'b_ada': nrm((DEPTH, 6 * D), 0.02),
        'norm_mix': 1.0 + nrm((DEPTH, D), 0.02),
        'norm_ffn': 1.0 + nrm((DEPTH, D), 0.02),
        'norm_final': 1.0 + nrm((D,), 0.02),
        'gla_w_in': nrm((N_GLA_LAYERS, D, gla_in), D ** -0.5),
        'gla_w_g2': nrm((N_GLA_LAYERS, GLA_RANK, hk), GLA_RANK ** -0.5),
        'gla_b_g2': nrm((N_GLA_LAYERS, hk), 0.1),
        'gla_gnorm': 1.0 + nrm((N_GLA_LAYERS, GLA_DV), 0.02),
        'gla_w_out': nrm((N_GLA_LAYERS, hv, D), hv ** -0.5),
        'dsa_w_in': nrm((N_DSA_LAYERS, D, dsa_in), D ** -0.5),
        'dsa_idx_ln_g': 1.0 + nrm((N_DSA_LAYERS, IDX_DH), 0.02),
        'dsa_idx_ln_b': nrm((N_DSA_LAYERS, IDX_DH), 0.02),
        'dsa_w_out': nrm((N_DSA_LAYERS, ATT_HEADS * ATT_DH, D), (ATT_HEADS * ATT_DH) ** -0.5),
        'moe_w_router': nrm((DEPTH, D, N_EXPERTS), D ** -0.5),
        'moe_router_bias': nrm((DEPTH, N_EXPERTS), 0.01),
        'moe_w_gate': nrm((DEPTH, N_EXPERTS, D, EXPERT_FF), D ** -0.5),
        'moe_w_up': nrm((DEPTH, N_EXPERTS, D, EXPERT_FF), D ** -0.5),
        'moe_w_down': nrm((DEPTH, N_EXPERTS, EXPERT_FF, D), EXPERT_FF ** -0.5),
        'shared_w_gate': nrm((DEPTH, D, SHARED_FF), D ** -0.5),
        'shared_w_up': nrm((DEPTH, D, SHARED_FF), D ** -0.5),
        'shared_w_down': nrm((DEPTH, SHARED_FF, D), SHARED_FF ** -0.5),
    }

def reference(x_prompt, x_sample, c_prompt, c_sample, state_gla, cache_k, cache_v, cache_idx_k, page_table,
              rel_bias, w_ada, b_ada, norm_mix, norm_ffn, norm_final,
              gla_w_in, gla_w_g2, gla_b_g2, gla_gnorm, gla_w_out,
              dsa_w_in, dsa_idx_ln_g, dsa_idx_ln_b, dsa_w_out,
              moe_w_router, moe_router_bias, moe_w_gate, moe_w_up, moe_w_down,
              shared_w_gate, shared_w_up, shared_w_down):
    xp, xs = x_prompt, x_sample
    gla_p, gla_s = [], []
    kp_l, vp_l, kip_l, ks_l, vs_l, kis_l = [], [], [], [], [], []
    for i in range(DEPTH):
        sh1p, sc1p, gt1p, sh2p, sc2p, gt2p = ada_mod(c_prompt, w_ada[i], b_ada[i])
        sh1s, sc1s, gt1s, sh2s, sc2s, gt2s = ada_mod(c_sample, w_ada[i], b_ada[i])
        hp = modulate(xp, norm_mix[i], sh1p, sc1p)
        hs = modulate(xs, norm_mix[i], sh1s, sc1s)
        j = i // 2
        if i % 2 == 0:
            gp = (gla_w_in[j], gla_w_g2[j], gla_b_g2[j], gla_gnorm[j], gla_w_out[j])
            mp, Sp = gla_mixer(hp, None, *gp)
            ms, Ss = gla_mixer(hs, state_gla[j], *gp)
            gla_p.append(Sp)
            gla_s.append(Ss)
        else:
            dp = (dsa_w_in[j], dsa_idx_ln_g[j], dsa_idx_ln_b[j], dsa_w_out[j])
            mp, (kp_, vp_, kip_) = dsa_mixer_prompt(hp, rel_bias, *dp)
            ms, (ks_, vs_, kis_) = dsa_mixer_sample(hs, cache_k[j], cache_v[j], cache_idx_k[j], page_table,
                                                   rel_bias, *dp)
            kp_l.append(kp_); vp_l.append(vp_); kip_l.append(kip_)
            ks_l.append(ks_); vs_l.append(vs_); kis_l.append(kis_)
        xp = xp + gt1p[:, None, :] * mp
        xs = xs + gt1s[:, None, :] * ms
        mo = (moe_w_router[i], moe_router_bias[i], moe_w_gate[i], moe_w_up[i], moe_w_down[i],
              shared_w_gate[i], shared_w_up[i], shared_w_down[i])
        xp = xp + gt2p[:, None, :] * moe_ffn(modulate(xp, norm_ffn[i], sh2p, sc2p), *mo)
        xs = xs + gt2s[:, None, :] * moe_ffn(modulate(xs, norm_ffn[i], sh2s, sc2s), *mo)
    y_prompt = rms_norm(xp, norm_final)
    y_sample = rms_norm(xs, norm_final)
    return (y_prompt, y_sample, jnp.stack(gla_p), jnp.stack(gla_s),
            jnp.stack(kp_l), jnp.stack(vp_l), jnp.stack(kip_l),
            jnp.stack(ks_l), jnp.stack(vs_l), jnp.stack(kis_l))


_drawn_inputs = setup_inputs


def setup_inputs(seed=0):
    import zlib

    import numpy as np

    out = dict(_drawn_inputs(seed))
    spreads = {}
    factors = {'norm_final': 2.876, 'gla_gnorm': 2.898, 'dsa_idx_ln_g': 3.389, 'dsa_idx_ln_b': 3.507}
    for name, (base, spread) in spreads.items():
        noise = np.random.default_rng([zlib.crc32(name.encode()), seed]).standard_normal(out[name].shape)
        drawn = base * np.exp(spread * noise) if base else spread * noise
        out[name] = __import__('jax').numpy.asarray(drawn.astype(out[name].dtype))
    for name, factor in factors.items():
        out[name] = (out[name] * factor).astype(out[name].dtype)
    return out
```

```python
from contextlib import ExitStack
import math

import numpy as np
import concourse.bass as bass
from concourse import mybir
from concourse.bass import IndirectOffsetOnAxis, ds

F32 = mybir.dt.float32
BF16 = mybir.dt.bfloat16
I32 = mybir.dt.int32
U32 = mybir.dt.uint32
ALU = mybir.AluOpType
ACT = mybir.ActivationFunctionType
AX = mybir.AxisListType.X

P = 128
D = 1024
KT = D // P
SEQ, DEC = 256, 8
TOK = SEQ + DEC
TP = 3 * P
TT = 3
GH, GDK, GDV, CH = 4, 128, 256, 64
NE, TOPK, NG, TOPG, FF = 64, 8, 8, 4, 256
CAP = 64
NOV = 34
NB = NE + NOV
OOB = 16384
EPS = 1e-6
AH, KVH, DH, IH, IDH = 16, 4, 64, 8, 64
PAGE, NPG = 128, 16
PAST = PAGE * NPG
WS = 4
THIRD = 2048
NEG = -1e30
GONE = -2e38
ROUTE_SCALE = 2.5

CONST = {}
_n = 0
for _name, _w in (("ident", 128), ("tri", 128), ("gmask", 64), ("slot", 128), ("fold", 9), ("gtri", 64),
                  ("valid", 3), ("pcol", 1), ("jcol", 1), ("iota", NOV), ("scanm", 256), 
                  ("ohs", 129), ("expand", 128), ("hsum", 8), ("cau", 128), ("ones", 1), ("ones1024", 128),
                  ("ones256", 128), ("blk64", 128), ("expt", 8), ("eps", 1)):
    CONST[_name] = (_n, _w)
    _n += _w
NCONST = _n


def bucket(dist):
    dist = max(dist, 0)
    if dist < 16:
        return dist
    return min(16 + int(math.log(dist / 16) / math.log(8) * 16 + 1e-9), 31)


def distance_onehot():
    c = np.zeros((32, 384), np.float32)
    for y in range(384):
        c[bucket(255 - y), y] = 1
    return c


def constants():
    c = {k: np.zeros((P, w), np.float32) for k, (_, w) in CONST.items()}
    p, f = np.arange(P)[:, None], np.arange(P)[None, :]
    c["ident"][:] = p == f
    c["tri"][:] = p < f
    c["gmask"][:] = (p % CH) <= np.arange(CH)[None, :]
    c["slot"][:] = f % CAP + 1
    c["fold"][:] = (p % 32) == np.arange(9)[None, :]
    g = np.arange(64)
    c["gtri"][:] = ((g % 8) < (g // 8))[None, :]
    c["valid"][:] = (np.arange(3)[None, :] * P + p) < TOK
    c["pcol"][:] = p
    c["jcol"][:] = (p >= CAP) + OOB
    c["iota"][:] = np.arange(NOV)[None, :]
    c["scanm"][:] = (np.arange(256) % CH != 0)[None, :]

    for y in range(129):
        c["ohs"][bucket(128 - y), y] = 1
    c["expand"][:8] = np.arange(128)[None, :] // 16 == np.arange(8)[:, None]
    c["hsum"][:64] = np.arange(64)[:, None] // 8 == np.arange(8)[None, :]
    c["cau"][:] = np.where(f <= p, 0.0, NEG)
    c["ones"][:] = 1
    c["eps"][:] = EPS
    c["ones1024"][:] = 1 / 1024
    c["ones256"][:] = 1 / 256
    c["blk64"][:] = (p // 64 == f // 64) / 64
    c["expt"][:] = p // 16 == np.arange(8)[None, :]
    return np.concatenate([c[k] for k in CONST], axis=1)


VROW = {"mix": 0, "ffn": 16, "final": 32, "gnorm": 40, "bg2": 42, "lng": 46, "lnb": 47}


def build(nc, ins, outs):
    ctx = ExitStack()
    with ctx:
        def sb(name, shape, dt=F32):
            return ctx.enter_context(nc.sbuf_tensor(name, shape, dt))

        sems = {}

        def S(name):
            if name not in sems:
                sems[name] = ctx.enter_context(nc.semaphore(name))
            return sems[name]

        class Chain:

            def __init__(self, eng, name):
                self.eng, self.sem, self.n, self.base = eng, S(name), 0, None

            def __call__(self, ins):
                ins.then_inc(self.sem, 1)
                self.n += 1
                self.eng.wait_ge(self.sem, self.n if self.base is None else self.base + self.n)

            def enter(self, base):
                self.kept, self.base, self.n = self.n, base, 0

            def leave(self, total, per):
                assert self.n == per, (self.n, per)
                self.base, self.n = None, self.kept + total

        def wait_alone(eng, name, value):
            eng.wait_ge(name, value)
            eng.sem_inc(S("passed"), 1)

        PS = ctx.enter_context(nc.psum_tensor("PS", [P, 8, 512], F32))
        cst = sb("cst", [P, NCONST])
        K = {k: cst[:, o:o + w] for k, (o, w) in CONST.items()}
        ring = sb("ring", [P, WS, 3, THIRD])
        xT = sb("xT", [P, KT, TOK])
        hT = sb("hT", [P, KT, TP])
        modT2 = sb("modT", [P, 2, 48, 9])
        modA = sb("modA", [P, KT, 9])
        cT = sb("cT", [P, KT, 32])
        vT = sb("vT", [P, 48])
        bT = sb("bT", [P, 96])
        rstd = sb("rstd", [P, TOK])
        mrow = sb("mrow", [P, 3 * 256])
        shT = sb("shT", [P, KT, TOK])
        triB = sb("triB", [P, P], BF16)
        onesB = sb("onesB", [P, P], BF16)
        slotB = sb("slotB", [P, P], BF16)
        AW = 17088
        arena = sb("arena", [P, AW])

        def carver(width=AW):
            at = [0]

            def take(*shape, dt=F32):
                n = int(np.prod(shape))
                words = n if dt != BF16 else (n + 1) // 2
                ap = arena[:, at[0]:at[0] + words]
                at[0] += words
                assert at[0] <= width, at
                if dt != F32:
                    ap = ap.bitcast(dt)
                names = "abcde"[:len(shape)]
                if len(shape) > 1:
                    ap = ap.rearrange(f"p ({' '.join(names)}) -> p {' '.join(names)}",
                                      **{q: s for q, s in zip(names[1:], shape[1:])})
                return ap
            take.at = at
            return take

        block = ctx.enter_context(nc.Block())
        pe, dve, act, pool, sp = nc.tensor, nc.vector, nc.scalar, nc.gpsimd, nc.sync
        dv = Chain(dve, "dve_chain")
        ac = Chain(act, "act_chain")

        def bank(i, n=512):
            return PS[:, i, 0:n]

        def bc(ap, axis, n):
            ap = ap.unsqueeze(axis)
            shape = list(ap.shape)
            shape[axis] = n
            return ap.broadcast_to(shape)

        class Ring:
            def __init__(self):
                self.next, self.loads, self.uses = 0, [0] * WS, [0] * WS

            def slot(self):
                s = self.next % WS
                self.next += 1
                return s
        W = Ring()

        prior = {}

        def plan(n, signals=True):
            got = []
            for _ in range(n):
                s = W.slot()
                W.loads[s] += 1
                prior[(s, W.loads[s])] = W.uses[s]
                W.uses[s] += signals
                got.append((s, W.loads[s]))
            return got

        def load_item(item, thirds, ovl=0):
            s, n = item
            if prior[item]:
                sp.wait_ge(S(f"slot_used{s}"), prior[item])
            if ovl:
                sp.wait_ge(S("over_done"), ovl)
            for t, src in enumerate(thirds):
                dst = ring[:, s, t, :]
                if len(src.shape) == 3:
                    dst = dst.rearrange("p (k n) -> p k n", n=src.shape[2])
                    if dst.shape[1] != src.shape[1]: dst = dst[:, 0:src.shape[1], :]
                elif src.shape[1] < THIRD:
                    dst = dst[:, 0:src.shape[1]]
                sp.dma_start(dst, src).then_inc(S(f"slot_loaded{s}"), 16)

        def item_ready(eng, item):
            s, n = item
            eng.wait_ge(S(f"slot_loaded{s}"), 48 * n)

        def cols(w, c0, n=256):
            return w[:, c0:c0 + n].rearrange("(k p) n -> p k n", p=P)

        def third(s, t):
            return ring[:, s, t, :].rearrange("p (k n) -> p k n", k=KT)

        it_ada = [plan(8), None]
        it_gla = plan(4)
        it_gout = plan(2)
        it_ada[1] = plan(8)
        it_sh = [plan(1)[0], None]
        it_ex = [plan(NE, False), None]
        it_dsa = plan(3)
        it_dout = plan(2)
        it_sh[1] = plan(1)[0]
        it_ex[1] = plan(NE, False)

        hk, hv = GH * GDK, GH * GDV
        w_in = ins["gla_w_in"][0]
        w_dsa = ins["dsa_w_in"][0]

        tk = carver()
        xrow = tk(TT, D)
        crow = tk(D)
        crow2 = tk(D)
        vrow = tk(P)
        brow = tk(P)

        def sp_setup():
            sp.dma_start(cst[:], ins["consts"]).then_inc(S("setup_in"), 16)
            sp.dma_start(crow[0:1, :], ins["c_prompt"]).then_inc(S("setup_in"), 16)
            sp.dma_start(crow[1:9, :], ins["c_sample"]).then_inc(S("setup_in"), 16)
            for name, key, n in (("norm_mix", "mix", 16), ("norm_ffn", "ffn", 16)):
                r = VROW[key]
                sp.dma_start(vrow[r:r + n, :], ins[name].rearrange("l (k p) -> (l k) p", p=P)).then_inc(S("setup_in"), 16)
            sp.dma_start(vrow[32:40, :], ins["norm_final"].rearrange("(k p) -> k p", p=P)).then_inc(S("setup_in"), 16)
            sp.dma_start(vrow[40:42, :], ins["gla_gnorm"].rearrange("l (k p) -> (l k) p", p=P)).then_inc(S("setup_in"), 16)
            sp.dma_start(vrow[42:46, :], ins["gla_b_g2"].rearrange("l (k p) -> (l k) p", p=P)).then_inc(S("setup_in"), 16)
            for r, name in ((46, "dsa_idx_ln_g"), (47, "dsa_idx_ln_b")):
                for half in range(2):
                    sp.dma_start(vrow[r:r + 1, 64 * half:64 * half + 64], ins[name]).then_inc(S("setup_in"), 16)
            sp.dma_start(brow[0:96, :], ins["b_ada"].rearrange("l (k p) -> (l k) p", p=P)).then_inc(S("setup_in"), 16)
            for t in range(2):
                sp.dma_start(xrow[:, t, :], ins["x_prompt"][0, t * P:(t + 1) * P, :]).then_inc(S("x_in"), 16)
            sp.dma_start(xrow[0:DEC, 2, :], ins["x_sample"][:, 0, :]).then_inc(S("x_in"), 16)
        N_SETUP = 16 * 13

        def pe_setup():
            pe.wait_ge(S("setup_in"), N_SETUP)
            pe.wait_ge(S("c_silu"), 1)
            for k in range(KT):
                m = pe.transpose(PS[:, 0, 16 * k:16 * k + 9], crow2[0:9, k * P:(k + 1) * P], K["ident"][0:9, 0:9])
            m = pe.transpose(PS[:, 1, 0:48], vrow[0:48, :], K["ident"][0:48, 0:48])
            m = pe.transpose(PS[:, 1, 64:160], brow[0:96, :], K["ident"][0:96, 0:96])
            m.then_inc(S("setup_T"), 1)
            pe.wait_ge(S("x_in"), 48)
            for t in range(TT):
                n = P if t < 2 else DEC
                for half in range(2):
                    for k in range(4):
                        m = pe.transpose(PS[:, 2 + 2 * t + half, k * P:k * P + n],
                                         xrow[0:n, t, (4 * half + k) * P:(4 * half + k + 1) * P], K["ident"][0:n, 0:n])
                    m.then_inc(S("x_T"), 1)

        def act_setup():
            act.wait_ge(S("setup_in"), N_SETUP)
            act.activation(crow2[0:9, :], crow[0:9, :], ACT.Silu).then_inc(S("c_silu"), 1)

        def dve_setup():
            dv(dve.memset(cT[:], 0.0))
            dv(dve.memset(hT[:], 0.0))
            dve.wait_ge(S("setup_in"), N_SETUP)
            dve.tensor_copy(triB[:], K["tri"])
            dve.memset(onesB[:], 1.0)
            dve.tensor_copy(slotB[:], K["slot"])
            dve.wait_ge(S("setup_T"), 1)
            dve.tensor_copy(cT[:, :, 0:9], PS[:, 0, 0:128].rearrange("p (k c) -> p k c", c=16)[:, :, 0:9]).then_inc(S("c_T"), 1)
            dv(dve.tensor_copy(vT[:], PS[:, 1, 0:48]))
            dv(dve.tensor_copy(bT[:], PS[:, 1, 64:160]))
            for t in range(TT):
                n = P if t < 2 else DEC
                for half in range(2):
                    dve.wait_ge(S("x_T"), 2 * t + half + 1)
                    ins_ = dve.tensor_copy(xT[:, 4 * half:4 * half + 4, t * P:t * P + n],
                                           PS[:, 2 + 2 * t + half, :].rearrange("p (k c) -> p k c", c=P)[:, :, 0:n])
            dv(ins_)

        def sp_ada(l):
            for i, item in enumerate(it_ada[l]):
                load_item(item, [cols(ins["w_ada"][l], 768 * i + 256 * t) for t in range(3)])

        def pe_ada(l):
            if l == 0:
                pe.wait_ge(S("c_T"), 1)
                pe.wait_ge(S("x_out_of_psum"), 1)
            for i, item in enumerate(it_ada[l]):
                s, _ = item
                n = 8 * l + i
                item_ready(pe, item)
                if n >= 1:
                    pe.wait_ge(S("mod_rows"), n)
                for t in range(3):
                    for kk in range(2):
                        for g in range(4):
                            m = pe.matmul(PS[32 * g:32 * g + 32, t // 2, 256 * (t % 2):256 * (t % 2) + 256],
                                          cT[:, 2 * g + kk, :], third(s, t)[:, 2 * g + kk, :],
                                          start=(kk == 0), stop=(kk == 1), skip_group_check=True)
                m.then_inc(S(f"slot_used{s}"), 1)
                m = pe.wait_ge(S("mod_rows"), n + 1)
                if n >= 1:
                    pe.wait_ge(S("mod_T"), n)
                for j in range(6):
                    m = pe.matmul(PS[:, 2, 16 * j:16 * j + 9], mrow[:, j * P:(j + 1) * P], K["fold"],
                                  start=True, stop=True)
                m.then_inc(S("mod_fold"), 1)

        def act_ada(l):
            for i, item in enumerate(it_ada[l]):
                n = 8 * l + i
                act.wait_ge(S(f"slot_used{item[0]}"), prior[item] + 1)
                if n >= 1:
                    act.wait_ge(S("mod_fold"), n)
                ac(act.copy(mrow[:, 0:512], bank(0)))
                act.copy(mrow[:, 512:768], PS[:, 1, 0:256]).then_inc(S("mod_rows"), 1)

        def dve_ada(l):
            for i in range(8):
                dve.wait_ge(S("mod_fold"), 8 * l + i + 1)
                dve.tensor_tensor(modT2[:, l, 6 * i:6 * i + 6, :],
                                  PS[:, 2, 0:96].rearrange("p (k c) -> p k c", c=16)[:, :, 0:9],
                                  bc(bT[:, 48 * l + 6 * i:48 * l + 6 * i + 6], 2, 9), ALU.add).then_inc(S("mod_T"), 1)
            dve.wait_ge(S("mod_T"), 8 * (l + 1))

        norm_sq = arena[:, 0:KT * TOK].rearrange("p (k t) -> p k t", k=KT)

        def act_norm(n, sqbuf, b):
            act.wait_ge(S("x_new"), n + 1)
            act.activation(sqbuf[:], xT[:], ACT.Square).then_inc(S("x_sq"), 1)
            act.wait_ge(S("x_ms"), n + 1)
            act.activation(rstd[:], PS[:, b, 0:TOK], ACT.Sqrt, bias=K["eps"]).then_inc(S("x_rms"), 1)

        def pe_norm(n, sqbuf, b):
            pe.wait_ge(S("x_sq"), n + 1)
            for k in range(KT):
                m = pe.matmul(PS[:, b, 0:TOK], K["ones1024"], sqbuf[:, k, :], start=(k == 0), stop=(k == KT - 1))
            m.then_inc(S("x_ms"), 1)

        def dve_norm(n, l, part, b):
            modT = modT2[:, l]
            shift, scale = modT[:, 24 * part:24 * part + 8, :], modT[:, 24 * part + 8:24 * part + 16, :]
            v0 = (VROW["ffn"] if part else VROW["mix"]) + 8 * l
            dv(dve.tensor_scalar(modA[:], scale, 1.0, None, ALU.add))
            dv(dve.tensor_tensor(modA[:], modA[:], bc(vT[:, v0:v0 + 8], 2, 9), ALU.mult))
            dve.wait_ge(S("x_rms"), n + 1)
            dv(dve.reciprocal(rstd[:], rstd[:]))
            dv(dve.tensor_tensor(hT[:, :, 0:TOK], xT[:], bc(rstd[:], 1, KT), ALU.mult))
            for k in range(KT):
                dve.tensor_scalar(hT[:, k, 0:SEQ], hT[:, k, 0:SEQ], modA[:, k, 0:1], shift[:, k, 0:1], ALU.mult, ALU.add)
            dv(dve.tensor_tensor(hT[:, :, SEQ:TOK], hT[:, :, SEQ:TOK], modA[:, :, 1:9], ALU.mult))
            dve.tensor_tensor(hT[:, :, SEQ:TOK], hT[:, :, SEQ:TOK], shift[:, :, 1:9], ALU.add).then_inc(S("h_ready"), 1)

        def add_gated(k, src, modT, g0, tmp):
            dve.scalar_tensor_tensor(out=xT[:, k, 0:SEQ], in0=src[:, 0:SEQ], scalar=modT[:, g0 + k, 0:1],
                                     in1=xT[:, k, 0:SEQ], op0=ALU.mult, op1=ALU.add)
            dv(dve.tensor_tensor(tmp, src[:, SEQ:TOK], modT[:, g0 + k, 1:9], ALU.mult))
            dv(dve.tensor_tensor(xT[:, k, SEQ:TOK], xT[:, k, SEQ:TOK], tmp, ALU.add))

        tk = carver()
        pT = tk(24, TOK)
        qe, ke, qb, kd = (tk(GH, SEQ) for _ in range(4))
        cL = tk(GH, SEQ)
        dL = tk(GH, SEQ)
        vtok = tk(2, hv)
        kdt = tk(2, hk)
        attS = tk(2, GH, CH)
        Sst = tk(GH, GDV)
        eg = sb("eg", [P, GH, DEC])[:]
        oT = shT
        wg1 = Sst.rearrange("p h v -> p (h v)")[:, TOK:TOK + P].rearrange("p (k n) -> p k n", k=KT)
        wg2 = dL.rearrange("p h t -> p (h t)")[:, 0:hk]
        g1T = Sst.rearrange("p h v -> p (h v)")[:, 0:TOK]
        kdt0 = 6336 + 4 * 1024 + 2 * 1024 + 2048
        Lg = arena[:, kdt0:kdt0 + GH * TOK].rearrange("p (h t) -> p h t", h=GH)
        kmask = arena[:, 6336:6336 + DEC * hk].rearrange("p (b n) -> p b n", b=DEC)
        osq = arena[:, 6336:6336 + KT * TOK].rearrange("p (k t) -> p k t", k=KT)
        ktok8 = cL.rearrange("p h t -> p (h t)")[:, 0:hk]
        vtok8 = dL.rearrange("p h t -> p (h t)")
        sbuf3 = [arena[:, o:o + 1024].rearrange("p (h v) -> p h v", h=GH) for o in (8 * TOK, 8 * TOK + 1024, 4 * TOK)]

        GP = {'g1': 0, 'z': 1, 'v_T': 2, 'kd_T': 4, 'att': 6, 'kv8_T': 8, 'o_ms': 9}
        GD = {'g1_out': 0, 'dL': 1, 'dE': 2, 'kd': 3, 'v_tok': 4, 'kd_tok': 6, 'att_out': 8, 'kmask': 10, 'o_all': 11}

        def sp_gla_small():
            sp.dma_start(wg1, w_in[:, 2 * hk + 2 * hv:].rearrange("(k p) n -> p k n", p=P)).then_inc(S("g_small"), 16)
            sp.dma_start(wg2[0:16, :], ins["gla_w_g2"][0]).then_inc(S("g_small"), 16)

        def sp_gla():
            for i, item in enumerate(it_gla):
                load_item(item, [cols(w_in, 768 * i + 256 * t) for t in range(3)])
            for i, item in enumerate(it_gout):
                load_item(item, [cols(ins["gla_w_out"][0], 512 * i), cols(ins["gla_w_out"][0], 512 * i + 256), cols(ins["gla_w_out"][0], 512 * i)])

        def pe_gla():
            pe.wait_ge(S("h_ready"), 1)
            pe.wait_ge(S("g_small"), 32)
            for k in range(KT):
                m = pe.matmul(PS[0:16, 0, 0:TOK], wg1[:, k, :], hT[:, k, 0:TOK], start=(k == 0), stop=(k == KT - 1))
            m.then_inc(S("gla_pe"), 1)
            pe.wait_ge(S("gla_dve"), GD["g1_out"] + 1)
            for h in range(GH):
                m = pe.matmul(PS[:, 4 + h, 0:TOK], wg2[0:16, h * P:(h + 1) * P], g1T[0:16, :], start=True, stop=True)
            m.then_inc(S("gla_pe"), 1)
            for m_ in range(24):
                item = it_gla[m_ // 6]
                if m_ % 6 == 0:
                    item_ready(pe, item)
                if 4 <= m_ < 20:
                    pe.wait_ge(S("proj_dve"), m_ - 3)
                elif m_ >= 20:
                    pe.wait_ge(S("proj_act"), m_ - 19)
                w3 = third(item[0], (m_ % 6) // 2)
                for k in range(KT):
                    m = pe.matmul(PS[:, m_ % 4, 0:TOK], w3[:, k, (m_ % 2) * P:(m_ % 2 + 1) * P], hT[:, k, 0:TOK],
                                  start=(k == 0), stop=(k == KT - 1))
                m.then_inc(S("proj"), 1)
                if m_ % 6 == 5:
                    pe.wait_ge(S("proj"), m_ + 1)
                    pe.sem_inc(S(f"slot_used{item[0]}"), 1)
            pe.wait_ge(S("proj_dve"), 16)
            pe.wait_ge(S("proj_act"), 8)
            for T in range(2):
                for j in range(8):
                    m = pe.transpose(PS[:, 2 * T + j // 4, (j % 4) * P:(j % 4 + 1) * P], pT[:, 8 + j, T * P:(T + 1) * P], K["ident"])
                m.then_inc(S("gla_pe"), 1)
            pe.wait_ge(S("gla_dve"), GD["kd"] + 1)
            for T in range(2):
                for h in range(GH):
                    m = pe.transpose(PS[:, 4 + T, h * P:(h + 1) * P], kd[:, h, T * P:(T + 1) * P], K["ident"])
                m.then_inc(S("gla_pe"), 1)
            for T in range(2):
                for h in range(GH):
                    for o in range(2):
                        c = 2 * T + o
                        m = pe.matmul(PS[64 * o:64 * o + 64, 6 + T, h * CH:(h + 1) * CH], ke[:, h, c * CH:(c + 1) * CH],
                                      qe[:, h, c * CH:(c + 1) * CH], start=True, stop=True)
                m.then_inc(S("gla_pe"), 1)
            pe.wait_ge(S("gla_dve"), GD["v_tok"] + 2)
            pe.wait_ge(S("gla_dve"), GD["kd_tok"] + 2)
            pe.wait_ge(S("gla_dve"), GD["att_out"] + 2)
            for c in range(4):
                T, o = c // 2, c % 2
                r = slice(64 * o, 64 * o + 64)
                if c >= 2:
                    pe.wait_ge(S("o_out"), c - 1)
                if c:
                    pe.wait_ge(S("state"), c)
                for h in range(GH):
                    m = pe.matmul(PS[:, 4 + 2 * (c % 2) + h // 2, (h % 2) * GDV:(h % 2 + 1) * GDV], kdt[r, T, h * P:(h + 1) * P],
                                  vtok[r, T, h * GDV:(h + 1) * GDV], start=True, stop=True)
                m.then_inc(S("upd"), 1)
                for h in range(GH):
                    for v in range(2):
                        j = 2 * h + v
                        dst = PS[:, c % 2, j * CH:(j + 1) * CH]
                        m = pe.matmul(dst, vtok[r, T, j * P:(j + 1) * P], attS[r, T, h, :], start=True, stop=(c == 0))
                        if c:
                            m = pe.matmul(dst, Sst[:, h, v * P:(v + 1) * P], qb[:, h, c * CH:(c + 1) * CH], start=False, stop=True)
                m.then_inc(S("o"), 1)
            pe.wait_ge(S("o_out"), 4)
            for h in range(GH):
                m = pe.transpose(PS[0:DEC, 2, h * P:(h + 1) * P], pT[:, 4 + h, SEQ:TOK], K["ident"])
            for j in range(8):
                m = pe.transpose(PS[0:DEC, j // 4, (j % 4) * P:(j % 4 + 1) * P], pT[:, 8 + j, SEQ:TOK], K["ident"])
            m.then_inc(S("gla_pe"), 1)
            pe.wait_ge(S("gla_dve"), GD["kmask"] + 1)
            pe.wait_ge(S("state"), 4)
            for b in range(DEC):
                B0 = 4 + 2 * (b % 2)
                if b >= 2:
                    pe.wait_ge(S("sstate"), b - 1)
                for h in range(GH):
                    m = pe.matmul(PS[:, B0 + h // 2, (h % 2) * GDV:(h % 2 + 1) * GDV], kmask[0:DEC, b, h * P:(h + 1) * P],
                                  vtok8[0:DEC, h * GDV:(h + 1) * GDV], start=True, stop=True)
                m.then_inc(S("outer"), 1)
                if b >= 1:
                    pe_sample_o(b - 1)
            pe_sample_o(DEC - 1)
            pe.wait_ge(S("o_sq"), 1)
            for h in range(GH):
                for v in range(2):
                    m = pe.matmul(PS[:, h, 0:TOK], K["ones256"], osq[:, 2 * h + v, :], start=(v == 0), stop=(v == 1))
            m.then_inc(S("gla_pe"), 1)
            pe.wait_ge(S("mix_in"), 1)
            pe_out_proj(it_gout, oT[:, :, :], 0)

        def pe_sample_o(b):
            pe.wait_ge(S("sstate"), b + 1)
            for h in range(GH):
                for v in range(2):
                    m = pe.matmul(PS[:, 3, (2 * h + v) * DEC + b:(2 * h + v) * DEC + b + 1], sbuf3[b % 3][:, h, v * P:(v + 1) * P],
                                  pT[:, h, SEQ + b:SEQ + b + 1], start=True, stop=True)
            m.then_inc(S("so"), 1)

        def pe_out_proj(items, src, n):
            for k in range(KT):
                item = items[k // 4]
                if k % 4 == 0:
                    item_ready(pe, item)
                if k >= 4:
                    pe.wait_ge(S("mix_added"), 8 * n + k - 3)
                w3 = third(item[0], (k % 4) // 2)
                for kk in range(KT):
                    m = pe.matmul(PS[:, 4 + k % 4, 0:TOK], w3[:, kk, (k % 2) * P:(k % 2 + 1) * P], src[:, kk, :],
                                  start=(kk == 0), stop=(kk == KT - 1))
                m.then_inc(S("mix_out"), 1)
                if k % 4 == 3:
                    pe.wait_ge(S("mix_out"), 8 * n + k + 1)
                    pe.sem_inc(S(f"slot_used{item[0]}"), 1)

        def dve_out_proj(n):
            tmp = modA[:, 0, 0:8]
            for k in range(KT):
                dve.wait_ge(S("mix_out"), 8 * n + k + 1)
                add_gated(k, PS[:, 4 + k % 4, :], modT2[:, n], 16, tmp)
                dve.sem_inc(S("mix_added"), 1)
            dve.sem_inc(S("x_new"), 1)

        def dve_gla():
            for i in range(2):
                dve.wait_ge(S(f"bias_out{i}"), 128)
            dve.wait_ge(S("gla_pe"), GP["g1"] + 1)
            dve.tensor_copy(g1T[0:16, :], PS[0:16, 0, 0:TOK]).then_inc(S("gla_dve"), 1)
            for m_ in range(16):
                dve.wait_ge(S("proj"), m_ + 1)
                src = PS[:, m_ % 4, 0:TOK]
                if m_ < 4:
                    ins_ = dve.tensor_scalar(pT[:, m_, :], src, GDK ** -0.5, None, ALU.mult)
                else:
                    ins_ = dve.tensor_copy(pT[:, m_, :], src)
                ins_.then_inc(S("proj_dve"), 1)
                if m_ == 5:
                    dve.wait_ge(S("softplus"), 1)
                    for h in range(GH):
                        dv(dve.tensor_tensor_scan(cL[:, h, :], K["scanm"], Lg[:, h, 0:SEQ], 0.0, ALU.mult, ALU.add))
                    c4 = cL.rearrange("p h (c t) -> p (h c) t", t=CH)
                    d4 = dL.rearrange("p h (c t) -> p (h c) t", t=CH)
                    dve.tensor_tensor(d4, c4, c4[:, :, 31:32].broadcast_to([P, GH * 4, CH]), ALU.subtract).then_inc(S("gla_dve"), 1)
            dve.wait_ge(S("proj_dve"), 16)
            dve.wait_ge(S("exps"), 2)
            q4, k4 = pT[:, 0:4, 0:SEQ], pT[:, 4:8, 0:SEQ]
            dve.tensor_tensor(qe, qe, q4, ALU.mult)
            dve.tensor_tensor(ke, ke, k4, ALU.mult)
            c4 = cL.rearrange("p h (c t) -> p (h c) t", t=CH)
            d4 = dL.rearrange("p h (c t) -> p (h c) t", t=CH)
            dve.tensor_tensor(d4, c4, c4[:, :, 63:64].broadcast_to([P, GH * 4, CH]), ALU.subtract).then_inc(S("gla_dve"), 1)
            dve.wait_ge(S("exps"), 4)
            dve.tensor_tensor(qb, q4, cL, ALU.mult)
            dve.tensor_tensor(kd, dL, k4, ALU.mult).then_inc(S("gla_dve"), 1)
            for T in range(2):
                dve.wait_ge(S("gla_pe"), GP["v_T"] + T + 1)
                dve.tensor_copy(vtok[:, T, :], PS[:, 2 * T:2 * T + 2, :].rearrange("p b n -> p (b n)")).then_inc(S("gla_dve"), 1)
            for T in range(2):
                dve.wait_ge(S("gla_pe"), GP["kd_T"] + T + 1)
                dve.tensor_copy(kdt[:, T, :], bank(4 + T)).then_inc(S("gla_dve"), 1)
            for T in range(2):
                dve.wait_ge(S("gla_pe"), GP["att"] + T + 1)
                dve.scalar_tensor_tensor(out=attS[:, T, :, :], in0=PS[:, 6 + T, 0:256].rearrange("p (h t) -> p h t", h=GH),
                                         scalar=3e38, in1=bc(K["gmask"], 1, GH), op0=ALU.min, op1=ALU.mult).then_inc(S("gla_dve"), 1)
            for c in range(4):
                dve.wait_ge(S("upd"), c + 1)
                if c:
                    dve.wait_ge(S("o"), c + 1)
                for h in range(GH):
                    src = PS[:, 4 + 2 * (c % 2) + h // 2, (h % 2) * GDV:(h % 2 + 1) * GDV]
                    if c == 0:
                        ins_ = dve.tensor_copy(Sst[:, h, :], src)
                    else:
                        ins_ = dve.scalar_tensor_tensor(out=Sst[:, h, :], in0=Sst[:, h, :], scalar=cL[:, h, c * CH + 63:c * CH + 64],
                                                        in1=src, op0=ALU.mult, op1=ALU.add)
                ins_.then_inc(S("state"), 1)
                dve.wait_ge(S("state"), c + 1)
            dve.wait_ge(S("gla_pe"), GP["kv8_T"] + 1)
            dve.tensor_copy(vtok8[0:DEC, :], PS[0:DEC, 0:2, :].rearrange("p b n -> p (b n)"))
            dv(dve.tensor_copy(ktok8[0:DEC, :], PS[0:DEC, 2, :]))
            dve.tensor_tensor(kmask[0:DEC], bc(ktok8[0:DEC, :], 1, DEC), bc(K["ident"][0:DEC, 0:DEC], 2, hk), ALU.mult).then_inc(S("gla_dve"), 1)
            for b in range(DEC):
                dve.wait_ge(S("outer"), b + 1)
                dve.wait_ge(S(f"sstate_in{b % 3}"), 16 * (b // 3 + 1))
                for h in range(GH):
                    ins_ = dve.scalar_tensor_tensor(out=sbuf3[b % 3][:, h, :], in0=sbuf3[b % 3][:, h, :], scalar=eg[:, h, b:b + 1],
                                                    in1=PS[:, 4 + 2 * (b % 2) + h // 2, (h % 2) * GDV:(h % 2 + 1) * GDV],
                                                    op0=ALU.mult, op1=ALU.add)
                ins_.then_inc(S("sstate"), 1)
            dve.wait_ge(S("so"), DEC)
            dve.tensor_copy(oT[:, :, SEQ:TOK], PS[:, 3, 0:64].rearrange("p (j b) -> p j b", b=DEC)).then_inc(S("gla_dve"), 1)
            rs4 = pT[:, 0:4, :]
            dve.wait_ge(S("o_rms"), 1)
            dv(dve.reciprocal(rs4, rs4))
            for j in range(8):
                ins_ = dve.scalar_tensor_tensor(out=oT[:, j, :], in0=oT[:, j, :], scalar=vT[:, 40 + j % 2:41 + j % 2],
                                                in1=pT[:, j // 2, :], op0=ALU.mult, op1=ALU.mult)
            dv(ins_)
            dve.tensor_tensor(oT[:], oT[:], pT[:, 16:24, :], ALU.mult).then_inc(S("mix_in"), 1)

        def act_gla():
            nb = eg.rearrange("p h b -> p (h b)")[:, 0:4]
            ac(act.mul(nb, vT[:, 42:46], -1.0))
            act.wait_ge(S("gla_pe"), GP["z"] + 1)
            for h in range(GH):
                ins_ = act.activation(Lg[:, h, :], PS[:, 4 + h, 0:TOK], ACT.Exp, bias=nb[:, h:h + 1], scale=-1.0)
            ac(ins_)
            act.activation(Lg, Lg, ACT.Ln, bias=K["ones"][:, 0:1], scale=1.0).then_inc(S("softplus"), 1)
            act.wait_ge(S("softplus"), 1)
            act.activation(eg, Lg[:, :, SEQ:TOK], ACT.Exp, scale=-1 / 16)
            act.wait_ge(S("gla_dve"), GD["dL"] + 1)
            act.activation(qe, dL, ACT.Exp, scale=-1 / 16).then_inc(S("exps"), 1)
            act.activation(ke, dL, ACT.Exp, scale=1 / 16).then_inc(S("exps"), 1)
            for m_ in range(16, 24):
                act.wait_ge(S("proj"), m_ + 1)
                act.activation(pT[:, m_, :], PS[:, m_ % 4, 0:TOK], ACT.Silu).then_inc(S("proj_act"), 1)
            act.wait_ge(S("gla_dve"), GD["dE"] + 1)
            act.activation(dL, dL, ACT.Exp, scale=1 / 16).then_inc(S("exps"), 1)
            act.activation(cL, cL, ACT.Exp, scale=-1 / 16).then_inc(S("exps"), 1)
            for c in range(4):
                act.wait_ge(S("o"), c + 1)
                act.copy(oT[:, :, c * CH:(c + 1) * CH], bank(c % 2).rearrange("p (j t) -> p j t", t=CH)).then_inc(S("o_out"), 1)
            act.wait_ge(S("gla_dve"), GD["o_all"] + 1)
            act.wait_ge(S("o_out"), 4)
            act.activation(osq, oT[:], ACT.Square).then_inc(S("o_sq"), 1)
            act.wait_ge(S("gla_pe"), GP["o_ms"] + 1)
            act.activation(pT[:, 0:4, :], PS[:, 0:4, 0:TOK], ACT.Sqrt, bias=K["eps"]).then_inc(S("o_rms"), 1)
            for i in range(3):
                act.wait_ge(S(f"sstate_out{i}"), 16 * len(range(i, DEC, 3)))
            act.wait_ge(S("out_pool"), 16)

        def pool_gla():
            pool.wait_ge(S("state"), 4)
            pool.dma_start(outs["gla_p"][0, 0].rearrange("h d v -> d h v"), Sst).then_inc(S("out_pool"), 16)
            pool.wait_ge(S("gla_pe"), GP["kv8_T"] + 1)
            pool.wait_ge(S("gla_dve"), GD["kd"] + 1)
            for b in range(DEC):
                if b >= 3:
                    pool.wait_ge(S(f"sstate_out{b % 3}"), 16 * (b // 3))
                    pool.wait_ge(S("so"), b - 2)
                pool.dma_start(sbuf3[b % 3], ins["state_gla"][0, b].rearrange("h d v -> d h v")).then_inc(S(f"sstate_in{b % 3}"), 16)
                if b >= 2:
                    store_state(b - 2)
            store_state(DEC - 2)
            store_state(DEC - 1)
            for i in range(3):
                pool.wait_ge(S(f"sstate_out{i}"), 16 * len(range(i, DEC, 3)))

        def store_state(b):
            pool.wait_ge(S("sstate"), b + 1)
            pool.dma_start(outs["gla_s"][0, b].rearrange("h d v -> d h v"), sbuf3[b % 3]).then_inc(S(f"sstate_out{b % 3}"), 16)

        tk = carver()
        xg = [tk(D) for _ in range(2)]
        xgT = [tk(KT, CAP) for _ in range(2)]
        sg = [tk(P) for _ in range(2)]
        hm = [tk(P) for _ in range(2)]
        hTt = [tk(P) for _ in range(2)]
        ysb = [tk(512) for _ in range(2)]
        hrow = tk(TT, D)
        yb = [arena[:, 4096 * i:4096 * (i + 1)].rearrange("p (k n) -> p k n", k=4) for i in range(2)]
        sgS, hsS = (arena[:, o:o + 2 * TOK].rearrange("p (k t) -> p k t", k=2) for o in (2112, 2112 + 2 * TOK))
        tk.at[0] = 8192
        s_, sel, c1, c2, msk, rep, Mf, Wt, Rr = (tk(TT, NE) for _ in range(9))
        gm = tk(24, 8)
        gs, rank = tk(24), tk(24)
        top8 = tk(TT, 8)
        wsum = tk(TT)
        Mb = tk(TT, NE, dt=BF16)
        Qall, Rall = tk(TT, NB), tk(TT, NB)
        MV = tk(NB, TT, 4, dt=BF16)
        acc = arena[:, tk.at[0]:tk.at[0] + D]
        Sel = [tk(TT, 7, P, dt=BF16) for _ in range(2)]
        QT, RT = tk(TT, P), tk(TT, P)
        cnt, nch, base, ovt = tk(1), tk(1), tk(1), tk(4)
        OV, OVb, OVc = tk(NOV), tk(NOV), tk(NOV)
        Ls = tk(NB, 4)
        t1, t2 = tk(NB), tk(NB)
        gidx, sidx = (tk(NB + 2).bitcast(I32) for _ in range(2))
        gi, si = (tk(2).bitcast(I32) for _ in range(2))
        eid, npr = tk(NOV).bitcast(I32), tk(1).bitcast(I32)
        nprf = tk(1)
        Wk = tk(TT, 8)
        wtmp = tk(8, NE)
        mix8 = tk(KT, DEC)
        wr = mrow[:, 0:KT * NE].rearrange("p (k e) -> p k e", k=KT)
        rb = mrow[:, 512:512 + NE]

        hrow_d = [nc.dram_tensor(f"h_rows{l}", (TOK, D), F32, kind="Internal").ap() for l in range(2)]
        y_d = [nc.dram_tensor(f"y_rows{l}", (TOK * TOPK * 2, D // 2), F32, kind="Internal").ap() for l in range(2)]

        PER = dict(route_w=32, logits=1, hrow_T=3, hrow_sb=3, route_exp=1, sh_gu=1, mask=1, place=1,
                   sh_h=1, sh_out=8, sh_y=8, nch=1, base=1, places=1, QR_T=1, OV=1,
                   over_T=1, sh_silu=1, hrow_out=48, acc=3, acc_T=3, acc_out=2, y_in0=48, y_in1=48,
                   y_used=6, all_scattered=1, lists=1, sel=14, sel_used=16)

        PER["route_pe"], PER["route_dve"] = 9, 5
        RP = {'logits': 0, 'hrow_T': 1, 'sh_gu': 4, 'place': 5, 'base': 6, 'QR_T': 7, 'over_T': 8}
        RD = {'mask': 0, 'sh_h': 1, 'places': 2, 'nch': 3, 'OV': 4}

        def M(l, name):
            return S(f"{name}_{l}")

        ex_base = [None, None]

        def expert_w(l, e):
            wg, wu, wd = (ins[f"moe_w_{x}"][l][e] if isinstance(e, int) else ins[f"moe_w_{x}"][l][ds(e, 1)].rearrange("a k n -> (a k) n")
                          for x in ("gate", "up", "down"))
            return [wg.rearrange("(p k) n -> p (k n)", k=KT), wu.rearrange("(p k) n -> p (k n)", k=KT),
                    wd.rearrange("(k p) n -> p k n", p=P)]

        def load_expert(s, e, l, sem):
            for t, src in enumerate(expert_w(l, e)):
                dst = ring[:, s, t, :]
                if t == 2:
                    dst = dst.rearrange("p (k n) -> p k n", k=2)
                sp.dma_start(dst, src).then_inc(sem, 16)

        def sp_router(l):
            sp.wait_ge(S("mod_fold"), 16) if l == 0 else sp.wait_ge(S("mix_in"), 2)
            sp.dma_start(wr, ins["moe_w_router"][l].rearrange("(k p) e -> p k e", p=P)).then_inc(S("route_w"), 16)
            sp.dma_start(rb, ins["moe_router_bias"][l:l + 1, :].broadcast_to([P, NE])).then_inc(S("route_w"), 16)

        def sp_moe(l):
            load_item(it_sh[l], [cols(ins["shared_w_gate"][l], 0), cols(ins["shared_w_up"][l], 0),
                                 ins["shared_w_down"][l].rearrange("(k p) n -> p k n", p=P)])

        def sp_experts_first(l):
            for u in range(WS):
                s, n = it_ex[l][u]
                sp.wait_ge(S(f"slot_used{s}"), slot_prior(it_ex[l][u]))
                load_expert(s, u, l, S(f"slot_loaded{s}"))

        def slot_prior(item):
            return prior[item]

        def sp_experts(l):
            with sp.Fori(1, NE // WS) as i:
                for u in range(WS):
                    s = it_ex[l][u][0]
                    sp.wait_ge(M(l, "y"), i * WS + (u - WS + 1))
                    load_expert(s, i * WS + u, l, S(f"slot_loaded{s}"))
            sp.wait_ge(S("lists"), PER["lists"] * l + 1)
            n2 = sp.value_load(npr[0:1, 0:1], min_val=1, max_val=NOV // 2)
            with sp.Fori(0, n2) as i:
                for u in range(2):
                    sp.wait_ge(M(l, "y"), i * 2 + (NE + u - 1))
                    e = sp.value_load(eid[0:1, ds(i * 2 + u, 1)], min_val=0, max_val=NE - 1)
                    load_expert(it_ex[l][u][0], e, l, M(l, f"over_loaded{u}"))

        def pe_route(l):
            pe.wait_ge(S("h_ready"), 2 * l + 2)
            pe.wait_ge(S("route_w"), PER["route_w"] * l + 32)
            for T in range(TT):
                for k in range(KT):
                    m = pe.matmul(PS[:, 0, T * NE:(T + 1) * NE], hT[:, k, T * P:(T + 1) * P], wr[:, k, :], start=(k == 0), stop=(k == KT - 1))
            m.then_inc(S("route_pe"), 1)
            for T in range(TT):
                n = P if T < 2 else DEC
                for half in range(2):
                    for k in range(4):
                        m = pe.transpose(PS[0:n, 1 + 2 * T + half, k * P:(k + 1) * P], hT[:, 4 * half + k, T * P:T * P + n], K["ident"])
                m.then_inc(S("route_pe"), 1)
            pe.wait_ge(S("hrow_sb"), PER["hrow_sb"] * l + 3)
            pe.wait_ge(S("route_exp"), PER["route_exp"] * l + 1)
            s = it_sh[l][0]
            item_ready(pe, it_sh[l])
            for t in range(2):
                for j in range(2):
                    for k in range(KT):
                        m = pe.matmul(PS[:, 4 + 2 * t + j, 0:TOK], third(s, t)[:, k, j * P:(j + 1) * P], hT[:, k, 0:TOK], start=(k == 0), stop=(k == KT - 1))
            m.then_inc(S("route_pe"), 1)
            pe.wait_ge(S("route_dve"), PER["route_dve"] * l + RD["mask"] + 1)
            for T in range(TT):
                for T2 in range(T + 1):
                    m = pe.matmul(PS[:, 1, T * NE:(T + 1) * NE], (triB if T2 == T else onesB)[:], Mb[:, T2, :], start=(T2 == 0), stop=(T2 == T))
            for T in range(TT):
                m = pe.matmul(PS[0:NE, 2, 0:1], Mb[:, T, :], onesB[:, 0:1], start=(T == 0), stop=(T == TT - 1))
            m.then_inc(S("route_pe"), 1)
            wd2 = ring[:, s, 2, :].rearrange("p (k n) -> p k n", k=2)
            pe.wait_ge(S("route_dve"), PER["route_dve"] * l + RD["sh_h"] + 1)
            for k in range(KT):
                if k >= 4:
                    pe.wait_ge(S("sh_out"), PER["sh_out"] * l + (k - 3))
                for kk in range(2):
                    m = pe.matmul(PS[:, 4 + k % 4, 0:TOK], wd2[:, kk, k * P:(k + 1) * P], hsS[:, kk, :], start=(kk == 0), stop=(kk == 1))
                m.then_inc(S("sh_y"), 1)
            pe.wait_ge(S("sh_y"), PER["sh_y"] * l + KT)
            pe.sem_inc(S(f"slot_used{s}"), 1)
            pe.wait_ge(S("route_dve"), PER["route_dve"] * l + RD["nch"] + 1)
            m = pe.matmul(PS[0:NE, 2, 8:9], K["tri"][0:NE, 0:NE], nch[0:NE, :], start=True, stop=True)
            m.then_inc(S("route_pe"), 1)
            pe.wait_ge(S("route_dve"), PER["route_dve"] * l + RD["places"] + 1)
            pe.wait_ge(S("sh_out"), PER["sh_out"] * l + KT)
            for T in range(TT):
                m = pe.transpose(PS[0:NE, 3, T * P:(T + 1) * P], Qall[:, T, 0:NE], K["ident"])
                m = pe.transpose(PS[0:NE, 4, T * P:(T + 1) * P], Rall[:, T, 0:NE], K["ident"])
            m.then_inc(S("route_pe"), 1)
            pe.wait_ge(S("route_dve"), PER["route_dve"] * l + RD["OV"] + 1)
            for T in range(TT):
                m = pe.matmul(PS[:, 5, T * NOV:(T + 1) * NOV], QT[0:NE, T, :], OV[0:NE, :], start=True, stop=False)
                m = pe.matmul(PS[:, 5, T * NOV:(T + 1) * NOV], K["ones1024"][0:NE, :], OVc[0:NE, :], start=False, stop=True)
                m = pe.matmul(PS[:, 7, T * NOV:(T + 1) * NOV], RT[0:NE, T, :], OV[0:NE, :], start=True, stop=True)
            m = pe.matmul(PS[0:1, 2, 16:16 + NOV], K["pcol"][0:NE, :], OV[0:NE, :], start=True, stop=True)
            m = pe.matmul(PS[0:1, 2, 64:65], K["ones"][0:NE, :], nch[0:NE, :], start=True, stop=True)
            m.then_inc(S("route_pe"), 1)
            pe.sem_inc(S("sel_used"), 2)
            with pe.Fori(0, 7) as i:
                for u in range(2):
                    pe.wait_ge(S("sel"), PER["sel"] * l + (i * 2 + (u + 1)))
                    for j in range(7):
                        for T in range(TT):
                            m = pe.matmul(PS[:, 6, ds(i * 56 + (28 * u + 4 * j), 4)], Sel[u][:, T, j, :],
                                          MV[:, ds(i * 14 + (7 * u + j), 1), T, :].rearrange("p a c -> p (a c)"), start=(T == 0), stop=(T == TT - 1))
                    m.then_inc(S("sel_used"), 1)

        def pe_body(l, n, h2, u, s, wsem, wval):
            b = u % 2
            wait_alone(pe, M(l, f"gathered{b}"), h2 * 16 + 16)
            xv = xg[b][0:CAP, :].rearrange("t (p k) -> t k p", k=KT)
            for k in range(KT):
                m = pe.transpose(PS[:, b, k * CAP:(k + 1) * CAP], xv[:, k, :], K["ident"][0:CAP, 0:CAP])
            m.then_inc(M(l, "tx"), 1)
            pe.wait_ge(M(l, "xgT"), n + 1)
            pe.wait_ge(wsem, wval)
            gu = ring[:, s, 0:2, :].rearrange("p g (k n) -> p g k n", k=KT)
            for k in range(KT):
                for half in range(2):
                    m = pe.matmul(PS[64 * half:64 * half + 64, 2 + b, 0:256].rearrange("p (g n) -> p g n", g=2), xgT[b][:, k, :],
                                  gu[:, :, k, half * P:(half + 1) * P], start=(k == 0), stop=(k == KT - 1), skip_group_check=True)
            m.then_inc(M(l, "gu"), 1)
            pe.wait_ge(M(l, "hm"), n + 1)
            pe.transpose(PS[:, 4 + b, 0:P], hm[b], K["ident"]).then_inc(M(l, "th"), 1)
            pe.wait_ge(M(l, "hT"), n + 1)
            for kk in range(2):
                for j in range(2):
                    m = pe.matmul(PS[64 * j:64 * j + 64, 6 + b, :], hTt[b][:, kk * CAP:(kk + 1) * CAP],
                                  ring[:, s, 2, kk * D + 512 * j:kk * D + 512 * j + 512], start=(kk == 0), stop=(kk == 1), skip_group_check=True)
            m.then_inc(M(l, "y"), 1)

        def main_and_overflow(eng, l, body, first_apart=False):
            if first_apart:
                for u in range(WS):
                    body(0, u, u // 2, u, False)
            with eng.Fori(int(first_apart), NE // WS) as i:
                for u in range(WS):
                    body(i, i * WS + u, i * 2 + u // 2, u, False)
            eng.wait_ge(S("lists"), PER["lists"] * l + 1)
            n2 = eng.value_load(npr[0:1, 0:1], min_val=1, max_val=NOV // 2)
            with eng.Fori(0, n2) as i:
                for u in range(2):
                    body(i, i * 2 + (NE + u), i + NE // 2, u, True)
            return n2

        def pe_experts(l):
            pe.wait_ge(S("lists"), PER["lists"] * l + 1)

            def body(i, n, h2, u, over):
                s, first = it_ex[l][u]
                if over:
                    pe_body(l, n, h2, u, s, M(l, f"over_loaded{u}"), i * 48 + 48)
                else:
                    pe_body(l, n, h2, u, s, S(f"slot_loaded{s}"), i * 48 + 48 * first)
            n2 = main_and_overflow(pe, l, body)
            pe.wait_ge(M(l, "y"), n2 * 2 + NE)
            pe.sem_inc(S("over_done"), 1)

        def pe_combine(l):
            for T in range(TT):
                n = P if T < 2 else DEC
                pe.wait_ge(S("acc"), PER["acc"] * l + (T + 1))
                if T:
                    pe.wait_ge(S("acc_out"), PER["acc_out"] * l + T)
                for k in range(KT):
                    m = pe.transpose(PS[:, k // 4, (k % 4) * P:(k % 4) * P + n], acc[0:n, k * P:(k + 1) * P], K["ident"][0:n, 0:n])
                m.then_inc(S("acc_T"), 1)

        def dve_route(l):
            dve.wait_ge(S("route_exp"), PER["route_exp"] * l + 1)
            f = lambda a: a.rearrange("p t e -> p (t e)")
            dv(dve.tensor_scalar(s_, s_, 1.0, None, ALU.add))
            dv(dve.reciprocal(s_, s_))
            dv(dve.tensor_tensor(sel, s_, bc(rb, 1, TT), ALU.add))
            for j in range(24):
                ins_ = dve.max(gm[:, j, :], f(sel)[:, 8 * j:8 * j + 8])
            dv(ins_)
            dv(dve.tensor_tensor(gs, gm[:, :, 0], gm[:, :, 1], ALU.add))
            g3 = gs.rearrange("p (t g) -> p t g", g=8)
            v4 = lambda a: a.rearrange("p t (g h) -> p t g h", g=8)
            dv(dve.tensor_tensor(v4(c1), bc(g3, 2, 8), bc(g3, 3, 8), ALU.is_gt))
            dv(dve.tensor_tensor(v4(c2), bc(g3, 2, 8), bc(g3, 3, 8), ALU.is_equal))
            dv(dve.tensor_tensor(c2, c2, bc(K["gtri"], 1, TT), ALU.mult))
            dv(dve.tensor_tensor(c1, c1, c2, ALU.add))
            dv(dve.tensor_reduce(rank, f(c1).rearrange("p (g h) -> p g h", h=8), AX, ALU.add))
            dv(dve.tensor_scalar(rank, rank, TOPG - 0.5, NEG, ALU.is_ge, ALU.mult))
            dv(dve.tensor_tensor(f(msk).rearrange("p (g h) -> p g h", h=8), f(sel).rearrange("p (g h) -> p g h", h=8), bc(rank, 2, 8), ALU.add))
            for T in range(TT):
                ins_ = dve.max(top8[:, T, :], msk[:, T, :])
            dv(ins_)
            for T in range(TT):
                ins_ = dve.match_replace(rep[:, T, :], top8[:, T, :], msk[:, T, :], GONE)
            dv(ins_)
            dv(dve.tensor_scalar(Mf, rep, GONE, None, ALU.is_equal))
            dv(dve.tensor_tensor(Wt, s_, Mf, ALU.mult))
            dv(dve.tensor_reduce(wsum, Wt, AX, ALU.add))
            dv(dve.reciprocal(wsum, wsum))
            dv(dve.tensor_scalar(wsum, wsum, ROUTE_SCALE, None, ALU.mult))
            dv(dve.tensor_tensor(Wt, Wt, bc(wsum, 2, NE), ALU.mult))
            dv(dve.tensor_tensor(Mf, Mf, bc(K["valid"], 2, NE), ALU.mult))
            dve.tensor_copy(Mb, Mf).then_inc(S("route_dve"), 1)
            for T in range(TT):
                ins_ = dve.tensor_tensor_scan(Rr[:, T, :], K["ones"].broadcast_to([P, NE]), Mf[:, T, :], 0.0, ALU.mult, ALU.add)
            dv(ins_)
            dv(dve.tensor_scalar(Rall[:, :, 0:NE], Rr, 1.0, None, ALU.subtract))
            dve.wait_ge(S("sh_silu"), PER["sh_silu"] * l + 1)
            dve.tensor_tensor(hsS, sgS, PS[:, 6:8, 0:TOK], ALU.mult).then_inc(S("route_dve"), 1)
            dve.wait_ge(S("route_pe"), PER["route_pe"] * l + RP["place"] + 1)
            dve.scalar_tensor_tensor(out=Qall[:, :, 0:NE], in0=PS[:, 1, 0:192].rearrange("p (t e) -> p t e", e=NE), scalar=1.0,
                                     in1=Mf, op0=ALU.add, op1=ALU.mult).then_inc(S("route_dve"), 1)
            dv(dve.tensor_copy(cnt[0:NE, :], PS[0:NE, 2, 0:1]))
            dv(dve.tensor_scalar(ovt[0:NE, :], K["iota"][0:NE, 1:5], float(CAP), cnt[0:NE, :], ALU.mult, ALU.is_lt))
            dve.tensor_reduce(nch[0:NE, :], ovt[0:NE, :], AX, ALU.add).then_inc(S("route_dve"), 1)
            dve.wait_ge(S("route_pe"), PER["route_pe"] * l + RP["base"] + 1)
            dv(dve.tensor_copy(base[0:NE, :], PS[0:NE, 2, 8:9]))
            dv(dve.tensor_scalar(OVc[0:NE, :], K["iota"][0:NE, :], base[0:NE, :], None, ALU.is_ge))
            dv(dve.tensor_scalar(OVb[0:NE, :], K["iota"][0:NE, :], base[0:NE, :], None, ALU.subtract))
            dve.wait_ge(S("route_dve"), PER["route_dve"] * l + RD["nch"] + 1)
            dv(dve.scalar_tensor_tensor(out=OV[0:NE, :], in0=OVb[0:NE, :], scalar=nch[0:NE, :], in1=OVc[0:NE, :], op0=ALU.is_lt, op1=ALU.mult))
            dv(dve.tensor_scalar(OVb[0:NE, :], OVb[0:NE, :], 1.0, -1024.0 * CAP, ALU.add, ALU.mult))
            dv(dve.tensor_tensor(OVc[0:NE, :], OVb[0:NE, :], OV[0:NE, :], ALU.mult))
            dve.wait_ge(S("route_pe"), PER["route_pe"] * l + RP["QR_T"] + 1)
            dve.tensor_copy(QT[0:NE], PS[0:NE, 3, 0:384].rearrange("p (t c) -> p t c", c=P))
            dve.tensor_copy(RT[0:NE], PS[0:NE, 4, 0:384].rearrange("p (t c) -> p t c", c=P)).then_inc(S("route_dve"), 1)
            dve.wait_ge(S("route_pe"), PER["route_pe"] * l + RP["over_T"] + 1)
            dve.tensor_copy(Qall[:, :, NE:NB], PS[:, 5, 0:TT * NOV].rearrange("p (t e) -> p t e", e=NOV))
            dve.tensor_copy(Rall[:, :, NE:NB], PS[:, 7, 0:TT * NOV].rearrange("p (t e) -> p t e", e=NOV))
            dve.tensor_copy(eid[0:1, :], PS[0:1, 2, 16:16 + NOV])
            dv(dve.tensor_scalar(nprf[0:1, :], PS[0:1, 2, 64:65], 0.5, 0.25, ALU.mult, ALU.add))
            dve.tensor_scalar(npr[0:1, :], nprf[0:1, :], 1.0, None, ALU.max)
            dve.tensor_copy(MV[:, :, :, 0], bc(K["pcol"].broadcast_to([P, TT]), 1, NB))
            for T in range(TT):
                dve.memset(MV[:, :, T, 1:2], float(T))
            dve.memset(MV[:, :, :, 3:4], 1.0)
            dve.memset(gidx, 0)
            dv(dve.tensor_copy(MV[:, :, :, 2], Rall.rearrange("p t b -> p b t")))
            with dve.Fori(0, 7) as i:
                for u in range(2):
                    dve.wait_ge(S("sel_used"), PER["sel_used"] * l + (i * 2 + (u + 1)))
                    for T in range(TT):
                        ins_ = dve.tensor_tensor(Sel[u][:, T], bc(slotB[:], 1, 7), bc(Qall[:, T, ds(i * 14 + 7 * u, 7)], 2, P), ALU.is_equal)
                    ins_.then_inc(S("sel"), 1)
            for T in range(TT):
                for r in range(8):
                    ins_ = dve.scalar_tensor_tensor(out=wtmp[:, r, :], in0=Rall[:, T, 0:NE], scalar=float(r), in1=Wt[:, T, :], op0=ALU.is_equal, op1=ALU.mult)
                dv(ins_)
                dv(dve.tensor_tensor(wtmp, wtmp, bc(Mf[:, T, :], 1, 8), ALU.mult))
                dv(dve.tensor_reduce(Wk[:, T, :], wtmp, AX, ALU.add))
            dve.wait_ge(S("sel_used"), PER["sel_used"] * l + 16)
            dv(dve.tensor_copy(Ls, PS[:, 6, 0:NB * 4].rearrange("p (b c) -> p b c", c=4)))
            dv(dve.scalar_tensor_tensor(out=t1, in0=Ls[:, :, 1], scalar=128.0, in1=Ls[:, :, 0], op0=ALU.mult, op1=ALU.add))
            dve.tensor_copy(gidx[:, 0:NB], t1)
            dv(dve.tensor_scalar(t2, t1, 16.0, K["jcol"], ALU.mult, ALU.add))
            dv(dve.scalar_tensor_tensor(out=t2, in0=Ls[:, :, 2], scalar=2.0, in1=t2, op0=ALU.mult, op1=ALU.add))
            dv(dve.scalar_tensor_tensor(out=t2, in0=Ls[:, :, 3], scalar=-float(OOB), in1=t2, op0=ALU.mult, op1=ALU.add))
            dve.tensor_copy(sidx[:, 0:NB], t2).then_inc(S("lists"), 1)

        def dve_experts(l):
            def body(i, n, h2, u, over):
                b = u % 2
                dve.wait_ge(M(l, "sg"), n + 1)
                dve.tensor_tensor(hm[b], sg[b], PS[:, 2 + b, P:2 * P], ALU.mult).then_inc(M(l, "hm"), 1)
                dve.wait_ge(M(l, "y"), n + 1)
                if not isinstance(n, int) or n >= 2:
                    dve.wait_ge(M(l, f"scattered{b}"), h2 * 16)
                dve.tensor_copy(ysb[b], bank(6 + b)).then_inc(M(l, "ysb"), 1)
            main_and_overflow(dve, l, body, True)

        def dve_combine(l):
            for T in range(TT):
                n = P if T < 2 else DEC
                if T:
                    dve.wait_ge(S("acc_T"), PER["acc_T"] * l + T)
                for half in range(2):
                    j = 2 * T + half
                    dve.wait_ge(S(f"y_in{half}"), PER["y_in0"] * l + 16 * (T + 1))
                    for r in range(4):
                        src, w = yb[half][0:n, r, :], Wk[0:n, T, 4 * half + r:4 * half + r + 1]
                        if half == 0 and r == 0:
                            dv(dve.tensor_scalar(acc[0:n, :], src, w, None, ALU.mult))
                        else:
                            ins_ = dve.scalar_tensor_tensor(out=acc[0:n, :], in0=src, scalar=w, in1=acc[0:n, :], op0=ALU.mult, op1=ALU.add)
                            dv(ins_)
                    dve.sem_inc(S("y_used"), 1)
                dve.sem_inc(S("acc"), 1)
                dve.wait_ge(S("acc_T"), PER["acc_T"] * l + (T + 1))
                if T < 2:
                    c0 = T * P
                    for half in range(2):
                        sh = shT[:, 4 * half:4 * half + 4, c0:c0 + P]
                        ins_ = dve.tensor_tensor(sh, PS[:, half, :].rearrange("p (k t) -> p k t", k=4), sh, ALU.add)
                    dv(ins_)
                    for k in range(KT):
                        ins_ = dve.scalar_tensor_tensor(out=xT[:, k, c0:c0 + P], in0=shT[:, k, c0:c0 + P], scalar=modT2[:, l, 40 + k, 0:1],
                                                        in1=xT[:, k, c0:c0 + P], op0=ALU.mult, op1=ALU.add)
                    ins_.then_inc(S("acc_out"), 1)
                else:
                    for half in range(2):
                        ins_ = dve.tensor_tensor(mix8[:, 4 * half:4 * half + 4, :], PS[:, half, :].rearrange("p (k t) -> p k t", k=4)[:, :, 0:DEC],
                                                 shT[:, 4 * half:4 * half + 4, SEQ:TOK], ALU.add)
                    dv(ins_)
                    dv(dve.tensor_tensor(mix8, mix8, modT2[:, l, 40:48, 1:9], ALU.mult))
                    dv(dve.tensor_tensor(xT[:, :, SEQ:TOK], xT[:, :, SEQ:TOK], mix8, ALU.add))
            dve.wait_ge(S("acc_out"), PER["acc_out"] * l + 2)
            dve.sem_inc(S("x_new"), 1)

        def act_route(l):
            act.wait_ge(S("route_pe"), PER["route_pe"] * l + RP["logits"] + 1)
            act.activation(s_, PS[:, 0, 0:192].rearrange("p (t e) -> p t e", e=NE), ACT.Exp, scale=-1.0).then_inc(S("route_exp"), 1)
            for T in range(TT):
                n = P if T < 2 else DEC
                act.wait_ge(S("route_pe"), PER["route_pe"] * l + RP["hrow_T"] + (T + 1))
                act.copy(hrow[0:n, T, :], PS[0:n, 1 + 2 * T:3 + 2 * T, :].rearrange("p b n -> p (b n)")).then_inc(S("hrow_sb"), 1)
                act.wait_ge(S("hrow_sb"), PER["hrow_sb"] * l + (T + 1))
                act.dma_start(hrow_d[l][T * P:T * P + n, :], hrow[0:n, T, :]).then_inc(S("hrow_out"), 16)
            act.wait_ge(S("route_pe"), PER["route_pe"] * l + RP["sh_gu"] + 1)
            act.activation(sgS, PS[:, 4:6, 0:TOK], ACT.Silu).then_inc(S("sh_silu"), 1)
            for k in range(KT):
                act.wait_ge(S("sh_y"), PER["sh_y"] * l + (k + 1))
                act.copy(shT[:, k, :], PS[:, 4 + k % 4, 0:TOK]).then_inc(S("sh_out"), 1)

        def act_experts(l):
            def body(i, n, h2, u, over):
                b = u % 2
                act.wait_ge(M(l, "tx"), n + 1)
                act.copy(xgT[b].rearrange("p k c -> p (k c)"), bank(b)).then_inc(M(l, "xgT"), 1)
                act.wait_ge(M(l, "gu"), n + 1)
                act.activation(sg[b], PS[:, 2 + b, 0:P], ACT.Silu).then_inc(M(l, "sg"), 1)
                act.wait_ge(M(l, "th"), n + 1)
                act.copy(hTt[b], PS[:, 4 + b, 0:P]).then_inc(M(l, "hT"), 1)
            main_and_overflow(act, l, body)

        def act_combine(l):
            act.wait_ge(S("all_scattered"), PER["all_scattered"] * l + 1)
            for T in range(TT):
                n = P if T < 2 else DEC
                for half in range(2):
                    if T:
                        act.wait_ge(S("y_used"), PER["y_used"] * l + (2 * (T - 1) + half + 1))
                    src = y_d[l].rearrange("(t k j) n -> t k (j n)", k=TOPK, j=2)[T * P:T * P + n, 4 * half:4 * half + 4, :]
                    act.dma_start(yb[half][0:n], src).then_inc(S(f"y_in{half}"), 16)

        def pool_experts(l):
            pool.wait_ge(S("lists"), PER["lists"] * l + 1)
            pool.wait_ge(S("hrow_out"), PER["hrow_out"] * l + 48)

            def gather(n1, b):
                pool.tensor_copy(gi[0:CAP, b:b + 1], gidx[0:CAP, ds(n1, 1)]).then_inc(M(l, "gi"), 1)
                wait_alone(pool, M(l, "gi"), n1 + 1)
                pool.indirect_dma_start(out=xg[b][0:CAP, :], out_offset=None, in_=hrow_d[l],
                                        in_offset=IndirectOffsetOnAxis(ap=gi[0:CAP, b:b + 1], axis=0)).then_inc(M(l, f"gathered{b}"), 16)

            gather(0, 0)

            def body(i, n, h2, u, over):
                b = u % 2
                if not isinstance(n, int) or n:
                    wait_alone(pool, M(l, "tx"), n)
                gather(n + 1, 1 - b)
                if not isinstance(n, int) or n >= 2:
                    wait_alone(pool, M(l, f"scattered{b}"), h2 * 16)
                pool.tensor_copy(si[:, b:b + 1], sidx[:, ds(n, 1)]).then_inc(M(l, "si"), 1)
                pool.wait_ge(M(l, "si"), n + 1)
                wait_alone(pool, M(l, "ysb"), n + 1)
                pool.indirect_dma_start(out=y_d[l], out_offset=IndirectOffsetOnAxis(ap=si[:, b:b + 1], axis=0),
                                        in_=ysb[b], in_offset=None, bounds_check=2 * TOK * TOPK - 1, oob_is_err=False).then_inc(M(l, f"scattered{b}"), 16)
            n2 = main_and_overflow(pool, l, body, True)
            pool.wait_ge(M(l, "gathered0"), n2 * 16 + (NE // 2 + 1) * 16)
            for b in range(2):
                pool.wait_ge(M(l, f"scattered{b}"), n2 * 16 + NE // 2 * 16)
            pool.sem_inc(S("all_scattered"), 1)

        bias_d = nc.dram_tensor("bias_rows", (AH, P, 384), F32, kind="Internal").ap()
        ohb = arena[:, 7000:7384]
        relb = arena[:, 7384:7400]
        brw = [arena[:, 7400 + 384 * i:7784 + 384 * i] for i in range(2)]

        def sp_bias():
            sp.dma_start(ohb[0:32, :], ins["onehot"]).then_inc(S("bias_in"), 16)
            sp.dma_start(relb[0:32, :], ins["rel_bias"]).then_inc(S("bias_in"), 16)

        def pe_bias():
            pe.wait_ge(S("bias_in"), 32)
            pe.wait_ge(S("x_out_of_psum"), 1)
            for h in range(AH):
                if h >= 2:
                    pe.wait_ge(S("bias_sb"), h - 1)
                pe.matmul(PS[:, 6 + h % 2, 0:384], relb[0:32, h:h + 1].broadcast_to([32, P]), ohb[0:32, :],
                          start=True, stop=True).then_inc(S("bias_mm"), 1)

        def dve_bias():
            for h in range(AH):
                dve.wait_ge(S("bias_mm"), h + 1)
                if h >= 2:
                    dve.wait_ge(S(f"bias_out{h % 2}"), 16 * (h // 2))
                dve.tensor_copy(brw[h % 2], PS[:, 6 + h % 2, 0:384]).then_inc(S("bias_sb"), 1)

        def pool_bias():
            for h in range(AH):
                pool.wait_ge(S("bias_sb"), h + 1)
                pool.dma_start(bias_d[h], brw[h % 2]).then_inc(S(f"bias_out{h % 2}"), 16)

        tk = carver()
        qT = tk(8, TOK)
        kT, vTt = tk(2, TOK), tk(2, TOK)
        qiT = tk(4, TOK)
        kiT = tk(TOK)
        ktk, vtk = tk(2, 256), tk(2, 256)
        kitk = tk(2, IDH)
        k8, v8 = tk(256), tk(256)
        ki8 = tk(IDH)
        wtk = tk(2, IH)
        w8 = tk(IH)
        ptab = tk(P).bitcast(I32)
        relb2 = tk(AH)
        m8 = tk(2, 8)
        nm, rs, mx = tk(4), tk(4), tk(4)
        wS, mxn = tk(1), tk(4)
        Pn = tk(P)
        DSA0 = tk.at[0]
        Mb_ = tk(AH, 256)
        sc, sw = tk(384), tk(384)
        rl = [tk(384) for _ in range(2)]
        A2 = [tk(4, 256) for _ in range(2)]
        PTs = [tk(2, 4, P) for _ in range(2)]
        tk = carver()
        tk.at[0] = DSA0
        Sx, Wx = tk(2052), tk(2052)
        KTs = [tk(2, 512) for _ in range(2)]
        raw = [tk(4, 256) for _ in range(2)]
        Qs = tk(2, 1152)
        Qb, kin2, rbx = mrow[:, 0:320], mrow[:, 320:324], mrow[:, 384:512]
        PT = Wx[:, 0:2048].rearrange("p (j c) -> p j c", c=P)
        iraw = [r.rearrange("p j (a r d) -> p (j a) r d", r=2, d=IDH)[:, 0:4] for r in raw]
        xi = KTs[0].rearrange("p a b -> p (a b)")[:, 0:64]
        qi8 = KTs[1].rearrange("p a b -> p (a b)")[:, 0:512]
        dsq = A2[0].rearrange("p a b -> p (a b)")[:, 0:TOK]
        lrs = A2[1].rearrange("p a b -> p (a b)")[:, 0:TOK]

        PE_STEP = {n: i + 1 for i, n in enumerate(("wi", "ki_mean", "ki_var", "kv_T", "qi8_T", "qi_half", "ik_new", "iscore", "slogit", "pn", "so_done"))}
        DVE_STEP = {n: i + 1 for i, n in enumerate(("ki_sq", "ki_ln", "kv_tok", "qi8", "Qb", "irelu", "iscore_sb", "smask", "snmax", "sprob", "pn_sb"))}

        def sp_dsa():
            sp.wait_ge(S("over_done"), 1)
            wq = w_dsa
            load_item(it_dsa[0], [cols(wq, 0), cols(wq, 256), cols(wq, 1024)])
            load_item(it_dsa[1], [cols(wq, 512), cols(wq, 768), cols(wq, 1280)])
            s, n = it_dsa[2]
            sem = S(f"slot_loaded{s}")
            for t in range(2):
                sp.dma_start(third(s, t), cols(wq, 1536 + 256 * t)).then_inc(sem, 16)
            for n_, (c0, c1_, a, b) in enumerate(((0, 64, 2048, 2112), (64, 128, 2048, 2112), (128, 136, 2112, 2120))):
                sp.dma_start(third(s, 2)[:, :, c0:c1_], wq[:, a:b].rearrange("(k p) n -> p k n", p=P)).then_inc(sem if n_ == 2 else S("dsa_small"), 16)
            sp.wait_ge(S("x_new"), 3)
            sp.dma_start(ptab[0:1, :], ins["page_table"].rearrange("(a b) n -> a (b n)", a=1)).then_inc(S("ptab"), 16)
            sp.dma_start(relb2[0:32, :], ins["rel_bias"]).then_inc(S("relb"), 16)
            sp.wait_ge(S("bias_out0"), 128)
            sp.wait_ge(S("bias_out1"), 128)
            sp.wait_ge(S("bias_free"), 1)
            for h in range(0, AH, 4):
                src = bias_d[h:h + 4].rearrange("h p f -> h (p f)")[:, 127:127 + 383 * P].rearrange("h (p f) -> p h f", f=383)[:, :, 0:256]
                sp.dma_start(Mb_[:, h:h + 4, :], src).then_inc(S("Mb"), 16)

        def sp_page(dst, cache, idx, sem):
            pid = sp.value_load(ptab[0:1, ds(idx, 1)], min_val=0, max_val=159)
            sp.dma_start(dst, cache[ds(pid, 1)].rearrange("a k n -> (a k) n")).then_inc(sem, 16)

        def sp_dout(i):
            w = ins["dsa_w_out"][0]
            load_item(it_dout[i], [cols(w, 512 * i), cols(w, 512 * i + 256), cols(w, 512 * i)])

        def sp_pages():
            cki = ins["cache_idx_k"][0]
            ckv = [ins[n][0].rearrange("a k h d -> a k (h d)") for n in ("cache_k", "cache_v")]
            sp.wait_ge(S("ptab"), 16)
            with sp.Fori(0, 4) as jj:
                for u in range(4):
                    sp.wait_ge(S("ik_free"), jj * 4 + (u + 1))
                    for pg in range(4):
                        for r in range(2):
                            sp_page(iraw[u % 2][:, pg, r, :], cki, jj * 4 + ((2 * u + r) * NPG + pg), S(f"ik_in{u % 2}"))
            for kv, name in ((0, "k"), (1, "v")):
                if kv == 1:
                    sp_moe(1)
                with sp.Fori(0, 4) as jj:
                    for b in range(DEC):
                        sp.wait_ge(S(f"{name}p_free"), jj * 8 + (b + 1))
                        for pg in range(4):
                            sp_page(raw[b % 2][:, pg, :], ckv[kv], jj * 4 + (b * NPG + pg), S(f"{name}p_in{b % 2}"))
                if kv == 0:
                    sp_dout(1)

        def pe_dsa():
            pe.wait_ge(S("h_ready"), 3)
            tiles = []
            for Pq in range(2):
                tiles += [("q", Pq, g) for g in range(4)] + [("kv", Pq, i) for i in range(2)]
            tiles += [("qi", 2, i) for i in range(4)] + [("ki", 2, 0)]
            for j, (kind, it, g) in enumerate(tiles):
                item = it_dsa[it]
                s = item[0]
                if j in (0, 6):
                    item_ready(pe, item)
                if j == 12:
                    item_ready(pe, item)
                    pe.wait_ge(S("dsa_small"), 32)
                if j >= 4:
                    pe.wait_ge(S("dproj_dve" if j % 2 == 0 else "dproj_act"), (j - 4) // 2 + 1)
                for k in range(KT):
                    if kind == "q":
                        for r in range(2):
                            m = pe.matmul(PS[64 * r:64 * r + 64, j % 4, 0:TOK], third(s, r)[:, k, g * 64:(g + 1) * 64],
                                          hT[:, k, 0:TOK], start=(k == 0), stop=(k == KT - 1), skip_group_check=True)
                        continue
                    elif kind == "qi":
                        lhsT = third(s, g // 2)[:, k, (g % 2) * P:(g % 2 + 1) * P]
                    else:
                        lhsT = third(s, 2)[:, k, g * P:(g + 1) * P]
                    m = pe.matmul(PS[:, j % 4, 0:TOK], lhsT, hT[:, k, 0:TOK], start=(k == 0), stop=(k == KT - 1))
                m.then_inc(S("dproj"), 1)
                if j in (5, 11):
                    pe.wait_ge(S("dproj"), j + 1)
                    pe.sem_inc(S(f"slot_used{s}"), 1)
            for T in range(3):
                n = P if T < 2 else DEC
                for k in range(KT):
                    m = pe.matmul(PS[0:n, 4, 8 * T:8 * T + 8], hT[:, k, T * P:T * P + n], third(s, 2)[:, k, 128:136], start=(k == 0), stop=(k == KT - 1))
            m.then_inc(S("dsa_pe"), 1)
            pe.wait_ge(S("dsa_pe"), PE_STEP["wi"])
            pe.sem_inc(S(f"slot_used{s}"), 1)
            pe.wait_ge(S("dproj_dve"), 9)
            pe.matmul(PS[:, 5, 0:TOK], K["blk64"], kiT, start=True, stop=True).then_inc(S("dsa_pe"), 1)
            pe.wait_ge(S("dsa_dve"), DVE_STEP["ki_sq"])
            pe.matmul(PS[:, 6, 0:TOK], K["blk64"], dsq, start=True, stop=True).then_inc(S("dsa_pe"), 1)
            pe.wait_ge(S("dsa_dve"), DVE_STEP["ki_ln"])
            for h in range(IH):
                if h >= 4:
                    pe.wait_ge(S("relu"), h - 3)
                elif h == 0:
                    pe.wait_ge(S("dproj_act"), 8)
                r = slice(64 * (h % 2), 64 * (h % 2) + 64)
                for T in range(2):
                    m = pe.matmul(PS[:, h % 4, P * T:P * T + P * (T + 1)], qiT[r, h // 2, T * P:(T + 1) * P], kiT[r, 0:P * (T + 1)], start=True, stop=True)
                m.then_inc(S("isc"), 1)
            for T in range(2):
                for i in range(2):
                    pe.transpose(PS[:, 4, 256 * T + P * i:256 * T + P * i + P], kT[:, i, T * P:(T + 1) * P], K["ident"])
                    pe.transpose(PS[:, 5, 256 * T + P * i:256 * T + P * i + P], vTt[:, i, T * P:(T + 1) * P], K["ident"])
                pe.transpose(PS[:, 6, 64 * T:64 * T + 64], kiT[0:64, T * P:(T + 1) * P], K["ident"][0:64, 0:64])
            for i in range(2):
                pe.transpose(PS[0:DEC, 7, P * i:P * i + P], kT[:, i, SEQ:TOK], K["ident"])
                pe.transpose(PS[0:DEC, 7, 256 + P * i:256 + P * i + P], vTt[:, i, SEQ:TOK], K["ident"])
            pe.transpose(PS[0:DEC, 6, 128:192], kiT[0:64, SEQ:TOK], K["ident"][0:64, 0:64]).then_inc(S("dsa_pe"), 1)
            pe.wait_ge(S("relu"), IH)
            pe.wait_ge(S("dsa_dve"), DVE_STEP["kv_tok"])
            for it in range(9):
                T, kv = it // 4, it % 4
                if it < 8:
                    if it >= 1:
                        pe.wait_ge(S("logit_sb"), it)
                    r = slice(64 * (kv % 2), 64 * (kv % 2) + 64)
                    for g in range(4):
                        m = pe.matmul(PS[:, g // 2, 256 * (g % 2):256 * (g % 2) + P * (T + 1)], qT[r, (kv // 2) * 4 + g, T * P:(T + 1) * P],
                                      kT[r, kv // 2, 0:P * (T + 1)], start=True, stop=True)
                    m.then_inc(S("asc"), 1)
                if it >= 1:
                    T, kv = (it - 1) // 4, (it - 1) % 4
                    b2 = (it - 1) % 2
                    pe.wait_ge(S("probs"), it)
                    for st in range(T + 1):
                        for g in range(4):
                            m = pe.transpose(PS[:, 4 + 2 * b2 + st, g * P:(g + 1) * P], A2[b2][:, g, st * P:(st + 1) * P], K["ident"])
                    m.then_inc(S("p_T"), 1)
                    pe.wait_ge(S("p_T_sb"), it)
                    if it == 5:
                        pe.wait_ge(S("att_o_sb"), 1)
                    for g in range(4):
                        ft = kv * 2 + g // 2
                        for st in range(T + 1):
                            m = pe.matmul(PS[64 * (g % 2):64 * (g % 2) + 64, 2 + ft // 4, (ft % 4) * P:(ft % 4 + 1) * P],
                                          vtk[:, st, kv * 64:(kv + 1) * 64], PTs[b2][:, st, g, :], start=(st == 0), stop=(st == T))
                    m.then_inc(S("pv"), 1)
            pe.wait_ge(S("att_o_sb"), 2)
            pe.sem_inc(S("ik_free"), 2)
            for i in range(4):
                m = pe.transpose(PS[0:DEC, 0, P * i:(i + 1) * P], qiT[:, i, SEQ:TOK], K["ident"])
            m.then_inc(S("dsa_pe"), 1)
            pe.wait_ge(S("dsa_dve"), DVE_STEP["qi8"])
            for r in range(2):
                for h in range(IH):
                    m = pe.matmul(PS[64 * r:64 * r + 64, 1, h * DEC:(h + 1) * DEC], qi8[0:DEC, h * 64:(h + 1) * 64], K["ident"][0:DEC, 0:DEC], start=True, stop=True)
            m = pe.matmul(PS[0:64, 2, 0:1], xi[0:DEC, :], K["ones"][0:DEC, :], start=True, stop=True)
            m.then_inc(S("dsa_pe"), 1)
            pe.wait_ge(S("dsa_dve"), DVE_STEP["Qb"])
            Qbv = Qb[:, 0:256].rearrange("p (u c) -> p u c", c=64)
            with pe.Fori(0, 4) as jj:
                for u in range(4):
                    b2 = u % 2
                    pe.wait_ge(S(f"ik_in{b2}"), jj * 256 + (128 + 128 * (u // 2)))
                    for pg in range(4):
                        m = pe.transpose(PS[:, 4 + b2, pg * P:(pg + 1) * P], iraw[b2][:, pg, :, :].rearrange("p r d -> p (r d)"), K["ident"])
                    m.then_inc(S("ik_free"), 1)
                    wait_alone(pe, S("ik_sb"), jj * 4 + (u + 1))
                    m = pe.matmul(PS[0:64, ds(jj, 1), :].rearrange("p a b -> p (a b)"), Qbv[:, u, :], KTs[b2].rearrange("p a b -> p (a b)")[:, 0:512], start=(u == 0), stop=(u == 3))
            for u in range(4):
                m = pe.matmul(PS[0:64, 6, 0:1], Qbv[:, u, :], kin2[:, u:u + 1], start=(u == 0), stop=(u == 3))
            m.then_inc(S("dsa_pe"), 1)
            pe.wait_ge(S("dsa_pe"), PE_STEP["ik_new"])
            pe.sem_inc(S("kp_free"), 2)
            pe.wait_ge(S("dsa_dve"), DVE_STEP["irelu"])
            for jj in range(4):
                m = pe.matmul(PS[0:DEC, jj, :], K["hsum"][0:64, :], Wx[0:64, jj * 512:(jj + 1) * 512], start=True, stop=True)
            m = pe.matmul(PS[0:DEC, 6, 8:9], K["hsum"][0:64, :], Wx[0:64, 2048:2049], start=True, stop=True)
            m.then_inc(S("dsa_pe"), 1)
            pe.wait_ge(S("dsa_dve"), DVE_STEP["iscore_sb"])
            with pe.Fori(0, 4) as jj:
                for b in range(DEC):
                    b2 = b % 2
                    pe.wait_ge(S(f"kp_in{b2}"), jj * 256 + 64 * (b // 2 + 1))
                    for Pq in range(2):
                        for pg in range(4):
                            m = pe.transpose(PS[:, 4 + 2 * b2 + Pq, pg * P:(pg + 1) * P], raw[b2][:, pg, Pq * P:(Pq + 1) * P], K["ident"])
                    m.then_inc(S("kp_free"), 1)
                    pe.wait_ge(S("kp_sb"), jj * 8 + (b + 1))
                    for Pq in range(2):
                        m = pe.matmul(PS[:, ds(jj, 1), :].rearrange("p a b -> p (a b)"), Qs[:, Pq, b * P:(b + 1) * P], KTs[b2][:, Pq, :],
                                      start=(b == 0 and Pq == 0), stop=False, skip_group_check=True)
            pe.sem_inc(S("vp_free"), 2)
            for Pq in range(2):
                for b in range(DEC):
                    m = pe.matmul(PS[:, 4, 0:1], Qs[:, Pq, b * P:(b + 1) * P], kT[:, Pq, SEQ + b:SEQ + b + 1], start=(b == 0 and Pq == 0), stop=False, skip_group_check=True)
            ohs = K["ohs"]
            b31 = lambda n: ohs[0:32, 0:1].broadcast_to([32, n])
            for jj in range(4):
                pe.matmul(PS[:, jj, 0:384], rbx[0:32, :], b31(384), start=False, stop=False, skip_group_check=True)
                pe.matmul(PS[:, jj, 384:512], rbx[0:32, :], b31(128) if jj < 3 else ohs[0:32, 0:128], start=False, stop=False, skip_group_check=True)
            pe.matmul(PS[:, 4, 0:1], rbx[0:32, :], ohs[0:32, 128:129], start=False, stop=False, skip_group_check=True)
            pe.wait_ge(S("dsa_dve"), DVE_STEP["smask"])
            for jj in range(4):
                pe.matmul(PS[:, jj, :], K["expand"][0:DEC, :], Wx[0:DEC, jj * 512:(jj + 1) * 512], start=False, stop=True, skip_group_check=True)
            pe.matmul(PS[:, 4, 0:1], K["expand"][0:DEC, :], Wx[0:DEC, 2048:2049], start=False, stop=True, skip_group_check=True).then_inc(S("dsa_pe"), 1)
            pe.wait_ge(S("dsa_dve"), DVE_STEP["sprob"])
            m = pe.matmul(PS[0:DEC, 0, 0:P], KTs[0][:, 0, 0:DEC], K["ident"], start=True, stop=True)
            m.then_inc(S("dsa_pe"), 1)
            for q in range(4):
                for j in range(4):
                    m = pe.transpose(PS[:, 4 + q, j * P:(j + 1) * P], Sx[:, (4 * q + j) * P:(4 * q + j + 1) * P], K["ident"])
                m.then_inc(S("sp_T"), 1)
            pe.wait_ge(S("dsa_dve"), DVE_STEP["pn_sb"])
            for Pq in range(2):
                m = pe.matmul(PS[:, 1, Pq * P:(Pq + 1) * P], v8[0:DEC, Pq * P:(Pq + 1) * P], Pn[0:DEC, :], start=(Pq == 0), stop=False, skip_group_check=True)
            pe.wait_ge(S("sp_sb"), 4)
            with pe.Fori(0, 4) as jj:
                for b in range(DEC):
                    b2 = b % 2
                    pe.wait_ge(S(f"vp_in{b2}"), jj * 256 + 64 * (b // 2 + 1))
                    for Pq in range(2):
                        c = b * 16 + Pq * 8
                        for pg in range(4):
                            m = pe.matmul(PS[:, 1, Pq * P + c:Pq * P + c + 8], raw[b2][:, pg, Pq * P:(Pq + 1) * P],
                                          PT[:, ds(jj * 4 + pg, 1), c:c + 8].rearrange("p a b -> p (a b)"), start=False, stop=False, skip_group_check=True)
                    m.then_inc(S("vp_free"), 1)
            pe.wait_ge(S("vp_free"), 34)
            pe.sem_inc(S("dsa_pe"), 1)
            pe.wait_ge(S("mix_in"), 2)
            pe_out_proj(it_dout, oT, 1)

        def dve_dsa():
            dsts = [qT[:, 0], qT[:, 2], kT[:, 0], qT[:, 4], qT[:, 6], vTt[:, 0], qiT[:, 0], qiT[:, 2], kiT]
            for n, dst in enumerate(dsts):
                dve.wait_ge(S("dproj"), 2 * n + 1)
                dve.tensor_copy(dst, PS[:, (2 * n) % 4, 0:TOK]).then_inc(S("dproj_dve"), 1)
            dve.wait_ge(S("dsa_pe"), PE_STEP["wi"])
            dve.tensor_scalar(wtk, PS[:, 4, 0:16].rearrange("p (t h) -> p t h", h=IH), IH ** -0.5, None, ALU.mult)
            dv(dve.tensor_scalar(w8[0:DEC, :], PS[0:DEC, 4, 16:24], IH ** -0.5, None, ALU.mult))
            dve.wait_ge(S("dsa_pe"), PE_STEP["ki_mean"])
            dv(dve.tensor_tensor(kiT, kiT, PS[:, 5, 0:TOK], ALU.subtract))
            dve.tensor_tensor(dsq, kiT, kiT, ALU.mult).then_inc(S("dsa_dve"), 1)
            dve.wait_ge(S("ki_rms"), 1)
            dv(dve.reciprocal(lrs, lrs))
            dv(dve.tensor_tensor(kiT, kiT, lrs, ALU.mult))
            dve.tensor_scalar(kiT, kiT, vT[:, 46:47], vT[:, 47:48], ALU.mult, ALU.add).then_inc(S("dsa_dve"), 1)
            for h in range(IH):
                dve.wait_ge(S("relu"), h + 1)
                for T in range(2):
                    c = slice(P * T, P * T + P * (T + 1))
                    if h == 0:
                        ins_ = dve.tensor_scalar(sc[:, c], rl[h % 2][:, c], wtk[:, T, h:h + 1], None, ALU.mult)
                    else:
                        ins_ = dve.scalar_tensor_tensor(out=sc[:, c], in0=rl[h % 2][:, c], scalar=wtk[:, T, h:h + 1], in1=sc[:, c], op0=ALU.mult, op1=ALU.add)
                ins_.then_inc(S("isum"), 1)
                dve.wait_ge(S("isum"), h + 1)
            dve.tensor_tensor(sc[:, 0:P], sc[:, 0:P], K["cau"], ALU.add)
            dv(dve.tensor_tensor(sc[:, 256:384], sc[:, 256:384], K["cau"], ALU.add))
            dve.wait_ge(S("dsa_pe"), PE_STEP["kv_T"])
            dve.tensor_copy(ktk, PS[:, 4, :].rearrange("p (t n) -> p t n", t=2))
            dve.tensor_copy(vtk, PS[:, 5, :].rearrange("p (t n) -> p t n", t=2))
            dve.tensor_copy(kitk, PS[:, 6, 0:P].rearrange("p (t n) -> p t n", t=2))
            dve.tensor_copy(k8[0:DEC, :], PS[0:DEC, 7, 0:256])
            dve.tensor_copy(v8[0:DEC, :], PS[0:DEC, 7, 256:512])
            dve.tensor_copy(ki8[0:DEC, :], PS[0:DEC, 6, 128:192]).then_inc(S("dsa_dve"), 1)
            for rnd in range(8):
                src = sc if rnd == 0 else sw
                dve.max(m8[:, 0, :], src[:, 0:P])
                dv(dve.max(m8[:, 1, :], src[:, P:384]))
                dve.match_replace(sw[:, 0:P], m8[:, 0, :], src[:, 0:P], GONE)
                dv(dve.match_replace(sw[:, P:384], m8[:, 1, :], src[:, P:384], GONE))
            dv(dve.tensor_scalar(sw, sw, GONE, NEG, ALU.not_equal, ALU.mult))
            dve.tensor_tensor(sw[:, 0:P], sw[:, 0:P], K["cau"], ALU.add)
            dv(dve.tensor_tensor(sw[:, 256:384], sw[:, 256:384], K["cau"], ALU.add))
            dve.wait_ge(S("Mb"), 64)
            for it in range(8):
                T, kv = it // 4, it % 4
                n = P * (T + 1)
                a = A2[it % 2][:, :, 0:n]
                if it >= 2:
                    dve.wait_ge(S("p_T"), it - 1)
                dve.wait_ge(S("asc"), it + 1)
                src = PS[:, 0:2, :].rearrange("p b (g n) -> p (b g) n", g=2)[:, :, 0:n]
                dve.scalar_tensor_tensor(out=a, in0=src, scalar=DH ** -0.5, in1=Mb_[:, 4 * kv:4 * kv + 4, 256 - n:256], op0=ALU.mult, op1=ALU.add).then_inc(S("logit_sb"), 1)
                dve.wait_ge(S("logit_sb"), it + 1)
                dv(dve.tensor_tensor(a, a, bc(sw[:, P * T:P * T + n], 1, 4), ALU.add))
                dv(dve.tensor_reduce(mx, a, AX, ALU.max))
                dve.tensor_scalar(nm, mx, -1.0, None, ALU.mult).then_inc(S("nmax"), 1)
                dve.wait_ge(S("pexp"), it + 1)
                dv(dve.reciprocal(rs, rs))
                dve.tensor_tensor(a, a, bc(rs, 2, n), ALU.mult).then_inc(S("probs"), 1)
            dve.wait_ge(S("att_o_sb"), 2)
            dve.memset(Qs, 0.0)
            dv(dve.memset(Qb, 0.0))
            for Pq in range(2):
                for r in range(2):
                    q = slice(64 * r, 64 * r + 64)
                    dst = Qs[q, Pq, :].rearrange("p (b x) -> p b x", x=144)[:, :, (2 * Pq + r) * 4:(2 * Pq + r) * 4 + 4]
                    dve.tensor_copy(dst, qT[q, 4 * Pq:4 * Pq + 4, SEQ:TOK].rearrange("p g b -> p b g"))
            for r in range(2):
                q = slice(64 * r, 64 * r + 64)
                ins_ = dve.tensor_copy(kin2[q, :], kiT[q, SEQ:TOK].rearrange("p (u r) -> p u r", r=2)[:, :, r])
            dve.tensor_tensor(xi[0:DEC, :].rearrange("p (b h) -> p b h", h=IH), bc(w8[0:DEC, :], 1, DEC), bc(K["ident"][0:DEC, 0:DEC], 2, IH), ALU.mult)
            dve.wait_ge(S("relb"), 16)
            dv(dve.tensor_scalar(rbx[0:32, :].rearrange("p (b h) -> p b h", h=AH), bc(relb2[0:32, :], 1, DEC), DH ** 0.5, None, ALU.mult))
            dve.wait_ge(S("dsa_pe"), PE_STEP["qi8_T"])
            dve.tensor_copy(qi8[0:DEC, :], PS[0:DEC, 0, :]).then_inc(S("dsa_dve"), 1)
            dve.wait_ge(S("dsa_pe"), PE_STEP["qi_half"])
            for r in range(2):
                q = slice(64 * r, 64 * r + 64)
                dve.tensor_copy(Qb[q, :].rearrange("p (u x) -> p u x", x=80)[:, :, 8 * r:8 * r + 8],
                                PS[q, 1, 0:64].rearrange("p (h u r) -> p u h r", r=2, u=4)[:, :, :, r])
            dv(dve.tensor_copy(wS[0:64, :], PS[0:64, 2, 0:1]))
            dve.sem_inc(S("dsa_dve"), 1)
            dve.wait_ge(S("irelu0"), 1)
            dve.tensor_scalar(Wx[0:64, 0:2049], Wx[0:64, 0:2049], wS[0:64, :], None, ALU.mult).then_inc(S("dsa_dve"), 1)
            dve.wait_ge(S("dsa_pe"), PE_STEP["iscore"])
            dve.tensor_copy(Sx[0:DEC, 2048:2049], PS[0:DEC, 6, 8:9])
            dve.tensor_copy(Sx[0:DEC, 0:2048], PS[0:DEC, 0:4, :].rearrange("p b n -> p (b n)")).then_inc(S("dsa_dve"), 1)
            dve.wait_ge(S("dsa_dve"), DVE_STEP["iscore_sb"])
            dv(dve.max(m8[0:DEC, 0, :], Sx[0:DEC, 0:2049]))
            dve.match_replace(Wx[0:DEC, 0:2049], m8[0:DEC, 0, :], Sx[0:DEC, 0:2049], GONE).then_inc(S("top_w"), 1)
            with dve.Fori(0, 31) as i:
                wait_alone(dve, S("top_w"), i + 1)
                dve.max(m8[0:DEC, 0, :], Wx[0:DEC, 0:2049]).then_inc(S("top_m"), 1)
                wait_alone(dve, S("top_m"), i + 1)
                dve.match_replace(Wx[0:DEC, 0:2049], m8[0:DEC, 0, :], Wx[0:DEC, 0:2049], GONE).then_inc(S("top_w"), 1)
            dve.wait_ge(S("top_w"), 32)
            dve.tensor_scalar(Wx[0:DEC, 0:2049], Wx[0:DEC, 0:2049], GONE, NEG, ALU.not_equal, ALU.mult).then_inc(S("dsa_dve"), 1)
            dve.wait_ge(S("dsa_pe"), PE_STEP["slogit"])
            dve.tensor_reduce(mxn[:, 0:1], PS[:, 0:4, :].rearrange("p b n -> p (b n)"), AX, ALU.max)
            dv(dve.tensor_copy(mxn[:, 1:2], PS[:, 4, 0:1]))
            dv(dve.tensor_tensor(mxn[:, 2:3], mxn[:, 0:1], mxn[:, 1:2], ALU.max))
            dve.tensor_scalar(mxn[:, 3:4], mxn[:, 2:3], -(DH ** -0.5), None, ALU.mult).then_inc(S("dsa_dve"), 1)
            dve.wait_ge(S("sexp"), 1)
            dv(dve.tensor_tensor(mxn[:, 0:1], mxn[:, 0:1], mxn[:, 1:2], ALU.add))
            dv(dve.reciprocal(mxn[:, 0:1], mxn[:, 0:1]))
            dv(dve.tensor_scalar(Sx[:, 0:2049], Sx[:, 0:2049], mxn[:, 0:1], None, ALU.mult))
            dve.tensor_scalar(KTs[0][:, 0, 0:DEC], K["expt"], Sx[:, 2048:2049], None, ALU.mult).then_inc(S("dsa_dve"), 1)
            dve.wait_ge(S("dsa_pe"), PE_STEP["pn"])
            dve.tensor_copy(Pn[0:DEC, :], PS[0:DEC, 0, 0:P]).then_inc(S("dsa_dve"), 1)
            dve.wait_ge(S("dsa_pe"), PE_STEP["so_done"])
            for h in range(AH):
                Pq, r, g = h // 8, (h % 8) // 4, h % 4
                ins_ = dve.tensor_copy(oT[64 * (g % 2):64 * (g % 2) + 64, h // 2, SEQ:TOK],
                                       PS[64 * r:64 * r + 64, 1, Pq * P:(Pq + 1) * P].rearrange("p (b h) -> p h b", h=AH)[:, h, :])
            ins_.then_inc(S("mix_in"), 1)

        def act_dsa():
            dsts = [qT[:, 1], qT[:, 3], kT[:, 1], qT[:, 5], qT[:, 7], vTt[:, 1], qiT[:, 1], qiT[:, 3]]
            for n, dst in enumerate(dsts):
                act.wait_ge(S("dproj"), 2 * n + 2)
                act.copy(dst, PS[:, (2 * n + 1) % 4, 0:TOK]).then_inc(S("dproj_act"), 1)
            act.wait_ge(S("dsa_pe"), PE_STEP["ki_var"])
            act.activation(lrs, PS[:, 6, 0:TOK], ACT.Sqrt, bias=K["eps"]).then_inc(S("ki_rms"), 1)
            for h in range(IH):
                act.wait_ge(S("isc"), h + 1)
                if h >= 2:
                    act.wait_ge(S("isum"), h - 1)
                act.activation(rl[h % 2], PS[:, h % 4, 0:384], ACT.Relu, scale=IDH ** -0.5).then_inc(S("relu"), 1)
            act.wait_ge(S("dsa_dve"), DVE_STEP["kv_tok"])
            tokv = lambda t: t[0, 0].rearrange("(t p) h d -> p t (h d)", p=P)
            for dst, src in ((tokv(outs["k_p"]), ktk), (tokv(outs["v_p"]), vtk), (outs["ki_p"][0, 0].rearrange("(t p) d -> p t d", p=P), kitk),
                             (outs["k_s"][0, :, 0].rearrange("b h d -> b (h d)"), k8[0:DEC, :]), (outs["v_s"][0, :, 0].rearrange("b h d -> b (h d)"), v8[0:DEC, :]),
                             (outs["ki_s"][0, :, 0], ki8[0:DEC, :])):
                act.dma_start(dst, src).then_inc(S("kv_out"), 16)
            for it in range(8):
                T = it // 4
                n = P * (T + 1)
                act.wait_ge(S("nmax"), it + 1)
                for g in range(4):
                    ins_ = act.activation(A2[it % 2][:, g, 0:n], A2[it % 2][:, g, 0:n], ACT.Exp, bias=nm[:, g:g + 1], accum_out=rs[:, g:g + 1])
                ins_.then_inc(S("pexp"), 1)
                act.wait_ge(S("p_T"), it + 1)
                if it >= 2:
                    act.wait_ge(S("pv"), it - 1)
                act.copy(PTs[it % 2][:, 0:T + 1].rearrange("p s g t -> p s (g t)"), PS[:, 4 + 2 * (it % 2):5 + 2 * (it % 2) + T, :]).then_inc(S("p_T_sb"), 1)
                if it % 4 == 3:
                    act.wait_ge(S("pv"), it + 1)
                    act.copy(oT[:, :, T * P:(T + 1) * P], PS[:, 2:4, :].rearrange("p b (f t) -> p (b f) t", t=P)).then_inc(S("att_o_sb"), 1)
            with act.Fori(0, 4) as jj:
                for u in range(4):
                    act.wait_ge(S("ik_free"), jj * 4 + (u + 3))
                    act.copy(KTs[u % 2].rearrange("p a b -> p (a b)")[:, 0:512], bank(4 + u % 2)).then_inc(S("ik_sb"), 1)
            act.wait_ge(S("dsa_pe"), PE_STEP["ik_new"])
            act.activation(Wx[0:64, 0:2048], PS[0:64, 0:4, :].rearrange("p b n -> p (b n)"), ACT.Relu, scale=IDH ** -0.5)
            act.activation(Wx[0:64, 2048:2049], PS[0:64, 6, 0:1], ACT.Relu, scale=IDH ** -0.5).then_inc(S("irelu0"), 1)
            with act.Fori(0, 4) as jj:
                for b in range(DEC):
                    act.wait_ge(S("kp_free"), jj * 8 + (b + 3))
                    act.copy(KTs[b % 2], PS[:, 4 + 2 * (b % 2):6 + 2 * (b % 2), :]).then_inc(S("kp_sb"), 1)
            act.wait_ge(S("dsa_dve"), DVE_STEP["snmax"])
            act.activation(Sx[:, 0:2048], PS[:, 0:4, :].rearrange("p b n -> p (b n)"), ACT.Exp, bias=mxn[:, 3:4], scale=DH ** -0.5, accum_out=mxn[:, 0:1])
            act.activation(Sx[:, 2048:2049], PS[:, 4, 0:1], ACT.Exp, bias=mxn[:, 3:4], scale=DH ** -0.5, accum_out=mxn[:, 1:2]).then_inc(S("sexp"), 1)
            for q in range(4):
                act.wait_ge(S("sp_T"), q + 1)
                act.copy(PT[:, 4 * q:4 * q + 4, :], PS[:, 4 + q, :].rearrange("p (j c) -> p j c", c=P)).then_inc(S("sp_sb"), 1)
            act.wait_ge(S("kv_out"), 96)

        fin = arena[:, 2112:2112 + KT * TOK].rearrange("p (k t) -> p k t", k=KT)
        orow = [arena[:, 4400 + D * i:4400 + D * (i + 1)] for i in range(3)]

        def dve_final():
            dve.wait_ge(S("x_rms"), 5)
            dv(dve.reciprocal(rstd[:], rstd[:]))
            for k in range(KT):
                ins_ = dve.scalar_tensor_tensor(out=fin[:, k, :], in0=xT[:, k, :], scalar=vT[:, 32 + k:33 + k], in1=rstd[:], op0=ALU.mult, op1=ALU.mult)
            ins_.then_inc(S("fin"), 1)
            for T in range(TT):
                n = P if T < 2 else DEC
                dve.wait_ge(S("fin_T"), T + 1)
                dve.tensor_copy(orow[T][0:n, :], PS[0:n, 2 + 2 * T:4 + 2 * T, :].rearrange("p b n -> p (b n)")).then_inc(S("fin_row"), 1)

        def pe_final():
            pe.wait_ge(S("fin"), 1)
            for T in range(TT):
                n = P if T < 2 else DEC
                for k in range(KT):
                    m = pe.transpose(PS[0:n, 2 + 2 * T + k // 4, (k % 4) * P:(k % 4 + 1) * P], fin[:, k, T * P:T * P + n], K["ident"])
                m.then_inc(S("fin_T"), 1)

        def sp_final():
            for T in range(TT):
                n = P if T < 2 else DEC
                sp.wait_ge(S("fin_row"), T + 1)
                dst = outs["y_p"][0, T * P:(T + 1) * P, :] if T < 2 else outs["y_s"][:, 0, :]
                sp.dma_start(dst, orow[T][0:n, :]).then_inc(S("y_out"), 16)
            sp.wait_ge(S("y_out"), 48)
            sp.wait_ge(S("kv_out"), 96)

        @block.sync
        def _(sp_):
            sp_setup()
            sp_gla_small()
            sp_bias()
            sp_ada(0)
            sp_gla()
            sp_ada(1)
            sp_moe(0)
            sp_router(0)
            sp_experts_first(0)
            sp_experts(0)
            sp_dsa()
            sp_dout(0)
            sp_pages()
            sp_router(1)
            sp_experts_first(1)
            sp_experts(1)
            sp_final()

        @block.tensor
        def _(pe_):
            pe_setup()
            pe_bias()
            pe_ada(0)
            pe_norm(0, norm_sq, 0)
            pe_gla()
            pe_ada(1)
            pe_norm(1, norm_sq, 0)
            pe_route(0)
            pe_experts(0)
            pe_combine(0)
            pe_norm(2, norm_sq, 0)
            pe_dsa()
            pe_norm(3, norm_sq, 0)
            pe_route(1)
            pe_experts(1)
            pe_combine(1)
            pe_norm(4, norm_sq, 0)
            pe_final()

        @block.vector
        def _(dve_):
            dve_setup()
            dve.sem_inc(S("x_out_of_psum"), 1)
            dve.sem_inc(S("x_new"), 1)
            dve_bias()
            dve_ada(0)
            dve_norm(0, 0, 0, 0)
            dve_gla()
            dve_out_proj(0)
            dve_ada(1)
            dve_norm(1, 0, 1, 0)
            dve_route(0)
            dve_experts(0)
            dve_combine(0)
            dve_norm(2, 1, 0, 0)
            dve.sem_inc(S("bias_free"), 1)
            dve_dsa()
            dve_out_proj(1)
            dve_norm(3, 1, 1, 0)
            dve_route(1)
            dve_experts(1)
            dve_combine(1)
            dve_final()

        @block.scalar
        def _(act_):
            act_setup()
            act_ada(0)
            act_norm(0, norm_sq, 0)
            act_gla()
            act_ada(1)
            act_norm(1, norm_sq, 0)
            act_route(0)
            act_experts(0)
            act_combine(0)
            act_norm(2, norm_sq, 0)
            act_dsa()
            act_norm(3, norm_sq, 0)
            act_route(1)
            act_experts(1)
            act_combine(1)
            act_norm(4, norm_sq, 0)

        @block.gpsimd
        def _(pool_):
            pool_bias()
            pool_gla()
            pool.wait_ge(S("out_pool"), 16)
            pool_experts(0)
            pool_experts(1)


_INS = ["x_prompt", "x_sample", "c_prompt", "c_sample", "state_gla", "cache_k", "cache_v", "cache_idx_k", "page_table",
        "rel_bias", "w_ada", "b_ada", "norm_mix", "norm_ffn", "norm_final", "gla_w_in", "gla_w_g2", "gla_b_g2",
        "gla_gnorm", "gla_w_out", "dsa_w_in", "dsa_idx_ln_g", "dsa_idx_ln_b", "dsa_w_out", "moe_w_router",
        "moe_router_bias", "moe_w_gate", "moe_w_up", "moe_w_down", "shared_w_gate", "shared_w_up", "shared_w_down"]
_OUTS = [("y_p", (1, SEQ, D)), ("y_s", (DEC, 1, D)), ("gla_p", (1, 1, GH, GDK, GDV)), ("gla_s", (1, DEC, GH, GDK, GDV)),
         ("k_p", (1, 1, SEQ, KVH, DH)), ("v_p", (1, 1, SEQ, KVH, DH)), ("ki_p", (1, 1, SEQ, IDH)),
         ("k_s", (1, DEC, 1, KVH, DH)), ("v_s", (1, DEC, 1, KVH, DH)), ("ki_s", (1, DEC, 1, IDH))]


def kernel(**inputs):
    import numpy as _np
    import concourse.bacc as _bacc
    from concourse import mybir as _mybir
    from concourse.bass_utils import run_bass_kernel_spmd as _run

    nc = _bacc.Bacc("TRN2", target_bir_lowering=False, num_devices=1)
    arrays, ins, outs = {}, {}, {}
    for name in _INS:
        a = _np.ascontiguousarray(inputs[name])
        arrays[f"in_{name}"] = a
        ins[name] = nc.dram_tensor(f"in_{name}", a.shape, _mybir.dt.from_np(a.dtype), kind="ExternalInput").ap()
    arrays["in_consts"] = constants()
    ins["consts"] = nc.dram_tensor("in_consts", (P, NCONST), F32, kind="ExternalInput").ap()
    arrays["in_onehot"] = distance_onehot()
    ins["onehot"] = nc.dram_tensor("in_onehot", (32, 384), F32, kind="ExternalInput").ap()
    for name, shape in _OUTS:
        outs[name] = nc.dram_tensor(f"out_{name}", shape, F32, kind="ExternalOutput").ap()
    build(nc, ins, outs)
    r = _run(nc, [arrays], core_ids=[0])
    return tuple(r.results[0][f"out_{name}"] for name, _ in _OUTS)
```

```python
from contextlib import ExitStack
import math

import numpy as np
import concourse.bass as bass
from concourse import mybir
from concourse.bass import IndirectOffsetOnAxis, ds

F32 = mybir.dt.float32
BF16 = mybir.dt.bfloat16
I32 = mybir.dt.int32
U32 = mybir.dt.uint32
ALU = mybir.AluOpType
ACT = mybir.ActivationFunctionType
AX = mybir.AxisListType.X

P = 128
D = 1024
KT = D // P
SEQ, DEC = 256, 8
TOK = SEQ + DEC
TP = 3 * P
TT = 3
GH, GDK, GDV, CH = 4, 128, 256, 64
NE, TOPK, NG, TOPG, FF = 64, 8, 8, 4, 256
CAP = 64
NOV = 34
NB = NE + NOV
OOB = 16384
EPS = 1e-6
AH, KVH, DH, IH, IDH = 16, 4, 64, 8, 64
PAGE, NPG = 128, 16
PAST = PAGE * NPG
ROW = 4
WS = 4
THIRD = 2048
NEG = -1e30
GONE = -2e38
ROUTE_SCALE = 2.5

CONST = {}
_n = 0
for _name, _w in (("ident", 128), ("tri", 128), ("gmask", 64), ("slot", 128), ("fold", 9), ("gtri", 64),
                  ("valid", 3), ("pcol", 1), ("jcol", 1), ("iota", NOV), ("scanm", 256), 
                  ("ohs", 129), ("expand", 128), ("hsum", 8), ("cau", 128), ("row", 1), ("kvsel", 4), ("ones", 1), ("ones1024", 128),
                  ("ones256", 128), ("blk64", 128), ("expt", 8), ("eps", 1)):
    CONST[_name] = (_n, _w)
    _n += _w
NCONST = _n


def bucket(dist):
    dist = max(dist, 0)
    if dist < 16:
        return dist
    return min(16 + int(math.log(dist / 16) / math.log(8) * 16 + 1e-9), 31)


def distance_onehot():
    c = np.zeros((32, 384), np.float32)
    for y in range(384):
        c[bucket(255 - y), y] = 1
    return c


def constants():
    c = {k: np.zeros((P, w), np.float32) for k, (_, w) in CONST.items()}
    p, f = np.arange(P)[:, None], np.arange(P)[None, :]
    c["ident"][:] = p == f
    c["tri"][:] = p < f
    c["gmask"][:] = (p % CH) <= np.arange(CH)[None, :]
    c["slot"][:] = f % CAP + 1
    c["fold"][:] = (p % 32) == np.arange(9)[None, :]
    g = np.arange(64)
    c["gtri"][:] = ((g % 8) < (g // 8))[None, :]
    c["valid"][:] = (np.arange(3)[None, :] * P + p) < TOK
    c["pcol"][:] = p
    c["jcol"][:] = (p >= CAP) + OOB
    c["iota"][:] = np.arange(NOV)[None, :]
    c["scanm"][:] = (np.arange(256) % CH != 0)[None, :]

    for y in range(129):
        c["ohs"][bucket(128 - y), y] = 1
    c["expand"][:8] = np.arange(128)[None, :] // 16 == np.arange(8)[:, None]
    c["expand"][32:40] = c["expand"][:8]
    c["hsum"][:64] = np.arange(64)[:, None] // 8 == np.arange(8)[None, :]
    c["kvsel"][:] = p % 32 // 4 == np.arange(4)[None, :]
    c["row"][:] = p % (PAGE // ROW)
    c["cau"][:] = np.where(f <= p, 0.0, NEG)
    c["ones"][:] = 1
    c["eps"][:] = EPS
    c["ones1024"][:] = 1 / 1024
    c["ones256"][:] = 1 / 256
    c["blk64"][:] = (p // 64 == f // 64) / 64
    c["expt"][:] = p // 16 == np.arange(8)[None, :]
    return np.concatenate([c[k] for k in CONST], axis=1)


VROW = {"mix": 0, "ffn": 16, "final": 32, "gnorm": 40, "bg2": 42, "lng": 46, "lnb": 47}


def build(nc, ins, outs):
    ctx = ExitStack()
    with ctx:
        def sb(name, shape, dt=F32):
            return ctx.enter_context(nc.sbuf_tensor(name, shape, dt))

        sems = {}

        def S(name):
            if name not in sems:
                sems[name] = ctx.enter_context(nc.semaphore(name))
            return sems[name]

        class Chain:

            def __init__(self, eng, name):
                self.eng, self.sem, self.n, self.base = eng, S(name), 0, None

            def __call__(self, ins):
                ins.then_inc(self.sem, 1)
                self.n += 1
                self.eng.wait_ge(self.sem, self.n if self.base is None else self.base + self.n)

            def enter(self, base):
                self.kept, self.base, self.n = self.n, base, 0

            def leave(self, total, per):
                assert self.n == per, (self.n, per)
                self.base, self.n = None, self.kept + total

        def wait_alone(eng, name, value):
            eng.wait_ge(name, value)
            eng.sem_inc(S("passed"), 1)

        PS = ctx.enter_context(nc.psum_tensor("PS", [P, 8, 512], F32))
        cst = sb("cst", [P, NCONST])
        K = {k: cst[:, o:o + w] for k, (o, w) in CONST.items()}
        ring = sb("ring", [P, WS, 3, THIRD])
        xT = sb("xT", [P, KT, TOK])
        hT = sb("hT", [P, KT, TP])
        modT2 = sb("modT", [P, 2, 48, 9])
        modA = sb("modA", [P, KT, 9])
        cT = sb("cT", [P, KT, 32])
        vT = sb("vT", [P, 48])
        bT = sb("bT", [P, 96])
        rstd = sb("rstd", [P, TOK])
        mrow = sb("mrow", [P, 3 * 256])
        shT = sb("shT", [P, KT, TOK])
        triB = sb("triB", [P, P], BF16)
        onesB = sb("onesB", [P, P], BF16)
        slotB = sb("slotB", [P, P], BF16)
        AW = 17088
        arena = sb("arena", [P, AW])

        def carver(width=AW):
            at = [0]

            def take(*shape, dt=F32):
                n = int(np.prod(shape))
                words = n if dt != BF16 else (n + 1) // 2
                ap = arena[:, at[0]:at[0] + words]
                at[0] += words
                assert at[0] <= width, at
                if dt != F32:
                    ap = ap.bitcast(dt)
                names = "abcde"[:len(shape)]
                if len(shape) > 1:
                    ap = ap.rearrange(f"p ({' '.join(names)}) -> p {' '.join(names)}",
                                      **{q: s for q, s in zip(names[1:], shape[1:])})
                return ap
            take.at = at
            return take

        block = ctx.enter_context(nc.Block())
        pe, dve, act, pool, sp = nc.tensor, nc.vector, nc.scalar, nc.gpsimd, nc.sync
        dv = Chain(dve, "dve_chain")
        ac = Chain(act, "act_chain")

        def bank(i, n=512):
            return PS[:, i, 0:n]

        def bc(ap, axis, n):
            ap = ap.unsqueeze(axis)
            shape = list(ap.shape)
            shape[axis] = n
            return ap.broadcast_to(shape)

        class Ring:
            def __init__(self):
                self.next, self.loads, self.uses = 0, [0] * WS, [0] * WS

            def slot(self):
                s = self.next % WS
                self.next += 1
                return s
        W = Ring()

        prior = {}

        def plan(n, signals=True):
            got = []
            for _ in range(n):
                s = W.slot()
                W.loads[s] += 1
                prior[(s, W.loads[s])] = W.uses[s]
                W.uses[s] += signals
                got.append((s, W.loads[s]))
            return got

        def load_item(item, thirds):
            s, n = item
            if prior[item]:
                sp.wait_ge(S(f"slot_used{s}"), prior[item])
            for t, src in enumerate(thirds):
                dst = ring[:, s, t, :]
                if len(src.shape) == 3:
                    dst = dst.rearrange("p (k n) -> p k n", n=src.shape[2])
                sp.dma_start(dst, src).then_inc(S(f"slot_loaded{s}"), 16)

        def item_ready(eng, item):
            s, n = item
            eng.wait_ge(S(f"slot_loaded{s}"), 48 * n)

        def cols(w, c0, n=256):
            return w[:, c0:c0 + n].rearrange("(k p) n -> p k n", p=P)

        def load_512(item, w, c0):
            s, n = item
            if prior[item]:
                sp.wait_ge(S(f"slot_used{s}"), prior[item])
            sp.dma_start(third(s, 0), cols(w, c0)).then_inc(S(f"slot_loaded{s}"), 16)
            for h in range(2):
                sp.dma_start(third(s, 1)[:, 4 * h:4 * h + 4, :], cols(w, c0 + 256)[:, 4 * h:4 * h + 4, :]).then_inc(S(f"slot_loaded{s}"), 16)

        def third(s, t):
            return ring[:, s, t, :].rearrange("p (k n) -> p k n", k=KT)

        it_ada = [plan(8), None]
        it_gla = plan(4)
        it_gout = plan(2)
        it_sh = [plan(1)[0], None]
        it_ada[1] = plan(8)
        it_ex = [plan(NE, False), None]
        it_dsa = plan(3)
        it_dout = plan(2)
        it_sh[1] = plan(1)[0]
        it_ex[1] = plan(NE, False)

        hk, hv = GH * GDK, GH * GDV
        w_in = ins["gla_w_in"][0]
        w_dsa = ins["dsa_w_in"][0]

        tk = carver()
        xrow = tk(TT, D)
        crow = tk(D)
        crow2 = tk(D)
        vrow = tk(P)
        brow = tk(P)

        def sp_setup():
            sp.dma_start(cst[:], ins["consts"]).then_inc(S("setup_in"), 16)
            sp.dma_start(crow[0:1, :], ins["c_prompt"]).then_inc(S("setup_in"), 16)
            sp.dma_start(crow[1:9, :], ins["c_sample"]).then_inc(S("setup_in"), 16)
            for name, key, n in (("norm_mix", "mix", 16), ("norm_ffn", "ffn", 16)):
                r = VROW[key]
                sp.dma_start(vrow[r:r + n, :], ins[name].rearrange("l (k p) -> (l k) p", p=P)).then_inc(S("setup_in"), 16)
            sp.dma_start(vrow[32:40, :], ins["norm_final"].rearrange("(k p) -> k p", p=P)).then_inc(S("setup_in"), 16)
            sp.dma_start(vrow[40:42, :], ins["gla_gnorm"].rearrange("l (k p) -> (l k) p", p=P)).then_inc(S("setup_in"), 16)
            sp.dma_start(vrow[42:46, :], ins["gla_b_g2"].rearrange("l (k p) -> (l k) p", p=P)).then_inc(S("setup_in"), 16)
            for r, name in ((46, "dsa_idx_ln_g"), (47, "dsa_idx_ln_b")):
                for half in range(2):
                    sp.dma_start(vrow[r:r + 1, 64 * half:64 * half + 64], ins[name]).then_inc(S("setup_in"), 16)
            sp.dma_start(brow[0:96, :], ins["b_ada"].rearrange("l (k p) -> (l k) p", p=P)).then_inc(S("setup_in"), 16)
            for t in range(2):
                sp.dma_start(xrow[:, t, :], ins["x_prompt"][0, t * P:(t + 1) * P, :]).then_inc(S("x_in"), 16)
            sp.dma_start(xrow[0:DEC, 2, :], ins["x_sample"][:, 0, :]).then_inc(S("x_in"), 16)
        N_SETUP = 16 * 13

        def pe_setup():
            pe.wait_ge(S("setup_in"), N_SETUP)
            pe.wait_ge(S("c_silu"), 1)
            for k in range(KT):
                m = pe.transpose(PS[:, 0, 16 * k:16 * k + 9], crow2[0:9, k * P:(k + 1) * P], K["ident"][0:9, 0:9])
            m = pe.transpose(PS[:, 1, 0:48], vrow[0:48, :], K["ident"][0:48, 0:48])
            m = pe.transpose(PS[:, 1, 64:160], brow[0:96, :], K["ident"][0:96, 0:96])
            m.then_inc(S("setup_turned"), 1)
            pe.wait_ge(S("x_in"), 48)
            for t in range(TT):
                n = P if t < 2 else DEC
                for half in range(2):
                    for k in range(4):
                        m = pe.transpose(PS[:, 2 + 2 * t + half, k * P:k * P + n],
                                         xrow[0:n, t, (4 * half + k) * P:(4 * half + k + 1) * P], K["ident"][0:n, 0:n])
                    m.then_inc(S("setup_turned"), 1)

        def act_setup():
            act.wait_ge(S("setup_in"), N_SETUP)
            act.activation(crow2[0:9, :], crow[0:9, :], ACT.Silu).then_inc(S("c_silu"), 1)

        def dve_setup():
            dv(dve.memset(cT[:], 0.0))
            dv(dve.memset(hT[:], 0.0))
            dve.wait_ge(S("setup_in"), N_SETUP)
            dve.tensor_copy(triB[:], K["tri"])
            dve.memset(onesB[:], 1.0)
            dve.tensor_copy(slotB[:], K["slot"])
            dve.wait_ge(S("setup_turned"), 1)
            dve.tensor_copy(cT[:, :, 0:9], PS[:, 0, 0:128].rearrange("p (k c) -> p k c", c=16)[:, :, 0:9]).then_inc(S("setup_taken"), 1)
            dv(dve.tensor_copy(vT[:], PS[:, 1, 0:48]))
            dv(dve.tensor_copy(bT[:], PS[:, 1, 64:160]))
            for t in range(TT):
                n = P if t < 2 else DEC
                for half in range(2):
                    dve.wait_ge(S("setup_turned"), 2 * t + half + 2)
                    ins_ = dve.tensor_copy(xT[:, 4 * half:4 * half + 4, t * P:t * P + n],
                                           PS[:, 2 + 2 * t + half, :].rearrange("p (k c) -> p k c", c=P)[:, :, 0:n])
            dv(ins_)

        def sp_ada(l):
            for i, item in enumerate(it_ada[l]):
                load_item(item, [cols(ins["w_ada"][l], 768 * i + 256 * t) for t in range(3)])

        def pe_ada(l, items=range(8)):
            if l == 0:
                pe.wait_ge(S("setup_taken"), 1)
                pe.wait_ge(S("setup_taken"), 2)
            for i in items:
                item = it_ada[l][i]
                s, _ = item
                n = 8 * l + i
                item_ready(pe, item)
                if n >= 1:
                    pe.wait_ge(S("mod_rows"), n)
                for t in range(3):
                    for kk in range(2):
                        for g in range(4):
                            m = pe.matmul(PS[32 * g:32 * g + 32, t // 2, 256 * (t % 2):256 * (t % 2) + 256],
                                          cT[:, 2 * g + kk, :], third(s, t)[:, 2 * g + kk, :],
                                          start=(kk == 0), stop=(kk == 1), skip_group_check=True)
                m.then_inc(S(f"slot_used{s}"), 1)
                m = pe.wait_ge(S("mod_rows"), n + 1)
                if n >= 1:
                    pe.wait_ge(S("mod_T"), n)
                for j in range(6):
                    m = pe.matmul(PS[:, 2, 16 * j:16 * j + 9], mrow[:, j * P:(j + 1) * P], K["fold"],
                                  start=True, stop=True)
                m.then_inc(S("mod_fold"), 1)

        def act_ada(l, items=range(8)):
            if l and 0 in items:
                act.wait_ge(S("route_dve"), RD[0]["mask"] + 1)
            for i in items:
                item = it_ada[l][i]
                n = 8 * l + i
                act.wait_ge(S(f"slot_used{item[0]}"), prior[item] + 1)
                if n >= 1:
                    act.wait_ge(S("mod_fold"), n)
                ac(act.copy(mrow[:, 0:512], bank(0)))
                act.copy(mrow[:, 512:768], PS[:, 1, 0:256]).then_inc(S("mod_rows"), 1)

        def dve_ada(l, items=range(8)):
            for i in items:
                dve.wait_ge(S("mod_fold"), 8 * l + i + 1)
                dve.tensor_tensor(modT2[:, l, 6 * i:6 * i + 6, :],
                                  PS[:, 2, 0:96].rearrange("p (k c) -> p k c", c=16)[:, :, 0:9],
                                  bc(bT[:, 48 * l + 6 * i:48 * l + 6 * i + 6], 2, 9), ALU.add).then_inc(S("mod_T"), 1)
            if 7 in items:
                dve.wait_ge(S("mod_T"), 8 * (l + 1))

        norm_sq = arena[:, 0:KT * TOK].rearrange("p (k t) -> p k t", k=KT)

        XSQ = [0, 1, 9, 10, 18]

        def act_norm(n, sqbuf, b):
            if n in (1, 3):
                for k in range(KT):
                    act.wait_ge(S("mix_added"), 8 * (n // 2) + k + 1)
                    act.activation(sqbuf[:, k, :], xT[:, k, :], ACT.Square).then_inc(S("x_sq"), 1)
            else:
                act.wait_ge(S("x_new"), n + 1)
                act.activation(sqbuf[:], xT[:], ACT.Square).then_inc(S("x_sq"), 1)
            act.wait_ge(S("x_ms"), n + 1)
            act.activation(rstd[:], PS[:, b, 0:TOK], ACT.Sqrt, bias=K["eps"]).then_inc(S("x_rms"), 1)

        def pe_norm(n, sqbuf, b):
            pe.wait_ge(S("x_sq"), XSQ[n] + 1)
            for k in range(KT):
                m = pe.matmul(PS[:, b, 0:TOK], K["ones1024"], sqbuf[:, k, :], start=(k == 0), stop=(k == KT - 1))
            m.then_inc(S("x_ms"), 1)

        def pe_norm_tile(n, k):
            pe.wait_ge(S("x_sq"), XSQ[n] + k + 1)
            m = pe.matmul(PS[:, 0, 0:TOK], K["ones1024"], norm_sq[:, k, :], start=(k == 0), stop=(k == KT - 1), skip_group_check=True)
            if k == KT - 1:
                m.then_inc(S("x_ms"), 1)

        def dve_norm(n, l, part, b):
            modT = modT2[:, l]
            shift, scale = modT[:, 24 * part:24 * part + 8, :], modT[:, 24 * part + 8:24 * part + 16, :]
            v0 = (VROW["ffn"] if part else VROW["mix"]) + 8 * l
            dv(dve.tensor_scalar(modA[:], scale, 1.0, None, ALU.add))
            dv(dve.tensor_tensor(modA[:], modA[:], bc(vT[:, v0:v0 + 8], 2, 9), ALU.mult))
            dve.wait_ge(S("x_rms"), n + 1)
            dv(dve.reciprocal(rstd[:], rstd[:]))
            dv(dve.tensor_tensor(hT[:, :, 0:TOK], xT[:], bc(rstd[:], 1, KT), ALU.mult))
            for k in range(KT):
                dve.tensor_scalar(hT[:, k, 0:SEQ], hT[:, k, 0:SEQ], modA[:, k, 0:1], shift[:, k, 0:1], ALU.mult, ALU.add)
            dv(dve.tensor_tensor(hT[:, :, SEQ:TOK], hT[:, :, SEQ:TOK], modA[:, :, 1:9], ALU.mult))
            dve.tensor_tensor(hT[:, :, SEQ:TOK], hT[:, :, SEQ:TOK], shift[:, :, 1:9], ALU.add).then_inc(S("h_ready"), 1)

        def add_gated(k, src, modT, g0, tmp):
            dve.scalar_tensor_tensor(out=xT[:, k, 0:SEQ], in0=src[:, 0:SEQ], scalar=modT[:, g0 + k, 0:1],
                                     in1=xT[:, k, 0:SEQ], op0=ALU.mult, op1=ALU.add)
            dv(dve.tensor_tensor(tmp, src[:, SEQ:TOK], modT[:, g0 + k, 1:9], ALU.mult))
            dv(dve.tensor_tensor(xT[:, k, SEQ:TOK], xT[:, k, SEQ:TOK], tmp, ALU.add))

        tk = carver()
        pT = tk(24, TOK)
        qe, ke, qb, kd = (tk(GH, SEQ) for _ in range(4))
        cL = tk(GH, SEQ)
        dL = tk(GH, SEQ)
        vtok = tk(2, hv)
        kdt = tk(2, hk)
        attS = tk(2, GH, CH)
        Sst = tk(GH, GDV)
        eg = sb("eg", [P, GH, DEC])[:]
        oT = shT
        wg1 = Sst.rearrange("p h v -> p (h v)")[:, TOK:TOK + P].rearrange("p (k n) -> p k n", k=KT)
        wg2 = dL.rearrange("p h t -> p (h t)")[:, 0:hk]
        g1T = Sst.rearrange("p h v -> p (h v)")[:, 0:TOK]
        kdt0 = 6336 + 4 * 1024 + 2 * 1024 + 2048
        Lg = arena[:, kdt0:kdt0 + GH * TOK].rearrange("p (h t) -> p h t", h=GH)
        kmask = arena[:, 6336:6336 + DEC * hk].rearrange("p (b n) -> p b n", b=DEC)
        osq = arena[:, 6336:6336 + KT * TOK].rearrange("p (k t) -> p k t", k=KT)
        ktok8 = cL.rearrange("p h t -> p (h t)")[:, 0:hk]
        vtok8 = dL.rearrange("p h t -> p (h t)")
        NS = 5
        sbuf = [arena[:, o:o + 1024].rearrange("p (h v) -> p h v", h=GH) for o in (8 * TOK, 8 * TOK + 1024, 4 * TOK)]
        sbuf += [hT.rearrange("p k t -> p (k t)")[:, o:o + 1024].rearrange("p (h v) -> p h v", h=GH) for o in (0, 1024)]

        GP = {'g1': 0, 'z': 1, 'v_T': 2, 'kd_T': 4, 'att': 6, 'kv8_T': 8, 'o_ms': 9}
        GD = {'g1_out': 0, 'dL': 1, 'dE': 2, 'kd': 3, 'v_tok': 4, 'kd_tok': 6, 'att_out': 8, 'kmask': 10, 'o_all': 11}

        def sp_gla_small():
            sp.dma_start(wg1, w_in[:, 2 * hk + 2 * hv:].rearrange("(k p) n -> p k n", p=P)).then_inc(S("small_in"), 16)
            sp.dma_start(wg2[0:16, :], ins["gla_w_g2"][0]).then_inc(S("small_in"), 16)

        def sp_gla():
            for i, item in enumerate(it_gla):
                load_item(item, [cols(w_in, 768 * i + 256 * t) for t in range(3)])
            for i, item in enumerate(it_gout):
                load_512(item, ins["gla_w_out"][0], 512 * i)

        def pe_gla():
            pe.wait_ge(S("h_ready"), 1)
            pe.wait_ge(S("small_in"), 64)
            for k in range(KT):
                m = pe.matmul(PS[0:16, 0, 0:TOK], wg1[:, k, :], hT[:, k, 0:TOK], start=(k == 0), stop=(k == KT - 1))
            m.then_inc(S("gla_pe"), 1)
            pe.wait_ge(S("gla_dve"), GD["g1_out"] + 1)
            for h in range(GH):
                m = pe.matmul(PS[:, 4 + h, 0:TOK], wg2[0:16, h * P:(h + 1) * P], g1T[0:16, :], start=True, stop=True)
            m.then_inc(S("gla_pe"), 1)
            for m_ in range(24):
                item = it_gla[m_ // 6]
                if m_ % 6 == 0:
                    item_ready(pe, item)
                if 4 <= m_ < 20:
                    pe.wait_ge(S("proj_dve"), m_ - 3)
                elif m_ >= 20:
                    pe.wait_ge(S("proj_act"), m_ - 19)
                w3 = third(item[0], (m_ % 6) // 2)
                for k in range(KT):
                    m = pe.matmul(PS[:, m_ % 4, 0:TOK], w3[:, k, (m_ % 2) * P:(m_ % 2 + 1) * P], hT[:, k, 0:TOK],
                                  start=(k == 0), stop=(k == KT - 1))
                m.then_inc(S("proj"), 1)
                if m_ % 6 == 5:
                    pe.wait_ge(S("proj"), m_ + 1)
                    pe.sem_inc(S(f"slot_used{item[0]}"), 1)
            pe.wait_ge(S("proj_dve"), 16)
            pe.wait_ge(S("proj_act"), 8)
            for T in range(2):
                for j in range(8):
                    m = pe.transpose(PS[:, 2 * T + j // 4, (j % 4) * P:(j % 4 + 1) * P], pT[:, 8 + j, T * P:(T + 1) * P], K["ident"])
                m.then_inc(S("gla_pe"), 1)
            pe.wait_ge(S("gla_dve"), GD["kd"] + 1)
            for T in range(2):
                for h in range(GH):
                    m = pe.transpose(PS[:, 4 + T, h * P:(h + 1) * P], kd[:, h, T * P:(T + 1) * P], K["ident"])
                m.then_inc(S("gla_pe"), 1)
            for T in range(2):
                for h in range(GH):
                    for o in range(2):
                        c = 2 * T + o
                        m = pe.matmul(PS[64 * o:64 * o + 64, 6 + T, h * CH:(h + 1) * CH], ke[:, h, c * CH:(c + 1) * CH],
                                      qe[:, h, c * CH:(c + 1) * CH], start=True, stop=True)
                m.then_inc(S("gla_pe"), 1)
            pe.wait_ge(S("gla_dve"), GD["v_tok"] + 2)
            pe.wait_ge(S("gla_dve"), GD["kd_tok"] + 2)
            pe.wait_ge(S("gla_dve"), GD["att_out"] + 2)
            for c in range(4):
                T, o = c // 2, c % 2
                r = slice(64 * o, 64 * o + 64)
                if c >= 2:
                    pe.wait_ge(S("o_out"), c - 1)
                if c:
                    pe.wait_ge(S("state"), c)
                for h in range(GH):
                    m = pe.matmul(PS[:, 4 + 2 * (c % 2) + h // 2, (h % 2) * GDV:(h % 2 + 1) * GDV], kdt[r, T, h * P:(h + 1) * P],
                                  vtok[r, T, h * GDV:(h + 1) * GDV], start=True, stop=True)
                m.then_inc(S("upd"), 1)
                for h in range(GH):
                    for v in range(2):
                        j = 2 * h + v
                        dst = PS[:, c % 2, j * CH:(j + 1) * CH]
                        m = pe.matmul(dst, vtok[r, T, j * P:(j + 1) * P], attS[r, T, h, :], start=True, stop=(c == 0))
                        if c:
                            m = pe.matmul(dst, Sst[:, h, v * P:(v + 1) * P], qb[:, h, c * CH:(c + 1) * CH], start=False, stop=True)
                m.then_inc(S("o"), 1)
            pe.wait_ge(S("o_out"), 4)
            for h in range(GH):
                m = pe.transpose(PS[0:DEC, 2, h * P:(h + 1) * P], pT[:, 4 + h, SEQ:TOK], K["ident"])
            for j in range(8):
                m = pe.transpose(PS[0:DEC, j // 4, (j % 4) * P:(j % 4 + 1) * P], pT[:, 8 + j, SEQ:TOK], K["ident"])
            m.then_inc(S("gla_pe"), 1)
            pe.wait_ge(S("gla_dve"), GD["kmask"] + 1)
            pe.wait_ge(S("state"), 4)
            for b in range(DEC):
                B0 = 4 + 2 * (b % 2)
                if b >= 2:
                    pe.wait_ge(S("sstate"), b - 1)
                for h in range(GH):
                    m = pe.matmul(PS[:, B0 + h // 2, (h % 2) * GDV:(h % 2 + 1) * GDV], kmask[0:DEC, b, h * P:(h + 1) * P],
                                  vtok8[0:DEC, h * GDV:(h + 1) * GDV], start=True, stop=True)
                m.then_inc(S("outer"), 1)
                if b >= 1:
                    pe_sample_o(b - 1)
            pe_sample_o(DEC - 1)
            pe.wait_ge(S("o_sq"), 1)
            for h in range(GH):
                for v in range(2):
                    m = pe.matmul(PS[:, h, 0:TOK], K["ones256"], osq[:, 2 * h + v, :], start=(v == 0), stop=(v == 1))
            m.then_inc(S("gla_pe"), 1)
            pe.wait_ge(S("mix_in"), 1)
            pe_out_proj(it_gout, oT[:, :, :], 0)

        def pe_sample_o(b):
            pe.wait_ge(S("sstate"), b + 1)
            for h in range(GH):
                for v in range(2):
                    m = pe.matmul(PS[:, 3, (2 * h + v) * DEC + b:(2 * h + v) * DEC + b + 1], sbuf[b % NS][:, h, v * P:(v + 1) * P],
                                  pT[:, h, SEQ + b:SEQ + b + 1], start=True, stop=True)
            m.then_inc(S("so"), 1)

        def pe_out_proj(items, src, n):
            for k in range(KT):
                item = items[k // 4]
                if k % 4 == 0:
                    item_ready(pe, item)
                if k >= 4:
                    pe.wait_ge(S("mix_added"), 8 * n + k - 3)
                w3 = third(item[0], (k % 4) // 2)
                for kk in range(KT):
                    m = pe.matmul(PS[:, 4 + k % 4, 0:TOK], w3[:, kk, (k % 2) * P:(k % 2 + 1) * P], src[:, kk, :],
                                  start=(kk == 0), stop=(kk == KT - 1))
                m.then_inc(S("mix_out"), 1)
                if k >= 2:
                    pe_norm_tile(2 * n + 1, k - 2)
                if k % 4 == 3:
                    pe.wait_ge(S("mix_out"), 8 * n + k + 1)
                    pe.sem_inc(S(f"slot_used{item[0]}"), 1)

            for k in range(KT - 2, KT):
                pe_norm_tile(2 * n + 1, k)

        def dve_out_proj(n):
            if n == 0:
                for i in range(3, NS):
                    dve.wait_ge(S(f"sstate_out{i}"), 16 * len(range(i, DEC, NS)))
                dve.memset(hT[:, :, TOK:TP], 0.0)
            tmp = modA[:, 0, 0:8]
            for k in range(KT):
                dve.wait_ge(S("mix_out"), 8 * n + k + 1)
                add_gated(k, PS[:, 4 + k % 4, :], modT2[:, n], 16, tmp)
                dve.sem_inc(S("mix_added"), 1)
            dve.sem_inc(S("x_new"), 1)

        def dve_gla():
            dve.wait_ge(S("bias_out"), 16)
            dve.wait_ge(S("gla_pe"), GP["g1"] + 1)
            dve.tensor_copy(g1T[0:16, :], PS[0:16, 0, 0:TOK]).then_inc(S("gla_dve"), 1)
            for m_ in range(16):
                dve.wait_ge(S("proj"), m_ + 1)
                src = PS[:, m_ % 4, 0:TOK]
                if m_ < 4:
                    ins_ = dve.tensor_scalar(pT[:, m_, :], src, GDK ** -0.5, None, ALU.mult)
                else:
                    ins_ = dve.tensor_copy(pT[:, m_, :], src)
                ins_.then_inc(S("proj_dve"), 1)
                if m_ == 5:
                    dve.wait_ge(S("softplus"), 1)
                    for h in range(GH):
                        dv(dve.tensor_tensor_scan(cL[:, h, :], K["scanm"], Lg[:, h, 0:SEQ], 0.0, ALU.mult, ALU.add))
                    c4 = cL.rearrange("p h (c t) -> p (h c) t", t=CH)
                    d4 = dL.rearrange("p h (c t) -> p (h c) t", t=CH)
                    dve.tensor_tensor(d4, c4, c4[:, :, 31:32].broadcast_to([P, GH * 4, CH]), ALU.subtract).then_inc(S("gla_dve"), 1)
            dve.wait_ge(S("proj_dve"), 16)
            dve.wait_ge(S("exps"), 2)
            q4, k4 = pT[:, 0:4, 0:SEQ], pT[:, 4:8, 0:SEQ]
            dve.tensor_tensor(qe, qe, q4, ALU.mult)
            dve.tensor_tensor(ke, ke, k4, ALU.mult)
            c4 = cL.rearrange("p h (c t) -> p (h c) t", t=CH)
            d4 = dL.rearrange("p h (c t) -> p (h c) t", t=CH)
            dve.tensor_tensor(d4, c4, c4[:, :, 63:64].broadcast_to([P, GH * 4, CH]), ALU.subtract).then_inc(S("gla_dve"), 1)
            dve.wait_ge(S("exps"), 4)
            dve.tensor_tensor(qb, q4, cL, ALU.mult)
            dve.tensor_tensor(kd, dL, k4, ALU.mult).then_inc(S("gla_dve"), 1)
            for T in range(2):
                dve.wait_ge(S("gla_pe"), GP["v_T"] + T + 1)
                dve.tensor_copy(vtok[:, T, :], PS[:, 2 * T:2 * T + 2, :].rearrange("p b n -> p (b n)")).then_inc(S("gla_dve"), 1)
            for T in range(2):
                dve.wait_ge(S("gla_pe"), GP["kd_T"] + T + 1)
                dve.tensor_copy(kdt[:, T, :], bank(4 + T)).then_inc(S("gla_dve"), 1)
            for T in range(2):
                dve.wait_ge(S("gla_pe"), GP["att"] + T + 1)
                dve.scalar_tensor_tensor(out=attS[:, T, :, :], in0=PS[:, 6 + T, 0:256].rearrange("p (h t) -> p h t", h=GH),
                                         scalar=3e38, in1=bc(K["gmask"], 1, GH), op0=ALU.min, op1=ALU.mult).then_inc(S("gla_dve"), 1)
            for c in range(4):
                dve.wait_ge(S("upd"), c + 1)
                if c:
                    dve.wait_ge(S("o"), c + 1)
                for h in range(GH):
                    src = PS[:, 4 + 2 * (c % 2) + h // 2, (h % 2) * GDV:(h % 2 + 1) * GDV]
                    if c == 0:
                        ins_ = dve.tensor_copy(Sst[:, h, :], src)
                    else:
                        ins_ = dve.scalar_tensor_tensor(out=Sst[:, h, :], in0=Sst[:, h, :], scalar=cL[:, h, c * CH + 63:c * CH + 64],
                                                        in1=src, op0=ALU.mult, op1=ALU.add)
                ins_.then_inc(S("state"), 1)
                dve.wait_ge(S("state"), c + 1)
            dve.wait_ge(S("gla_pe"), GP["kv8_T"] + 1)
            dve.tensor_copy(vtok8[0:DEC, :], PS[0:DEC, 0:2, :].rearrange("p b n -> p (b n)"))
            dv(dve.tensor_copy(ktok8[0:DEC, :], PS[0:DEC, 2, :]))
            dve.tensor_tensor(kmask[0:DEC], bc(ktok8[0:DEC, :], 1, DEC), bc(K["ident"][0:DEC, 0:DEC], 2, hk), ALU.mult).then_inc(S("gla_dve"), 1)
            for b in range(DEC):
                dve.wait_ge(S("outer"), b + 1)
                dve.wait_ge(S(f"sstate_in{b % NS}"), 16 * (b // NS + 1))
                for h in range(GH):
                    ins_ = dve.scalar_tensor_tensor(out=sbuf[b % NS][:, h, :], in0=sbuf[b % NS][:, h, :], scalar=eg[:, h, b:b + 1],
                                                    in1=PS[:, 4 + 2 * (b % 2) + h // 2, (h % 2) * GDV:(h % 2 + 1) * GDV],
                                                    op0=ALU.mult, op1=ALU.add)
                ins_.then_inc(S("sstate"), 1)
            dve.wait_ge(S("so"), DEC)
            dve.tensor_copy(oT[:, :, SEQ:TOK], PS[:, 3, 0:64].rearrange("p (j b) -> p j b", b=DEC)).then_inc(S("gla_dve"), 1)
            rs4 = pT[:, 0:4, :]
            dve.wait_ge(S("o_rms"), 1)
            dv(dve.reciprocal(rs4, rs4))
            for j in range(8):
                ins_ = dve.scalar_tensor_tensor(out=oT[:, j, :], in0=oT[:, j, :], scalar=vT[:, 40 + j % 2:41 + j % 2],
                                                in1=pT[:, j // 2, :], op0=ALU.mult, op1=ALU.mult)
            dv(ins_)
            dve.tensor_tensor(oT[:], oT[:], pT[:, 16:24, :], ALU.mult).then_inc(S("mix_in"), 1)

        def act_gla():
            nb = eg.rearrange("p h b -> p (h b)")[:, 0:4]
            ac(act.mul(nb, vT[:, 42:46], -1.0))
            act.wait_ge(S("gla_pe"), GP["z"] + 1)
            for h in range(GH):
                ins_ = act.activation(Lg[:, h, :], PS[:, 4 + h, 0:TOK], ACT.Exp, bias=nb[:, h:h + 1], scale=-1.0)
            ac(ins_)
            act.activation(Lg, Lg, ACT.Ln, bias=K["ones"][:, 0:1], scale=1.0).then_inc(S("softplus"), 1)
            act.wait_ge(S("softplus"), 1)
            act.activation(eg, Lg[:, :, SEQ:TOK], ACT.Exp, scale=-1 / 16)
            act.wait_ge(S("gla_dve"), GD["dL"] + 1)
            act.activation(qe, dL, ACT.Exp, scale=-1 / 16).then_inc(S("exps"), 1)
            act.activation(ke, dL, ACT.Exp, scale=1 / 16).then_inc(S("exps"), 1)
            for m_ in range(16, 24):
                act.wait_ge(S("proj"), m_ + 1)
                act.activation(pT[:, m_, :], PS[:, m_ % 4, 0:TOK], ACT.Silu).then_inc(S("proj_act"), 1)
            act.wait_ge(S("gla_dve"), GD["dE"] + 1)
            act.activation(dL, dL, ACT.Exp, scale=1 / 16).then_inc(S("exps"), 1)
            act.activation(cL, cL, ACT.Exp, scale=-1 / 16).then_inc(S("exps"), 1)
            for c in range(4):
                act.wait_ge(S("o"), c + 1)
                act.copy(oT[:, :, c * CH:(c + 1) * CH], bank(c % 2).rearrange("p (j t) -> p j t", t=CH)).then_inc(S("o_out"), 1)
            act.wait_ge(S("gla_dve"), GD["o_all"] + 1)
            act.wait_ge(S("o_out"), 4)
            act.activation(osq, oT[:], ACT.Square).then_inc(S("o_sq"), 1)
            act.wait_ge(S("gla_pe"), GP["o_ms"] + 1)
            act.activation(pT[:, 0:4, :], PS[:, 0:4, 0:TOK], ACT.Sqrt, bias=K["eps"]).then_inc(S("o_rms"), 1)
            for i in range(NS):
                act.wait_ge(S(f"sstate_out{i}"), 16 * len(range(i, DEC, NS)))
            act.wait_ge(S("out_pool"), 16)

        def pool_gla():
            pool.wait_ge(S("state"), 4)
            pool.dma_start(outs["gla_p"][0, 0].rearrange("h d v -> d h v"), Sst).then_inc(S("out_pool"), 16)
            pool.wait_ge(S("gla_pe"), GP["kv8_T"] + 1)
            pool.wait_ge(S("gla_dve"), GD["kd"] + 1)
            for b in range(DEC):
                if b >= NS:
                    store_state(b - NS)
                    pool.wait_ge(S(f"sstate_out{b % NS}"), 16 * (b // NS))
                    pool.wait_ge(S("so"), b - NS + 1)
                pool.dma_start(sbuf[b % NS], ins["state_gla"][0, b].rearrange("h d v -> d h v")).then_inc(S(f"sstate_in{b % NS}"), 16)
            for b in range(DEC - NS, DEC):
                store_state(b)
            for i in range(NS):
                pool.wait_ge(S(f"sstate_out{i}"), 16 * len(range(i, DEC, NS)))

        def store_state(b):
            pool.wait_ge(S("sstate"), b + 1)
            pool.dma_start(outs["gla_s"][0, b].rearrange("h d v -> d h v"), sbuf[b % NS]).then_inc(S(f"sstate_out{b % NS}"), 16)

        tk = carver()
        xg = tk(D)
        xgT = tk(KT, P)
        sg = [tk(P) for _ in range(2)]
        hm = [tk(P) for _ in range(2)]
        hTt = [tk(P) for _ in range(2)]
        ysb = [tk(512) for _ in range(2)]
        tk.at[0] = 4096
        hrow = tk(TT, D)
        yb = [arena[:, 4096 * i:4096 * (i + 1)].rearrange("p (k n) -> p k n", k=4) for i in range(2)]
        sgS, hsS = (arena[:, o:o + 2 * TOK].rearrange("p (k t) -> p k t", k=2) for o in (2112, 2112 + 2 * TOK))
        tk.at[0] = 8192
        s_, sel, c1, c2, msk, rep, Mf, Wt, Rr = (tk(TT, NE) for _ in range(9))
        gm = tk(24, 8)
        gs, rank = tk(24), tk(24)
        top8 = tk(TT, 8)
        wsum = tk(TT)
        Mb = tk(TT, NE, dt=BF16)
        Qall, Rall = tk(TT, NB), tk(TT, NB)
        MV = tk(NB, TT, 4, dt=BF16)
        acc = arena[:, tk.at[0]:tk.at[0] + D]
        yS = arena[:, tk.at[0] + D:tk.at[0] + D + 512].rearrange("p (k n) -> p k n", k=TOPK)
        accS = arena[:, tk.at[0] + D + 512:tk.at[0] + D + 640].rearrange("p (c n) -> p c n", c=2)
        WkS = arena[:, tk.at[0] + D + 640:tk.at[0] + D + 648]
        Sel = [tk(TT, 7, P, dt=BF16) for _ in range(2)]
        QT, RT = tk(TT, P), tk(TT, P)
        cnt, nch, base, ovt = tk(1), tk(1), tk(1), tk(4)
        OV, OVb, OVc = tk(NOV), tk(NOV), tk(NOV)
        Ls = tk(NB, 4)
        Lx = arena[:, 7168:7168 + 2 * NB].rearrange("p (m c) -> p m c", c=4)
        t1, t2 = tk(NB), tk(NB)
        gidx = tk(NB // 2 + 1).bitcast(I32)
        sidx = tk(NB).bitcast(I32)
        gi, si = tk(1).bitcast(I32), tk(2).bitcast(I32)
        eid, npr = tk(NOV).bitcast(I32), tk(1).bitcast(I32)
        nprf = tk(1)
        Wk = tk(TT, 8)
        wtmp = tk(8, NE)
        mix8 = tk(KT, DEC)
        wr = mrow[:, 0:KT * NE].rearrange("p (k e) -> p k e", k=KT)
        rb = mrow[:, 512:512 + NE]

        hrow_d = [nc.dram_tensor(f"h_rows{l}", (TOK, D), F32, kind="Internal").ap() for l in range(2)]
        y_d = [nc.dram_tensor(f"y_rows{l}", (TOK * TOPK * 2, D // 2), F32, kind="Internal").ap() for l in range(2)]

        PER = dict(route_w=32, logits=1, hrow_T=3, hrow_sb=3, route_exp=1, sh_gu=1, mask=1, place=1,
                   sh_h=1, sh_out=8, sh_y=8, nch=1, base=1, places=1, QR_T=1, OV=1,
                   over_T=1, sh_silu=1, hrow_out=48, acc=4, acc_T=4, acc_out=2, y_in0=32, y_in1=32, y_in2=128,
                   y_used=4, all_scattered=1, lists=1, sel=7, sel_used=7)

        PER["route_pe"], PER["route_dve"] = 10, 6
        RP = [{'logits': 0, 'hrow_T': 1, 'sh_gu': 4, 'place': 5, 'base': 6, 'QR_T': 7, 'over_T': 8, 'swap': 9},
              {'logits': 0, 'hrow_T': 1, 'place': 4, 'base': 5, 'QR_T': 6, 'over_T': 7, 'sh_gu': 8, 'swap': 9}]
        RD = [{'mask': 0, 'sh_h': 1, 'places': 2, 'nch': 3, 'OV': 4, 'pair': 5},
              {'mask': 0, 'places': 1, 'nch': 2, 'OV': 3, 'sh_h': 4, 'pair': 5}]

        def M(l, name):
            return S(f"{name}_{l}")

        def expert_w(l, e):
            wg, wu, wd = (ins[f"moe_w_{x}"][l][e] if isinstance(e, int) else ins[f"moe_w_{x}"][l][ds(e, 1)].rearrange("a k n -> (a k) n")
                          for x in ("gate", "up", "down"))
            return [wg.rearrange("(p k) n -> p (k n)", k=KT), wu.rearrange("(p k) n -> p (k n)", k=KT),
                    wd.rearrange("(k p) n -> p k n", p=P)]

        def load_expert(s, e, l, sem):
            for t, src in enumerate(expert_w(l, e)):
                dst = ring[:, s, t, :]
                if t == 2:
                    dst = dst.rearrange("p (k n) -> p k n", k=2)
                sp.dma_start(dst, src).then_inc(sem, 16)

        def sp_router(l):
            if l:
                sp.wait_ge(S("mix_in"), 2)
            else:
                sp.wait_ge(S("mod_fold"), 8)
            sp.dma_start(wr, ins["moe_w_router"][l].rearrange("(k p) e -> p k e", p=P)).then_inc(S("route_w"), 16)
            sp.dma_start(rb, ins["moe_router_bias"][l:l + 1, :].broadcast_to([P, NE])).then_inc(S("route_w"), 16)

        def sp_moe(l):
            load_item(it_sh[l], [cols(ins["shared_w_gate"][l], 0), cols(ins["shared_w_up"][l], 0),
                                 ins["shared_w_down"][l].rearrange("(k p) n -> p k n", p=P)])

        def sp_experts_first(l):
            for u in range(WS):
                s, n = it_ex[l][u]
                sp.wait_ge(S(f"slot_used{s}"), prior[it_ex[l][u]])
                load_expert(s, u, l, S(f"slot_loaded{s}"))

        def sp_experts(l):
            with sp.Fori(1, NE // WS) as i:
                for u in range(WS):
                    s = it_ex[l][u][0]
                    sp.wait_ge(M(l, "y"), i * WS + (u - WS + 1))
                    load_expert(s, i * WS + u, l, S(f"slot_loaded{s}"))
            sp.wait_ge(S("lists"), PER["lists"] * l + 1)
            n2 = sp.value_load(npr[0:1, 0:1], min_val=1, max_val=NOV // 2)
            with sp.Fori(0, n2) as i:
                for u in range(2):
                    sp.wait_ge(M(l, "y"), i * 2 + (NE + u - 1))
                    e = sp.value_load(eid[0:1, ds(i * 2 + u, 1)], min_val=0, max_val=NE - 1)
                    load_expert(it_ex[l][u][0], e, l, M(l, f"over_loaded{u}"))

        def pe_route(l):
            pe.wait_ge(S("h_ready"), 2 * l + 2)
            pe.wait_ge(S("route_w"), PER["route_w"] * l + 32)
            for T in range(TT):
                for k in range(KT):
                    m = pe.matmul(PS[:, 0, T * NE:(T + 1) * NE], hT[:, k, T * P:(T + 1) * P], wr[:, k, :], start=(k == 0), stop=(k == KT - 1))
            m.then_inc(S("route_pe"), 1)
            for T in range(TT):
                n = P if T < 2 else DEC
                for half in range(2):
                    for k in range(4):
                        m = pe.transpose(PS[0:n, 1 + 2 * T + half, k * P:(k + 1) * P], hT[:, 4 * half + k, T * P:T * P + n], K["ident"])
                m.then_inc(S("route_pe"), 1)
            s = it_sh[l][0]
            wd2 = ring[:, s, 2, :].rearrange("p (k n) -> p k n", k=2)

            def shared_in(t):
                item_ready(pe, it_sh[l])
                for j in range(2):
                    for k in range(KT):
                        m = pe.matmul(PS[:, 4 + 2 * t + j, 0:TOK], third(s, t)[:, k, j * P:(j + 1) * P], hT[:, k, 0:TOK], start=(k == 0), stop=(k == KT - 1))
                if t:
                    m.then_inc(S("route_pe"), 1)

            def shared_out():
                pe.wait_ge(S("route_dve"), PER["route_dve"] * l + RD[l]["sh_h"] + 1)
                for k in range(KT):
                    if k >= 4:
                        pe.wait_ge(S("sh_out"), PER["sh_out"] * l + (k - 3))
                    for kk in range(2):
                        m = pe.matmul(PS[:, 4 + k % 4, 0:TOK], wd2[:, kk, k * P:(k + 1) * P], hsS[:, kk, :], start=(kk == 0), stop=(kk == 1))
                    m.then_inc(S("sh_y"), 1)
                pe.wait_ge(S("sh_y"), PER["sh_y"] * l + KT)
                pe.sem_inc(S(f"slot_used{s}"), 1)
            pe.wait_ge(S("hrow_sb"), PER["hrow_sb"] * l + 3)
            pe.wait_ge(S("route_exp"), PER["route_exp"] * l + 1)
            if l == 0:
                shared_in(0)
                shared_in(1)
            pe.wait_ge(S("route_dve"), PER["route_dve"] * l + RD[l]["mask"] + 1)
            for T in range(TT):
                for T2 in range(T + 1):
                    m = pe.matmul(PS[:, 1, T * NE:(T + 1) * NE], (triB if T2 == T else onesB)[:], Mb[:, T2, :], start=(T2 == 0), stop=(T2 == T))
            for T in range(TT):
                m = pe.matmul(PS[0:NE, 2, 0:1], Mb[:, T, :], onesB[:, 0:1], start=(T == 0), stop=(T == TT - 1))
            m.then_inc(S("route_pe"), 1)
            if l == 0:
                shared_out()
            pe.wait_ge(S("route_dve"), PER["route_dve"] * l + RD[l]["nch"] + 1)
            m = pe.matmul(PS[0:NE, 2, 8:9], K["tri"][0:NE, 0:NE], nch[0:NE, :], start=True, stop=True)
            m.then_inc(S("route_pe"), 1)
            pe.wait_ge(S("route_dve"), PER["route_dve"] * l + RD[l]["places"] + 1)
            if l == 0:
                pe.wait_ge(S("sh_out"), KT)
            for T in range(TT):
                m = pe.transpose(PS[0:NE, 3, T * P:(T + 1) * P], Qall[:, T, 0:NE], K["ident"])
                m = pe.transpose(PS[0:NE, 4, T * P:(T + 1) * P], Rall[:, T, 0:NE], K["ident"])
            m.then_inc(S("route_pe"), 1)
            pe.wait_ge(S("route_dve"), PER["route_dve"] * l + RD[l]["OV"] + 1)
            for T in range(TT):
                m = pe.matmul(PS[:, 0, T * NOV:(T + 1) * NOV], QT[0:NE, T, :], OV[0:NE, :], start=True, stop=False)
                m = pe.matmul(PS[:, 0, T * NOV:(T + 1) * NOV], K["ones1024"][0:NE, :], OVc[0:NE, :], start=False, stop=True)
                m = pe.matmul(PS[:, 0, 128 + T * NOV:128 + (T + 1) * NOV], RT[0:NE, T, :], OV[0:NE, :], start=True, stop=True)
            m = pe.matmul(PS[0:1, 2, 16:16 + NOV], K["pcol"][0:NE, :], OV[0:NE, :], start=True, stop=True)
            m = pe.matmul(PS[0:1, 2, 64:65], K["ones"][0:NE, :], nch[0:NE, :], start=True, stop=True)
            m.then_inc(S("route_pe"), 1)
            for i in range(7):
                if l == 1 and i < 2:
                    shared_in(i)
                elif l == 1 and i == 3:
                    shared_out()
                pe.wait_ge(S("sel"), PER["sel"] * l + i + 1)
                for m2 in range(7 * i, 7 * i + 7):
                    for T in range(TT):
                        m = pe.matmul(PS[:, 3, 8 * m2:8 * m2 + 8].rearrange("p (b c) -> p b c", c=4), Sel[i % 2][:, T, m2 - 7 * i, :],
                                      MV[:, 2 * m2:2 * m2 + 2, T, :], start=(T == 0), stop=(T == TT - 1))
                m.then_inc(S("sel_used"), 1)
                if l == 0:
                    pe_ada(1, [i])
            pe.wait_ge(S("route_dve"), PER["route_dve"] * l + RD[l]["pair"] + 1)
            pe.wait_ge(S("sh_out"), PER["sh_out"] * l + KT)
            for b in range(2):
                m = pe.matmul(PS[CAP * b:CAP * b + CAP, 7, 0:2 * NB], K["ident"][:, CAP * (1 - b):CAP * (2 - b)], Lx.rearrange("p m c -> p (m c)"), start=True, stop=True)
            m.then_inc(S("route_pe"), 1)
            if l == 0:
                pe_ada(1, [7])
                pe.wait_ge(S("mod_T"), 16)

        def pe_turn_pair(l, m):
            wait_alone(pe, M(l, "gathered"), m * 16 + 16)
            xv = xg.rearrange("t (p k) -> t k p", k=KT)
            for k in range(KT):
                ins_ = pe.transpose(PS[:, k // 4, (k % 4) * P:(k % 4 + 1) * P], xv[:, k, :], K["ident"])
            ins_.then_inc(M(l, "tx"), 1)

        def pe_body(l, n, h2, u, s, wsem, wval):
            b = u % 2
            if b == 0:
                pe.wait_ge(M(l, "xgT"), h2 + 1)
            wait_alone(pe, wsem, wval)
            gu = ring[:, s, 0:2, :].rearrange("p g (k n) -> p g k n", k=KT)
            for k in range(KT):
                for half in range(2):
                    m = pe.matmul(PS[64 * half:64 * half + 64, 2 + b, 0:256].rearrange("p (g n) -> p g n", g=2), xgT[:, k, CAP * b:CAP * b + CAP],
                                  gu[:, :, k, half * P:(half + 1) * P], start=(k == 0), stop=(k == KT - 1), skip_group_check=True)
            m.then_inc(M(l, "gu"), 1)
            if b == 1:
                pe_turn_pair(l, h2 + 1)
            pe.wait_ge(M(l, "hm"), n + 1)
            pe.transpose(PS[:, 4 + b, 0:P], hm[b], K["ident"]).then_inc(M(l, "th"), 1)
            pe.wait_ge(M(l, "hT"), n + 1)
            for kk in range(2):
                for j in range(2):
                    m = pe.matmul(PS[64 * j:64 * j + 64, 6 + b, :], hTt[b][:, kk * CAP:(kk + 1) * CAP],
                                  ring[:, s, 2, kk * D + 512 * j:kk * D + 512 * j + 512], start=(kk == 0), stop=(kk == 1), skip_group_check=True)
            m.then_inc(M(l, "y"), 1)

        def main_and_overflow(eng, l, body, first_apart=False):
            if first_apart:
                for u in range(WS):
                    body(0, u, u // 2, u, False)
            with eng.Fori(int(first_apart), NE // WS) as i:
                for u in range(WS):
                    body(i, i * WS + u, i * 2 + u // 2, u, False)
            eng.wait_ge(S("lists"), PER["lists"] * l + 1)
            n2 = eng.value_load(npr[0:1, 0:1], min_val=1, max_val=NOV // 2)
            with eng.Fori(0, n2) as i:
                for u in range(2):
                    body(i, i * 2 + (NE + u), i + NE // 2, u, True)
            return n2

        def pe_experts(l):
            pe.wait_ge(S("lists"), PER["lists"] * l + 1)

            def body(i, n, h2, u, over):
                s, first = it_ex[l][u]
                if over:
                    pe_body(l, n, h2, u, s, M(l, f"over_loaded{u}"), i * 48 + 48)
                else:
                    pe_body(l, n, h2, u, s, S(f"slot_loaded{s}"), i * 48 + 48 * first)
            pe_turn_pair(l, 0)
            main_and_overflow(pe, l, body)

        def pe_combine(l):
            pe.wait_ge(S("acc"), PER["acc"] * l + 1)
            pe.matmul(PS[:, 2, 0:TOPK], K["expand"][0:DEC, :], Wk[0:DEC, 2, :], start=True, stop=True).then_inc(S("acc_T"), 1)
            pe.wait_ge(S("acc"), PER["acc"] * l + 2)
            pe.transpose(PS[:, 3, 0:P], accS.rearrange("p c n -> p (c n)"), K["ident"]).then_inc(S("acc_T"), 1)
            for T in range(2):
                pe.wait_ge(S("acc"), PER["acc"] * l + (T + 3))
                if T:
                    pe.wait_ge(S("acc_out"), PER["acc_out"] * l + T)
                for k in range(KT):
                    m = pe.transpose(PS[:, k // 4, (k % 4) * P:(k % 4 + 1) * P], acc[:, k * P:(k + 1) * P], K["ident"])
                m.then_inc(S("acc_T"), 1)

        def dve_shared(l):
            dve.wait_ge(S("sh_silu"), PER["sh_silu"] * l + 1)
            dve.tensor_tensor(hsS, sgS, PS[:, 6:8, 0:TOK], ALU.mult).then_inc(S("route_dve"), 1)

        def dve_route(l):
            dve.wait_ge(S("route_exp"), PER["route_exp"] * l + 1)
            f = lambda a: a.rearrange("p t e -> p (t e)")
            dv(dve.tensor_scalar(s_, s_, 1.0, None, ALU.add))
            dv(dve.reciprocal(s_, s_))
            dv(dve.tensor_tensor(sel, s_, bc(rb, 1, TT), ALU.add))
            for j in range(24):
                ins_ = dve.max(gm[:, j, :], f(sel)[:, 8 * j:8 * j + 8])
            dv(ins_)
            dv(dve.tensor_tensor(gs, gm[:, :, 0], gm[:, :, 1], ALU.add))
            g3 = gs.rearrange("p (t g) -> p t g", g=8)
            v4 = lambda a: a.rearrange("p t (g h) -> p t g h", g=8)
            dv(dve.tensor_tensor(v4(c1), bc(g3, 2, 8), bc(g3, 3, 8), ALU.is_gt))
            dv(dve.tensor_tensor(v4(c2), bc(g3, 2, 8), bc(g3, 3, 8), ALU.is_equal))
            dv(dve.tensor_tensor(c2, c2, bc(K["gtri"], 1, TT), ALU.mult))
            dv(dve.tensor_tensor(c1, c1, c2, ALU.add))
            dv(dve.tensor_reduce(rank, f(c1).rearrange("p (g h) -> p g h", h=8), AX, ALU.add))
            dv(dve.tensor_scalar(rank, rank, TOPG - 0.5, NEG, ALU.is_ge, ALU.mult))
            dv(dve.tensor_tensor(f(msk).rearrange("p (g h) -> p g h", h=8), f(sel).rearrange("p (g h) -> p g h", h=8), bc(rank, 2, 8), ALU.add))
            for T in range(TT):
                ins_ = dve.max(top8[:, T, :], msk[:, T, :])
            dv(ins_)
            for T in range(TT):
                ins_ = dve.match_replace(rep[:, T, :], top8[:, T, :], msk[:, T, :], GONE)
            dv(ins_)
            dv(dve.tensor_scalar(Mf, rep, GONE, None, ALU.is_equal))
            dv(dve.tensor_tensor(Wt, s_, Mf, ALU.mult))
            dv(dve.tensor_reduce(wsum, Wt, AX, ALU.add))
            dv(dve.reciprocal(wsum, wsum))
            dv(dve.tensor_scalar(wsum, wsum, ROUTE_SCALE, None, ALU.mult))
            dv(dve.tensor_tensor(Wt, Wt, bc(wsum, 2, NE), ALU.mult))
            dv(dve.tensor_tensor(Mf, Mf, bc(K["valid"], 2, NE), ALU.mult))
            dve.tensor_copy(Mb, Mf).then_inc(S("route_dve"), 1)
            for T in range(TT):
                ins_ = dve.tensor_tensor_scan(Rr[:, T, :], K["ones"].broadcast_to([P, NE]), Mf[:, T, :], 0.0, ALU.mult, ALU.add)
            dv(ins_)
            dv(dve.tensor_scalar(Rall[:, :, 0:NE], Rr, 1.0, None, ALU.subtract))
            if l == 0:
                dve_shared(l)
            dve.wait_ge(S("route_pe"), PER["route_pe"] * l + RP[l]["place"] + 1)
            dve.scalar_tensor_tensor(out=Qall[:, :, 0:NE], in0=PS[:, 1, 0:192].rearrange("p (t e) -> p t e", e=NE), scalar=1.0,
                                     in1=Mf, op0=ALU.add, op1=ALU.mult).then_inc(S("route_dve"), 1)
            dv(dve.tensor_copy(cnt[0:NE, :], PS[0:NE, 2, 0:1]))
            dv(dve.tensor_scalar(ovt[0:NE, :], K["iota"][0:NE, 1:5], float(CAP), cnt[0:NE, :], ALU.mult, ALU.is_lt))
            dve.tensor_reduce(nch[0:NE, :], ovt[0:NE, :], AX, ALU.add).then_inc(S("route_dve"), 1)
            dve.wait_ge(S("route_pe"), PER["route_pe"] * l + RP[l]["base"] + 1)
            dv(dve.tensor_copy(base[0:NE, :], PS[0:NE, 2, 8:9]))
            dv(dve.tensor_scalar(OVc[0:NE, :], K["iota"][0:NE, :], base[0:NE, :], None, ALU.is_ge))
            dv(dve.tensor_scalar(OVb[0:NE, :], K["iota"][0:NE, :], base[0:NE, :], None, ALU.subtract))
            dve.wait_ge(S("route_dve"), PER["route_dve"] * l + RD[l]["nch"] + 1)
            dv(dve.scalar_tensor_tensor(out=OV[0:NE, :], in0=OVb[0:NE, :], scalar=nch[0:NE, :], in1=OVc[0:NE, :], op0=ALU.is_lt, op1=ALU.mult))
            dv(dve.tensor_scalar(OVb[0:NE, :], OVb[0:NE, :], 1.0, -1024.0 * CAP, ALU.add, ALU.mult))
            dv(dve.tensor_tensor(OVc[0:NE, :], OVb[0:NE, :], OV[0:NE, :], ALU.mult))
            dve.wait_ge(S("route_pe"), PER["route_pe"] * l + RP[l]["QR_T"] + 1)
            dve.tensor_copy(QT[0:NE], PS[0:NE, 3, 0:384].rearrange("p (t c) -> p t c", c=P))
            dve.tensor_copy(RT[0:NE], PS[0:NE, 4, 0:384].rearrange("p (t c) -> p t c", c=P)).then_inc(S("route_dve"), 1)
            dve.wait_ge(S("route_pe"), PER["route_pe"] * l + RP[l]["over_T"] + 1)
            dve.tensor_copy(Qall[:, :, NE:NB], PS[:, 0, 0:TT * NOV].rearrange("p (t e) -> p t e", e=NOV))
            dve.tensor_copy(Rall[:, :, NE:NB], PS[:, 0, 128:128 + TT * NOV].rearrange("p (t e) -> p t e", e=NOV))
            dve.tensor_copy(eid[0:1, :], PS[0:1, 2, 16:16 + NOV])
            dv(dve.tensor_scalar(nprf[0:1, :], PS[0:1, 2, 64:65], 0.5, 0.25, ALU.mult, ALU.add))
            dve.tensor_scalar(npr[0:1, :], nprf[0:1, :], 1.0, None, ALU.max)
            dve.tensor_copy(MV[:, :, :, 0], bc(K["pcol"].broadcast_to([P, TT]), 1, NB))
            for T in range(TT):
                dve.memset(MV[:, :, T, 1:2], float(T))
            dve.memset(MV[:, :, :, 3:4], 1.0)
            dve.memset(gidx, 0)
            dv(dve.tensor_copy(MV[:, :, :, 2], Rall.rearrange("p t b -> p b t")))
            for i in range(7):
                if l == 1 and i == 3:
                    dve_shared(l)
                if i >= 2:
                    dve.wait_ge(S("sel_used"), PER["sel_used"] * l + i - 1)
                for T in range(TT):
                    ins_ = dve.tensor_tensor(Sel[i % 2][:, T].rearrange("p m (b s) -> p (m b) s", b=2), bc(slotB[:, 0:CAP], 1, 14),
                                             bc(Qall[:, T, 14 * i:14 * i + 14], 2, CAP), ALU.is_equal)
                ins_.then_inc(S("sel"), 1)
                if l == 0 and i:
                    dve_ada(1, [i - 1])
            dve.wait_ge(S("sel_used"), PER["sel_used"] * l + 7)
            halves = [slice(CAP * b, CAP * b + CAP) for b in range(2)]
            pairs = lambda a: a.rearrange("p (m b) c -> p b m c", b=2)
            for b, q in enumerate(halves):
                ins_ = dve.tensor_copy(Lx[q], pairs(PS[:, 3, 0:NB * 4].rearrange("p (b c) -> p b c", c=4))[q, b])
            ins_.then_inc(S("route_dve"), 1)
            dve.wait_ge(S("route_dve"), PER["route_dve"] * l + RD[l]["pair"] + 1)
            for b, q in enumerate(halves):
                dve.tensor_copy(pairs(Ls)[q, b], Lx[q])
            dve.wait_ge(S("route_pe"), PER["route_pe"] * l + RP[l]["swap"] + 1)
            for b, q in enumerate(halves):
                ins_ = dve.tensor_copy(pairs(Ls)[q, 1 - b], PS[q, 7, 0:2 * NB].rearrange("p (m c) -> p m c", c=4))
            dv(ins_)
            dv(dve.scalar_tensor_tensor(out=t1, in0=Ls[:, :, 1], scalar=128.0, in1=Ls[:, :, 0], op0=ALU.mult, op1=ALU.add))
            dv(dve.scalar_tensor_tensor(out=t2, in0=Ls[:, :, 3], scalar=-float(OOB), in1=t1, op0=ALU.mult, op1=ALU.add))
            dv(dve.tensor_scalar(t2, t2, float(OOB), None, ALU.add))
            for b in range(2):
                q = slice(CAP * b, CAP * b + CAP)
                dve.tensor_copy(gidx[q, 0:NB // 2], t2.rearrange("p (m b) -> p b m", b=2)[q, b])
            dv(dve.memset(xg, 0.0))
            dv(dve.tensor_scalar(t2, t1, 16.0, K["jcol"], ALU.mult, ALU.add))
            dv(dve.scalar_tensor_tensor(out=t2, in0=Ls[:, :, 2], scalar=2.0, in1=t2, op0=ALU.mult, op1=ALU.add))
            dv(dve.scalar_tensor_tensor(out=t2, in0=Ls[:, :, 3], scalar=-float(OOB), in1=t2, op0=ALU.mult, op1=ALU.add))
            dve.tensor_copy(sidx[:, 0:NB], t2).then_inc(S("lists"), 1)
            if l == 0:
                dve_ada(1, [6, 7])

        def dve_experts(l):
            def body(i, n, h2, u, over):
                b = u % 2
                dve.wait_ge(M(l, "sg"), n + 1)
                dve.tensor_tensor(hm[b], sg[b], PS[:, 2 + b, P:2 * P], ALU.mult).then_inc(M(l, "hm"), 1)
                dve.wait_ge(M(l, "y"), n + 1)
                if not isinstance(n, int) or n >= 2:
                    dve.wait_ge(M(l, f"scattered{b}"), h2 * 16)
                dve.tensor_copy(ysb[b], bank(6 + b)).then_inc(M(l, "ysb"), 1)
            main_and_overflow(dve, l, body, True)

        def dve_combine(l):
            for T in range(TT):
                for r in range(8):
                    ins_ = dve.scalar_tensor_tensor(out=wtmp[:, r, :], in0=Rall[:, T, 0:NE], scalar=float(r), in1=Wt[:, T, :], op0=ALU.is_equal, op1=ALU.mult)
                dv(ins_)
                dv(dve.tensor_tensor(wtmp, wtmp, bc(Mf[:, T, :], 1, 8), ALU.mult))
                dv(dve.tensor_reduce(Wk[:, T, :], wtmp, AX, ALU.add))
            dve.sem_inc(S("acc"), 1)
            dve.wait_ge(S("acc_T"), PER["acc_T"] * l + 1)
            dv(dve.tensor_copy(WkS, PS[:, 2, 0:TOPK]))
            dve.wait_ge(S("y_in2"), PER["y_in2"] * (l + 1))
            for r in range(TOPK):
                if r == 0:
                    ins_ = dve.tensor_scalar(accS[:, 0, :], yS[:, r, :], WkS[:, r:r + 1], None, ALU.mult)
                else:
                    ins_ = dve.scalar_tensor_tensor(out=accS[:, 0, :], in0=yS[:, r, :], scalar=WkS[:, r:r + 1], in1=accS[:, 0, :], op0=ALU.mult, op1=ALU.add)
                dv(ins_)
            dve.tensor_copy(accS[:, 1, :], accS[:, 0, :]).then_inc(S("acc"), 1)
            dve.wait_ge(S("acc_T"), PER["acc_T"] * l + 2)
            for c in range(2):
                q = slice(64 * c, 64 * c + 64)
                ins_ = dve.tensor_tensor(mix8[q], PS[q, 3, 0:P].rearrange("p (t k c) -> p c k t", k=KT, c=2)[:, c], shT[q, :, SEQ:TOK], ALU.add)
            dv(ins_)
            dv(dve.tensor_tensor(mix8, mix8, modT2[:, l, 40:48, 1:9], ALU.mult))
            dve.tensor_tensor(xT[:, :, SEQ:TOK], xT[:, :, SEQ:TOK], mix8, ALU.add)
            for T in range(2):
                if T:
                    dve.wait_ge(S("acc_T"), PER["acc_T"] * l + (T + 2))
                for half in range(2):
                    dve.wait_ge(S(f"y_in{half}"), PER["y_in0"] * l + 16 * (T + 1))
                    for r in range(4):
                        src, w = yb[half][:, r, :], Wk[:, T, 4 * half + r:4 * half + r + 1]
                        if half == 0 and r == 0:
                            ins_ = dve.tensor_scalar(acc, src, w, None, ALU.mult)
                        else:
                            ins_ = dve.scalar_tensor_tensor(out=acc, in0=src, scalar=w, in1=acc, op0=ALU.mult, op1=ALU.add)
                        dv(ins_)
                    dve.sem_inc(S("y_used"), 1)
                dve.sem_inc(S("acc"), 1)
                dve.wait_ge(S("acc_T"), PER["acc_T"] * l + (T + 3))
                c0 = T * P
                for half in range(2):
                    sh = shT[:, 4 * half:4 * half + 4, c0:c0 + P]
                    ins_ = dve.tensor_tensor(sh, PS[:, half, :].rearrange("p (k t) -> p k t", k=4), sh, ALU.add)
                dv(ins_)
                for k in range(KT):
                    ins_ = dve.scalar_tensor_tensor(out=xT[:, k, c0:c0 + P], in0=shT[:, k, c0:c0 + P], scalar=modT2[:, l, 40 + k, 0:1],
                                                    in1=xT[:, k, c0:c0 + P], op0=ALU.mult, op1=ALU.add)
                ins_.then_inc(S("acc_out"), 1)
            dve.wait_ge(S("acc_out"), PER["acc_out"] * l + 2)
            dve.sem_inc(S("x_new"), 1)

        def act_route(l):
            act.wait_ge(S("route_pe"), PER["route_pe"] * l + RP[l]["logits"] + 1)
            act.activation(s_, PS[:, 0, 0:192].rearrange("p (t e) -> p t e", e=NE), ACT.Exp, scale=-1.0).then_inc(S("route_exp"), 1)
            for T in range(TT):
                n = P if T < 2 else DEC
                act.wait_ge(S("route_pe"), PER["route_pe"] * l + RP[l]["hrow_T"] + (T + 1))
                act.copy(hrow[0:n, T, :], PS[0:n, 1 + 2 * T:3 + 2 * T, :].rearrange("p b n -> p (b n)")).then_inc(S("hrow_sb"), 1)
                act.wait_ge(S("hrow_sb"), PER["hrow_sb"] * l + (T + 1))
                act.dma_start(hrow_d[l][T * P:T * P + n, :], hrow[0:n, T, :]).then_inc(S("hrow_out"), 16)
            act.wait_ge(S("route_pe"), PER["route_pe"] * l + RP[l]["sh_gu"] + 1)
            act.activation(sgS, PS[:, 4:6, 0:TOK], ACT.Silu).then_inc(S("sh_silu"), 1)
            for k in range(KT):
                act.wait_ge(S("sh_y"), PER["sh_y"] * l + (k + 1))
                act.copy(shT[:, k, :], PS[:, 4 + k % 4, 0:TOK]).then_inc(S("sh_out"), 1)

        def act_experts(l):
            def body(i, n, h2, u, over):
                b = u % 2
                act.wait_ge(M(l, "gu"), n + 1)
                act.activation(sg[b], PS[:, 2 + b, 0:P], ACT.Silu).then_inc(M(l, "sg"), 1)
                act.wait_ge(M(l, "th"), n + 1)
                act.copy(hTt[b], PS[:, 4 + b, 0:P]).then_inc(M(l, "hT"), 1)
                if b == 1:
                    evict_pair(h2 + 1)

            def evict_pair(m):
                act.wait_ge(M(l, "tx"), m + 1)
                act.copy(xgT.rearrange("p k c -> p (k c)"), PS[:, 0:2, :].rearrange("p b n -> p (b n)")).then_inc(M(l, "xgT"), 1)
            evict_pair(0)
            n2 = main_and_overflow(act, l, body)
            act.wait_ge(M(l, "xgT"), n2 + (NE // 2 + 1))

        def act_combine(l):
            act.wait_ge(S("all_scattered"), PER["all_scattered"] * l + 1)
            for k in range(TOPK):
                src = y_d[l].rearrange("(t k j) n -> t k (j n)", k=TOPK, j=2)[SEQ:TOK, k, :].rearrange("t (f n) -> t f n", n=64)
                act.dma_start(yS[:, k, :], src).then_inc(S("y_in2"), 16)
            for T in range(2):
                for half in range(2):
                    if T:
                        act.wait_ge(S("y_used"), PER["y_used"] * l + (2 * (T - 1) + half + 1))
                    src = y_d[l].rearrange("(t k j) n -> t k (j n)", k=TOPK, j=2)[T * P:(T + 1) * P, 4 * half:4 * half + 4, :]
                    act.dma_start(yb[half], src).then_inc(S(f"y_in{half}"), 16)

        def pool_experts(l):
            pool.wait_ge(S("lists"), PER["lists"] * l + 1)
            pool.wait_ge(S("hrow_out"), PER["hrow_out"] * l + 48)

            def gather(m):
                pool.tensor_copy(gi, gidx[:, ds(m, 1)]).then_inc(M(l, "gi"), 1)
                wait_alone(pool, M(l, "gi"), m + 1)
                pool.indirect_dma_start(out=xg, out_offset=None, in_=hrow_d[l],
                                        in_offset=IndirectOffsetOnAxis(ap=gi, axis=0), bounds_check=TOK - 1, oob_is_err=False).then_inc(M(l, "gathered"), 16)

            gather(0)

            def body(i, n, h2, u, over):
                b = u % 2
                if b == 0:
                    wait_alone(pool, M(l, "tx"), h2 + 1)
                    gather(h2 + 1)
                if not isinstance(n, int) or n >= 2:
                    wait_alone(pool, M(l, f"scattered{b}"), h2 * 16)
                pool.tensor_copy(si[:, b:b + 1], sidx[:, ds(n, 1)]).then_inc(M(l, "si"), 1)
                pool.wait_ge(M(l, "si"), n + 1)
                wait_alone(pool, M(l, "ysb"), n + 1)
                pool.indirect_dma_start(out=y_d[l], out_offset=IndirectOffsetOnAxis(ap=si[:, b:b + 1], axis=0),
                                        in_=ysb[b], in_offset=None, bounds_check=2 * TOK * TOPK - 1, oob_is_err=False).then_inc(M(l, f"scattered{b}"), 16)
            n2 = main_and_overflow(pool, l, body, True)
            pool.wait_ge(M(l, "gathered"), n2 * 16 + (NE // 2 + 1) * 16)
            for b in range(2):
                pool.wait_ge(M(l, f"scattered{b}"), n2 * 16 + NE // 2 * 16)
            pool.sem_inc(S("all_scattered"), 1)

        bias_d = nc.dram_tensor("bias_rows", (AH, P, 384), F32, kind="Internal").ap()
        ohb = arena[:, 12480:12864]
        relb = arena[:, 12864:12880]
        brw = arena[:, 5264:5264 + 384 * AH].rearrange("p (h f) -> p h f", h=AH)

        def sp_bias():
            sp.dma_start(ohb[0:32, :], ins["onehot"]).then_inc(S("small_in"), 16)
            sp.dma_start(relb[0:32, :], ins["rel_bias"]).then_inc(S("small_in"), 16)

        def pe_bias(heads):
            pe.wait_ge(S("small_in"), 64)
            pe.wait_ge(S("setup_taken"), 2)
            for h in heads:
                if h >= 2:
                    pe.wait_ge(S("bias_sb"), h - 1)
                pe.matmul(PS[:, 6 + h % 2, 0:384], relb[0:32, h:h + 1].broadcast_to([32, P]), ohb[0:32, :],
                          start=True, stop=True).then_inc(S("bias_mm"), 1)

        def dve_bias(heads):
            for h in heads:
                dve.wait_ge(S("bias_mm"), h + 1)
                dve.tensor_copy(brw[:, h, :], PS[:, 6 + h % 2, 0:384]).then_inc(S("bias_sb"), 1)

        def pool_bias():
            pool.wait_ge(S("bias_sb"), AH)
            pool.dma_start(bias_d.rearrange("h p f -> p h f"), brw).then_inc(S("bias_out"), 16)

        tk = carver()
        qT = tk(8, TOK)
        kT, vTt = tk(2, TOK), tk(2, TOK)
        qiT = tk(4, TOK)
        kiT = tk(TOK)
        ktk, vtk = tk(2, 256), tk(2, 256)
        kitk = tk(2, IDH)
        k8, v8 = tk(256), tk(256)
        ki8 = tk(IDH)
        wtk = tk(2, IH)
        w8 = tk(IH)
        ptab = tk(P).bitcast(I32)
        relb2 = tk(AH)
        m8 = tk(2, 8)
        nm, rs, mx = tk(4), tk(4), tk(4)
        wS, mxn = tk(1), tk(4)
        Pn = tk(P)
        DSA0 = tk.at[0]
        Mb_ = tk(AH, 256)
        sc, sw = tk(384), tk(384)
        rl = [tk(384) for _ in range(2)]
        A2 = [tk(4, 256) for _ in range(2)]
        PTs = [tk(2, 4, P) for _ in range(2)]
        tk = carver()
        tk.at[0] = DSA0
        Sx, Wx = tk(2052), tk(2052)
        KTs = [tk(2, 512) for _ in range(2)]
        raw = [tk(4, 256) for _ in range(2)]
        Qs = tk(2, 1152)
        Qb, kin2, rbx = mrow[:, 0:320], mrow[:, 320:324], mrow[:, 384:512]
        PT = Wx[:, 0:2048].rearrange("p (j c) -> p j c", c=P)
        iraw = [r.rearrange("p a b -> p (a b)")[:, 0:512] for r in raw]
        iord = [r.rearrange("p a b -> p (a b)")[:, 512:1024] for r in raw]
        vraw = raw + [k.rearrange("p a (b n) -> p (a b) n", n=256) for k in KTs]
        vraw += [f[:, o:o + 1024].rearrange("p (a n) -> p a n", n=256) for f, o in ((Qs.rearrange("p a b -> p (a b)"), 256),
                 (Qs.rearrange("p a b -> p (a b)"), 1280), (Sx, 0), (Sx, 1024))]
        vsem = [("vp_in0", 0), ("vp_in1", 0), ("vp_in2", 0), ("vp_in3", 0), ("ik_in0", 256), ("ik_in1", 256), ("kp_in0", 256), ("kp_in1", 256)]
        prow, pcol_ = ptab[:, 0:32], ptab[:, 32:40]
        Osel = Qs.rearrange("p a b -> p (a b)")[:, 0:256]
        HK, R2 = PAST // 2 + 1, 32 + DEC
        topk_half = [slice(0, DEC), slice(32, R2)]
        Sk, Wk_, Ek = Sx[0:R2, 0:HK], Wx[0:R2, 0:HK], Wx[0:R2, HK:2 * HK]
        best = Sx[0:R2, HK:HK + 256]
        rise = Sx[0:DEC, HK + 256:HK + 512]
        thr, ngt, neq, need, nb_ = (m8[0:R2, 0, j:j + 1] for j in range(5))
        by_row = lambda a: a.rearrange("p (n r) -> p r n", r=ROW)
        xi = KTs[0].rearrange("p a b -> p (a b)")[:, 0:64]
        qi8 = KTs[1].rearrange("p a b -> p (a b)")[:, 0:512]
        dsq = A2[0].rearrange("p a b -> p (a b)")[:, 0:TOK]
        lrs = A2[1].rearrange("p a b -> p (a b)")[:, 0:TOK]

        PE_STEP = {n: i + 1 for i, n in enumerate(("wi", "ki_mean", "ki_var", "kv_T", "qi8_T", "qi_half", "ik_new", "iscore", "k_mm", "dist", "slogit", "pn", "so_done", "osel_T", "rows0", "rows1", "rows2"))}
        DVE_STEP = {n: i + 1 for i, n in enumerate(("ki_sq", "ki_ln", "kv_tok", "prow", "qi8", "Qb", "irelu", "iscore_sb", "smask", "snmax", "sprob", "pn_sb", "osel", "final", "row0", "row1", "row2"))}

        def sp_dsa():
            sp.wait_ge(S("y_used"), 3)
            wq = w_dsa
            load_item(it_dsa[0], [cols(wq, 0), cols(wq, 256), cols(wq, 1024)])
            load_item(it_dsa[1], [cols(wq, 512), cols(wq, 768), cols(wq, 1280)])
            s, n = it_dsa[2]
            sem = S(f"slot_loaded{s}")
            for t in range(2):
                sp.dma_start(third(s, t), cols(wq, 1536 + 256 * t)).then_inc(sem, 16)
            for n_, (c0, c1_, a, b) in enumerate(((0, 64, 2048, 2112), (64, 128, 2048, 2112), (128, 136, 2112, 2120))):
                sp.dma_start(third(s, 2)[:, :, c0:c1_], wq[:, a:b].rearrange("(k p) n -> p k n", p=P)).then_inc(sem if n_ == 2 else S("dsa_small"), 16)
            sp.wait_ge(S("x_new"), 3)
            sp.dma_start(ptab, ins["page_table"].rearrange("(a b) n -> a (b n)", a=1).broadcast_to([P, DEC * NPG])).then_inc(S("dsa_in"), 16)
            sp.dma_start(relb2[0:32, :], ins["rel_bias"]).then_inc(S("dsa_in"), 16)
            sp.wait_ge(S("bias_out"), 16)
            sp.wait_ge(S("bias_free"), 1)
            for h in range(0, AH, 4):
                src = bias_d[h:h + 4].rearrange("h p f -> h (p f)")[:, 127:127 + 383 * P].rearrange("h (p f) -> p h f", f=383)[:, :, 0:256]
                sp.dma_start(Mb_[:, h:h + 4, :], src).then_inc(S("Mb"), 16)

        def sp_dout(i):
            load_512(it_dout[i], ins["dsa_w_out"][0], 512 * i)

        def pool_pages():
            rows = [ins["cache_idx_k"][0].rearrange("a (t r) d -> (a t) (r d)", r=ROW)]
            rows += [ins[n][0].rearrange("a (t r) h d -> (a t) (r h d)", r=ROW) for n in ("cache_k", "cache_v")]
            pool.wait_ge(S("dsa_dve"), DVE_STEP["prow"])

            def page_rows(kind, dst, column, b2, nth, sem):
                pool.tensor_copy(pcol_[:, b2:b2 + 1], prow[:, ds(column, 1)]).then_inc(S("pcol"), 1)
                wait_alone(pool, S("pcol"), nth + 1)
                pool.indirect_dma_start(out=dst, out_offset=None, in_=rows[kind],
                                        in_offset=IndirectOffsetOnAxis(ap=pcol_[:, b2:b2 + 1], axis=0)).then_inc(sem, 16)
            with pool.Fori(0, 4) as jj:
                for u in range(4):
                    wait_alone(pool, S("ik_free"), jj * 4 + (u + 1))
                    for r in range(2):
                        page_rows(0, iraw[u % 2][:, 256 * r:256 * r + 256], jj * 8 + (2 * u + r), 2 * (u % 2) + r, jj * 8 + (2 * u + r), S(f"ik_in{u % 2}"))
            for kind, name, bufs, in_ in ((1, "kp", raw, ["kp_in0", "kp_in1"]), (2, "vp", vraw, [n for n, _ in vsem])):
                nb = len(bufs)
                with pool.Fori(0, 4) as jj:
                    for b in range(DEC):
                        wait_alone(pool, S(f"{name}_free"), jj * 8 + (b + 1))
                        page_rows(kind, bufs[b % nb].rearrange("p a b -> p (a b)"), jj * 8 + b, b % nb, jj * 8 + (32 * kind + b), S(in_[b % nb]))

        def pe_dsa():
            pe.wait_ge(S("h_ready"), 3)
            tiles = []
            for Pq in range(2):
                tiles += [("q", Pq, g) for g in range(4)] + [("kv", Pq, i) for i in range(2)]
            tiles += [("qi", 2, i) for i in range(4)] + [("ki", 2, 0)]
            for j, (kind, it, g) in enumerate(tiles):
                item = it_dsa[it]
                s = item[0]
                if j in (0, 6):
                    item_ready(pe, item)
                if j == 12:
                    item_ready(pe, item)
                    pe.wait_ge(S("dsa_small"), 32)
                if j >= 4:
                    pe.wait_ge(S("dproj_dve" if j % 2 == 0 else "dproj_act"), (j - 4) // 2 + 1)
                for k in range(KT):
                    if kind == "q":
                        for r in range(2):
                            m = pe.matmul(PS[64 * r:64 * r + 64, j % 4, 0:TOK], third(s, r)[:, k, g * 64:(g + 1) * 64],
                                          hT[:, k, 0:TOK], start=(k == 0), stop=(k == KT - 1), skip_group_check=True)
                        continue
                    elif kind == "qi":
                        lhsT = third(s, g // 2)[:, k, (g % 2) * P:(g % 2 + 1) * P]
                    else:
                        lhsT = third(s, 2)[:, k, g * P:(g + 1) * P]
                    m = pe.matmul(PS[:, j % 4, 0:TOK], lhsT, hT[:, k, 0:TOK], start=(k == 0), stop=(k == KT - 1))
                m.then_inc(S("dproj"), 1)
                if j in (5, 11):
                    pe.wait_ge(S("dproj"), j + 1)
                    pe.sem_inc(S(f"slot_used{s}"), 1)
            for T in range(3):
                n = P if T < 2 else DEC
                for k in range(KT):
                    m = pe.matmul(PS[0:n, 4, 8 * T:8 * T + 8], hT[:, k, T * P:T * P + n], third(s, 2)[:, k, 128:136], start=(k == 0), stop=(k == KT - 1))
            m.then_inc(S("dsa_pe"), 1)
            pe.wait_ge(S("dsa_pe"), PE_STEP["wi"])
            pe.sem_inc(S(f"slot_used{s}"), 1)
            pe.wait_ge(S("dproj_dve"), 9)
            pe.matmul(PS[:, 5, 0:TOK], K["blk64"], kiT, start=True, stop=True).then_inc(S("dsa_pe"), 1)
            pe.wait_ge(S("dsa_dve"), DVE_STEP["ki_sq"])
            pe.matmul(PS[:, 6, 0:TOK], K["blk64"], dsq, start=True, stop=True).then_inc(S("dsa_pe"), 1)
            pe.wait_ge(S("dsa_dve"), DVE_STEP["ki_ln"])
            for h in range(IH):
                if h >= 4:
                    pe.wait_ge(S("relu"), h - 3)
                elif h == 0:
                    pe.wait_ge(S("dproj_act"), 8)
                r = slice(64 * (h % 2), 64 * (h % 2) + 64)
                for T in range(2):
                    m = pe.matmul(PS[:, h % 4, P * T:P * T + P * (T + 1)], qiT[r, h // 2, T * P:(T + 1) * P], kiT[r, 0:P * (T + 1)], start=True, stop=True)
                m.then_inc(S("isc"), 1)
            for T in range(2):
                for i in range(2):
                    pe.transpose(PS[:, 4, 256 * T + P * i:256 * T + P * i + P], kT[:, i, T * P:(T + 1) * P], K["ident"])
                    pe.transpose(PS[:, 5, 256 * T + P * i:256 * T + P * i + P], vTt[:, i, T * P:(T + 1) * P], K["ident"])
                pe.transpose(PS[:, 6, 64 * T:64 * T + 64], kiT[0:64, T * P:(T + 1) * P], K["ident"][0:64, 0:64])
            for i in range(2):
                pe.transpose(PS[0:DEC, 7, P * i:P * i + P], kT[:, i, SEQ:TOK], K["ident"])
                pe.transpose(PS[0:DEC, 7, 256 + P * i:256 + P * i + P], vTt[:, i, SEQ:TOK], K["ident"])
            pe.transpose(PS[0:DEC, 6, 128:192], kiT[0:64, SEQ:TOK], K["ident"][0:64, 0:64]).then_inc(S("dsa_pe"), 1)
            pe.wait_ge(S("relu"), IH)
            pe.wait_ge(S("dsa_dve"), DVE_STEP["kv_tok"])
            for it in range(9):
                T, kv = it // 4, it % 4
                if it < 8:
                    if it >= 1:
                        pe.wait_ge(S("logit_sb"), it)
                    r = slice(64 * (kv % 2), 64 * (kv % 2) + 64)
                    for g in range(4):
                        m = pe.matmul(PS[:, g // 2, 256 * (g % 2):256 * (g % 2) + P * (T + 1)], qT[r, (kv // 2) * 4 + g, T * P:(T + 1) * P],
                                      kT[r, kv // 2, 0:P * (T + 1)], start=True, stop=True)
                    m.then_inc(S("asc"), 1)
                if it >= 1:
                    T, kv = (it - 1) // 4, (it - 1) % 4
                    b2 = (it - 1) % 2
                    pe.wait_ge(S("probs"), it)
                    for st in range(T + 1):
                        for g in range(4):
                            m = pe.transpose(PS[:, 4 + 2 * b2 + st, g * P:(g + 1) * P], A2[b2][:, g, st * P:(st + 1) * P], K["ident"])
                    m.then_inc(S("p_T"), 1)
                    pe.wait_ge(S("p_T_sb"), it)
                    if it == 5:
                        pe.wait_ge(S("att_o_sb"), 1)
                    for g in range(4):
                        ft = kv * 2 + g // 2
                        for st in range(T + 1):
                            m = pe.matmul(PS[64 * (g % 2):64 * (g % 2) + 64, 2 + ft // 4, (ft % 4) * P:(ft % 4 + 1) * P],
                                          vtk[:, st, kv * 64:(kv + 1) * 64], PTs[b2][:, st, g, :], start=(st == 0), stop=(st == T))
                    m.then_inc(S("pv"), 1)
            pe.wait_ge(S("att_o_sb"), 2)
            pe.sem_inc(S("ik_free"), 2)
            for i in range(4):
                m = pe.transpose(PS[0:DEC, 0, P * i:(i + 1) * P], qiT[:, i, SEQ:TOK], K["ident"])
            m.then_inc(S("dsa_pe"), 1)
            pe.wait_ge(S("dsa_dve"), DVE_STEP["qi8"])
            for r in range(2):
                for h in range(IH):
                    m = pe.matmul(PS[64 * r:64 * r + 64, 1, h * DEC:(h + 1) * DEC], qi8[0:DEC, h * 64:(h + 1) * 64], K["ident"][0:DEC, 0:DEC], start=True, stop=True)
            m = pe.matmul(PS[0:64, 2, 0:1], xi[0:DEC, :], K["ones"][0:DEC, :], start=True, stop=True)
            m.then_inc(S("dsa_pe"), 1)
            pe.wait_ge(S("dsa_dve"), DVE_STEP["Qb"])
            Qbv = Qb[:, 0:256].rearrange("p (u c) -> p u c", c=64)

            def turn_keys(jj, u):
                pe.wait_ge(S("ik_ord"), jj * 4 + (u + 1))
                for pg in range(4):
                    m = pe.transpose(PS[:, 4 + u % 2, pg * P:(pg + 1) * P], iord[u % 2][:, pg * P:(pg + 1) * P], K["ident"])
                m.then_inc(S("ik_free"), 1)

            def score_keys(jj, u):
                wait_alone(pe, S("ik_sb"), jj * 4 + (u + 1))
                pe.matmul(PS[0:64, ds(jj, 1), :].rearrange("p a b -> p (a b)"), Qbv[:, u, :], KTs[u % 2].rearrange("p a b -> p (a b)")[:, 0:512],
                          start=(u == 0), stop=(u == 3))
            turn_keys(0, 0)
            with pe.Fori(0, 3) as jj:
                for u in range(4):
                    turn_keys(jj + (u + 1) // 4, (u + 1) % 4)
                    score_keys(jj, u)
            for u in range(4):
                if u < 3:
                    turn_keys(3, u + 1)
                score_keys(3, u)
            for u in range(4):
                m = pe.matmul(PS[0:64, 6, 0:1], Qbv[:, u, :], kin2[:, u:u + 1], start=(u == 0), stop=(u == 3))
            m.then_inc(S("dsa_pe"), 1)
            pe.wait_ge(S("dsa_pe"), PE_STEP["ik_new"])
            pe.sem_inc(S("kp_free"), 2)
            pe.wait_ge(S("dsa_dve"), DVE_STEP["irelu"])
            for jj in range(4):
                q0 = 32 * (jj // 2)
                m = pe.matmul(PS[q0:q0 + DEC, jj, :], K["hsum"][0:64, :], Wx[0:64, jj * 512:(jj + 1) * 512], start=True, stop=True)
            m = pe.matmul(PS[32:32 + DEC, 6, 8:9], K["hsum"][0:64, :], Wx[0:64, 2048:2049], start=True, stop=True)
            m.then_inc(S("dsa_pe"), 1)
            pe.wait_ge(S("dsa_dve"), DVE_STEP["iscore_sb"])

            def turn_pages(jj, b):
                b2 = b % 2
                pe.wait_ge(S(f"kp_in{b2}"), jj * 64 + 16 * (b // 2 + 1))
                for Pq in range(2):
                    for pg in range(4):
                        m = pe.transpose(PS[:, 4 + 2 * b2 + Pq, pg * P:(pg + 1) * P], raw[b2][:, pg, Pq * P:(Pq + 1) * P], K["ident"])
                m.then_inc(S("kp_free"), 1)

            def score_pages(jj, b):
                pe.wait_ge(S("kp_sb"), jj * 8 + (b + 1))
                for Pq in range(2):
                    pe.matmul(PS[:, ds(jj, 1), :].rearrange("p a b -> p (a b)"), Qs[:, Pq, b * P:(b + 1) * P], KTs[b % 2][:, Pq, :],
                              start=(b == 0 and Pq == 0), stop=False, skip_group_check=True)
            turn_pages(0, 0)
            with pe.Fori(0, 3) as jj:
                for b in range(DEC):
                    turn_pages(jj + (b + 1) // DEC, (b + 1) % DEC)
                    score_pages(jj, b)
            for b in range(DEC):
                if b < DEC - 1:
                    turn_pages(3, b + 1)
                score_pages(3, b)
            for Pq in range(2):
                for b in range(DEC):
                    m = pe.matmul(PS[:, 4, 0:1], Qs[:, Pq, b * P:(b + 1) * P], kT[:, Pq, SEQ + b:SEQ + b + 1], start=(b == 0 and Pq == 0), stop=False, skip_group_check=True)
            m.then_inc(S("dsa_pe"), 1)
            pe.wait_ge(S("dsa_pe"), PE_STEP["k_mm"])
            pe.sem_inc(S("vp_free"), 6)
            ohs = K["ohs"]
            b31 = lambda n: ohs[0:32, 0:1].broadcast_to([32, n])
            for jj in range(4):
                pe.matmul(PS[:, jj, 0:384], rbx[0:32, :], b31(384), start=False, stop=False, skip_group_check=True)
                pe.matmul(PS[:, jj, 384:512], rbx[0:32, :], b31(128) if jj < 3 else ohs[0:32, 0:128], start=False, stop=False, skip_group_check=True)
            pe.matmul(PS[:, 4, 0:1], rbx[0:32, :], ohs[0:32, 128:129], start=False, stop=False, skip_group_check=True).then_inc(S("dsa_pe"), 1)
            pe.wait_ge(S("dsa_pe"), PE_STEP["dist"])
            pe.wait_ge(S("dsa_dve"), DVE_STEP["smask"])
            for jj in range(4):
                q = topk_half[jj // 2]
                pe.matmul(PS[:, jj, :], K["expand"][q, :], Wk_[q, jj % 2 * 512:(jj % 2 + 1) * 512], start=False, stop=True, skip_group_check=True)
            pe.matmul(PS[:, 4, 0:1], K["expand"][topk_half[1], :], Wk_[topk_half[1], 1024:1025], start=False, stop=True, skip_group_check=True).then_inc(S("dsa_pe"), 1)
            pe.wait_ge(S("dsa_dve"), DVE_STEP["sprob"])
            m = pe.matmul(PS[0:DEC, 0, 0:P], Qb[:, 0:DEC], K["ident"], start=True, stop=True)
            m.then_inc(S("dsa_pe"), 1)
            for q in range(4):
                for j in range(4):
                    m = pe.transpose(PS[:, 4 + q, j * P:(j + 1) * P], by_row(Sx[:, 512 * q:512 * (q + 1)])[:, j, :], K["ident"])
                m.then_inc(S("sp_T"), 1)
            pe.wait_ge(S("sp_T"), 4)
            pe.sem_inc(S("vp_free"), 2)
            pe.wait_ge(S("dsa_dve"), DVE_STEP["pn_sb"])
            def sums(b):
                return PS[32 * (b % 4):32 * (b % 4) + AH, 1, 256 * (b // 4):256 * (b // 4) + 256]
            for b in range(DEC):
                pe.matmul(sums(b), Pn[0:DEC, AH * b:AH * (b + 1)], v8[0:DEC, :], start=(b < 4), stop=False, skip_group_check=True)
            pe.wait_ge(S("sp_sb"), 4)
            for jj in range(4):
                for b in range(DEC):
                    pe.wait_ge(S(vsem[b][0]), vsem[b][1] + 16 * (jj + 1))
                    for pg in range(4):
                        m = pe.matmul(sums(b), PT[:, jj * 4 + pg, AH * b:AH * (b + 1)], vraw[b][:, pg, :], start=False, stop=(jj == 3 and pg == 3),
                                      skip_group_check=True)
                    m.then_inc(S("vp_free"), 1)
            pe.wait_ge(S("vp_free"), 40)
            pe.sem_inc(S("dsa_pe"), 1)
            pe.wait_ge(S("dsa_dve"), DVE_STEP["osel"])
            for b8 in range(2):
                m = pe.transpose(PS[:, 0, b8 * P:(b8 + 1) * P], Osel[:, b8 * P:(b8 + 1) * P], K["ident"])
            m.then_inc(S("dsa_pe"), 1)
            pe.wait_ge(S("mix_in"), 2)
            pe_out_proj(it_dout, oT, 1)

        def dve_dsa():
            dsts = [qT[:, 0], qT[:, 2], kT[:, 0], qT[:, 4], qT[:, 6], vTt[:, 0], qiT[:, 0], qiT[:, 2], kiT]
            for n, dst in enumerate(dsts):
                dve.wait_ge(S("dproj"), 2 * n + 1)
                dve.tensor_copy(dst, PS[:, (2 * n) % 4, 0:TOK]).then_inc(S("dproj_dve"), 1)
            dve.wait_ge(S("dsa_pe"), PE_STEP["wi"])
            dve.tensor_scalar(wtk, PS[:, 4, 0:16].rearrange("p (t h) -> p t h", h=IH), IH ** -0.5, None, ALU.mult)
            dv(dve.tensor_scalar(w8[0:DEC, :], PS[0:DEC, 4, 16:24], IH ** -0.5, None, ALU.mult))
            dve.wait_ge(S("dsa_pe"), PE_STEP["ki_mean"])
            dv(dve.tensor_tensor(kiT, kiT, PS[:, 5, 0:TOK], ALU.subtract))
            dve.tensor_tensor(dsq, kiT, kiT, ALU.mult).then_inc(S("dsa_dve"), 1)
            dve.wait_ge(S("ki_rms"), 1)
            dv(dve.reciprocal(lrs, lrs))
            dv(dve.tensor_tensor(kiT, kiT, lrs, ALU.mult))
            dve.tensor_scalar(kiT, kiT, vT[:, 46:47], vT[:, 47:48], ALU.mult, ALU.add).then_inc(S("dsa_dve"), 1)
            for h in range(IH):
                dve.wait_ge(S("relu"), h + 1)
                for T in range(2):
                    c = slice(P * T, P * T + P * (T + 1))
                    if h == 0:
                        ins_ = dve.tensor_scalar(sc[:, c], rl[h % 2][:, c], wtk[:, T, h:h + 1], None, ALU.mult)
                    else:
                        ins_ = dve.scalar_tensor_tensor(out=sc[:, c], in0=rl[h % 2][:, c], scalar=wtk[:, T, h:h + 1], in1=sc[:, c], op0=ALU.mult, op1=ALU.add)
                ins_.then_inc(S("isum"), 1)
                dve.wait_ge(S("isum"), h + 1)
            dve.tensor_tensor(sc[:, 0:P], sc[:, 0:P], K["cau"], ALU.add)
            dv(dve.tensor_tensor(sc[:, 256:384], sc[:, 256:384], K["cau"], ALU.add))
            dve.wait_ge(S("dsa_pe"), PE_STEP["kv_T"])
            dve.tensor_copy(ktk, PS[:, 4, :].rearrange("p (t n) -> p t n", t=2))
            dve.tensor_copy(vtk, PS[:, 5, :].rearrange("p (t n) -> p t n", t=2))
            dve.tensor_copy(kitk, PS[:, 6, 0:P].rearrange("p (t n) -> p t n", t=2))
            dve.tensor_copy(k8[0:DEC, :], PS[0:DEC, 7, 0:256])
            dve.tensor_copy(v8[0:DEC, :], PS[0:DEC, 7, 256:512])
            dve.tensor_copy(ki8[0:DEC, :], PS[0:DEC, 6, 128:192]).then_inc(S("dsa_dve"), 1)
            for rnd in range(8):
                src = sc if rnd == 0 else sw
                dve.max(m8[:, 0, :], src[:, 0:P])
                dv(dve.max(m8[:, 1, :], src[:, P:384]))
                dve.match_replace(sw[:, 0:P], m8[:, 0, :], src[:, 0:P], GONE)
                dv(dve.match_replace(sw[:, P:384], m8[:, 1, :], src[:, P:384], GONE))
            dv(dve.tensor_scalar(sw, sw, GONE, NEG, ALU.not_equal, ALU.mult))
            dve.tensor_tensor(sw[:, 0:P], sw[:, 0:P], K["cau"], ALU.add)
            dv(dve.tensor_tensor(sw[:, 256:384], sw[:, 256:384], K["cau"], ALU.add))
            dve.wait_ge(S("Mb"), 64)
            for it in range(8):
                T, kv = it // 4, it % 4
                n = P * (T + 1)
                a = A2[it % 2][:, :, 0:n]
                if it >= 2:
                    dve.wait_ge(S("p_T"), it - 1)
                dve.wait_ge(S("asc"), it + 1)
                src = PS[:, 0:2, :].rearrange("p b (g n) -> p (b g) n", g=2)[:, :, 0:n]
                dve.scalar_tensor_tensor(out=a, in0=src, scalar=DH ** -0.5, in1=Mb_[:, 4 * kv:4 * kv + 4, 256 - n:256], op0=ALU.mult, op1=ALU.add).then_inc(S("logit_sb"), 1)
                dve.wait_ge(S("logit_sb"), it + 1)
                dv(dve.tensor_tensor(a, a, bc(sw[:, P * T:P * T + n], 1, 4), ALU.add))
                dv(dve.tensor_reduce(mx, a, AX, ALU.max))
                dve.tensor_scalar(nm, mx, -1.0, None, ALU.mult).then_inc(S("nmax"), 1)
                dve.wait_ge(S("pexp"), it + 1)
                dv(dve.reciprocal(rs, rs))
                dve.tensor_tensor(a, a, bc(rs, 2, n), ALU.mult).then_inc(S("probs"), 1)
            dve.wait_ge(S("att_o_sb"), 2)
            dve.wait_ge(S("dsa_in"), 32)
            dv(dve.tensor_copy(Wx[:, 0:DEC * NPG], ptab))
            for g in range(4):
                q = slice(32 * g, 32 * g + 32)
                pages = Wx[q, 0:DEC * NPG].rearrange("p (b j g) -> p g j b", g=4, b=DEC)[:, g]
                ins_ = dve.tensor_scalar(Wx[q, 128:160].rearrange("p (j b) -> p j b", b=DEC), pages, float(PAGE // ROW), K["row"][q, :], ALU.mult, ALU.add)
            dv(ins_)
            dve.tensor_copy(prow, Wx[:, 128:160]).then_inc(S("dsa_dve"), 1)
            dve.memset(Qs, 0.0)
            dv(dve.memset(Qb, 0.0))
            for Pq in range(2):
                for r in range(2):
                    q = slice(64 * r, 64 * r + 64)
                    dst = Qs[q, Pq, :].rearrange("p (b x) -> p b x", x=144)[:, :, (2 * Pq + r) * 4:(2 * Pq + r) * 4 + 4]
                    dve.tensor_copy(dst, qT[q, 4 * Pq:4 * Pq + 4, SEQ:TOK].rearrange("p g b -> p b g"))
            for r in range(2):
                q = slice(64 * r, 64 * r + 64)
                ins_ = dve.tensor_copy(kin2[q, :], kiT[q, SEQ:TOK].rearrange("p (u r) -> p u r", r=2)[:, :, r])
            dve.tensor_tensor(xi[0:DEC, :].rearrange("p (b h) -> p b h", h=IH), bc(w8[0:DEC, :], 1, DEC), bc(K["ident"][0:DEC, 0:DEC], 2, IH), ALU.mult)
            dve.wait_ge(S("dsa_in"), 32)
            dv(dve.tensor_scalar(rbx[0:32, :].rearrange("p (b h) -> p b h", h=AH), bc(relb2[0:32, :], 1, DEC), DH ** 0.5, None, ALU.mult))
            dve.wait_ge(S("dsa_pe"), PE_STEP["qi8_T"])
            dve.tensor_copy(qi8[0:DEC, :], PS[0:DEC, 0, :]).then_inc(S("dsa_dve"), 1)
            dve.wait_ge(S("dsa_pe"), PE_STEP["qi_half"])
            for r in range(2):
                q = slice(64 * r, 64 * r + 64)
                dve.tensor_copy(Qb[q, :].rearrange("p (u x) -> p u x", x=80)[:, :, 8 * r:8 * r + 8],
                                PS[q, 1, 0:64].rearrange("p (h u r) -> p u h r", r=2, u=4)[:, :, :, r])
            dv(dve.tensor_copy(wS[0:64, :], PS[0:64, 2, 0:1]))
            dve.sem_inc(S("dsa_dve"), 1)
            dve.memset(m8, 0.0)
            dve.memset(Sk, -3e38)
            with dve.Fori(0, 4) as jj:
                for u in range(4):
                    dve.wait_ge(S(f"ik_in{u % 2}"), jj * 64 + 32 * (u // 2 + 1))
                    dve.tensor_copy(iord[u % 2].rearrange("p (r s d) -> p s r d", s=2, d=IDH),
                                    iraw[u % 2].rearrange("p (s r d) -> p s r d", s=2, d=IDH)).then_inc(S("ik_ord"), 1)
            dve.wait_ge(S("irelu0"), 1)
            dve.tensor_scalar(Wx[0:64, 0:2049], Wx[0:64, 0:2049], wS[0:64, :], None, ALU.mult).then_inc(S("dsa_dve"), 1)
            dve.wait_ge(S("dsa_pe"), PE_STEP["iscore"])
            for b, q in enumerate(topk_half):
                dve.tensor_copy(Sk[q, 0:1024], PS[q, 2 * b:2 * b + 2, :].rearrange("p b n -> p (b n)"))
            dve.tensor_copy(Sk[topk_half[1], 1024:1025], PS[topk_half[1], 6, 8:9]).then_inc(S("dsa_dve"), 1)
            dve.wait_ge(S("dsa_dve"), DVE_STEP["iscore_sb"])
            eight = m8[0:R2, 1, :]
            dv(dve.max(eight, Sk))
            dve.tensor_copy(best[:, 0:8], eight)
            dve.match_replace(Wk_, eight, Sk, GONE).then_inc(S("top_w"), 1)
            with dve.Fori(0, 31) as i:
                wait_alone(dve, S("top_w"), i + 1)
                dve.max(eight, Wk_).then_inc(S("top_m"), 1)
                wait_alone(dve, S("top_m"), i + 1)
                dve.tensor_copy(best[:, ds(i * 8 + 8, 8)], eight)
                dve.match_replace(Wk_, eight, Wk_, GONE).then_inc(S("top_w"), 1)
            dve.wait_ge(S("top_w"), 32)
            dv(dve.tensor_copy(rise, best[32:R2, ::-1]))
            a = best[0:DEC, :]
            dv(dve.tensor_tensor(Ek[0:DEC, 0:255], a[:, 0:255], rise[:, 1:256], ALU.min))
            dv(dve.tensor_tensor(Ek[0:DEC, 255:256], a[:, 255:256], rise[:, 0:1], ALU.max))
            dv(dve.tensor_reduce(thr[0:DEC], Ek[0:DEC, 0:256], AX, ALU.max))
            dv(dve.tensor_copy(thr[32:R2], thr[0:DEC]))
            dve.tensor_scalar(Wk_, Sk, thr, None, ALU.is_gt)
            dv(dve.tensor_scalar(Ek, Sk, thr, None, ALU.is_equal))
            dv(dve.tensor_reduce(ngt, Wk_, AX, ALU.add))
            dv(dve.tensor_tensor_scan(Sk, K["ones"][0:R2].broadcast_to([R2, HK]), Ek, 0.0, ALU.mult, ALU.add))
            dve.tensor_copy(neq[32:R2], Sk[0:DEC, HK - 1:HK])
            dv(dve.tensor_copy(nb_[0:DEC], ngt[32:R2]))
            dv(dve.tensor_tensor(need[0:DEC], ngt[0:DEC], nb_[0:DEC], ALU.add))
            dv(dve.tensor_scalar(need[0:DEC], need[0:DEC], -1.0, 256.0, ALU.mult, ALU.add))
            dv(dve.tensor_copy(need[32:R2], need[0:DEC]))
            dv(dve.tensor_tensor(need[32:R2], need[32:R2], neq[32:R2], ALU.subtract))
            dv(dve.scalar_tensor_tensor(out=Ek, in0=Sk, scalar=need, in1=Ek, op0=ALU.is_le, op1=ALU.mult))
            dv(dve.tensor_tensor(Wk_, Wk_, Ek, ALU.add))
            dve.tensor_scalar(Wk_, Wk_, 0.5, NEG, ALU.is_lt, ALU.mult).then_inc(S("dsa_dve"), 1)
            dve.wait_ge(S("dsa_pe"), PE_STEP["slogit"])
            dve.tensor_reduce(mxn[:, 0:1], PS[:, 0:4, :].rearrange("p b n -> p (b n)"), AX, ALU.max)
            dv(dve.tensor_copy(mxn[:, 1:2], PS[:, 4, 0:1]))
            dv(dve.tensor_tensor(mxn[:, 2:3], mxn[:, 0:1], mxn[:, 1:2], ALU.max))
            dve.tensor_scalar(mxn[:, 3:4], mxn[:, 2:3], -(DH ** -0.5), None, ALU.mult).then_inc(S("dsa_dve"), 1)
            dve.wait_ge(S("sexp"), 1)
            dv(dve.tensor_tensor(mxn[:, 0:1], mxn[:, 0:1], mxn[:, 1:2], ALU.add))
            dv(dve.reciprocal(mxn[:, 0:1], mxn[:, 0:1]))
            dv(dve.tensor_scalar(Sx[:, 0:2049], Sx[:, 0:2049], mxn[:, 0:1], None, ALU.mult))
            dve.tensor_scalar(Qb[:, 0:DEC], K["expt"], Sx[:, 2048:2049], None, ALU.mult).then_inc(S("dsa_dve"), 1)
            dve.wait_ge(S("dsa_pe"), PE_STEP["pn"])
            dve.tensor_copy(Pn[0:DEC, :], PS[0:DEC, 0, 0:P]).then_inc(S("dsa_dve"), 1)
            dv(dve.memset(Osel, 0.0))
            dve.wait_ge(S("dsa_pe"), PE_STEP["so_done"])
            for kv in range(KVH):
                for g in range(4):
                    q = slice(32 * g, 32 * g + AH)
                    dst = Osel[q, :].rearrange("p (b c d) -> p b c d", b=2, c=2)[:, :, 0]
                    src = PS[q, 1, :].rearrange("p (b k d) -> p k b d", b=2, k=KVH)[:, kv]
                    if kv == 0:
                        ins_ = dve.tensor_scalar(dst, src, K["kvsel"][q, 0:1], None, ALU.mult)
                    else:
                        ins_ = dve.scalar_tensor_tensor(out=dst, in0=src, scalar=K["kvsel"][q, kv:kv + 1], in1=dst, op0=ALU.mult, op1=ALU.add)
                dv(ins_)
            copies = Osel.rearrange("p (b c d) -> p b c d", b=2, c=2)
            dve.tensor_copy(copies[:, :, 1], copies[:, :, 0]).then_inc(S("dsa_dve"), 1)
            dve.wait_ge(S("dsa_pe"), PE_STEP["osel_T"])
            for r in range(2):
                q = slice(64 * r, 64 * r + 64)
                ins_ = dve.tensor_copy(oT[q, :, SEQ:TOK], PS[q, 0, 0:256].rearrange("p (b h) -> p h b", h=32)[:, r:AH:2, :])
            ins_.then_inc(S("mix_in"), 1)

        def act_dsa():
            dsts = [qT[:, 1], qT[:, 3], kT[:, 1], qT[:, 5], qT[:, 7], vTt[:, 1], qiT[:, 1], qiT[:, 3]]
            for n, dst in enumerate(dsts):
                act.wait_ge(S("dproj"), 2 * n + 2)
                act.copy(dst, PS[:, (2 * n + 1) % 4, 0:TOK]).then_inc(S("dproj_act"), 1)
            act.wait_ge(S("dsa_pe"), PE_STEP["ki_var"])
            act.activation(lrs, PS[:, 6, 0:TOK], ACT.Sqrt, bias=K["eps"]).then_inc(S("ki_rms"), 1)
            for h in range(IH):
                act.wait_ge(S("isc"), h + 1)
                if h >= 2:
                    act.wait_ge(S("isum"), h - 1)
                act.activation(rl[h % 2], PS[:, h % 4, 0:384], ACT.Relu, scale=IDH ** -0.5).then_inc(S("relu"), 1)
            act.wait_ge(S("dsa_dve"), DVE_STEP["kv_tok"])
            tokv = lambda t: t[0, 0].rearrange("(t p) h d -> p t (h d)", p=P)
            for dst, src in ((tokv(outs["k_p"]), ktk), (tokv(outs["v_p"]), vtk), (outs["ki_p"][0, 0].rearrange("(t p) d -> p t d", p=P), kitk),
                             (outs["k_s"][0, :, 0].rearrange("b h d -> b (h d)"), k8[0:DEC, :]), (outs["v_s"][0, :, 0].rearrange("b h d -> b (h d)"), v8[0:DEC, :]),
                             (outs["ki_s"][0, :, 0], ki8[0:DEC, :])):
                act.dma_start(dst, src).then_inc(S("kv_out"), 16)
            for it in range(8):
                T = it // 4
                n = P * (T + 1)
                act.wait_ge(S("nmax"), it + 1)
                for g in range(4):
                    ins_ = act.activation(A2[it % 2][:, g, 0:n], A2[it % 2][:, g, 0:n], ACT.Exp, bias=nm[:, g:g + 1], accum_out=rs[:, g:g + 1])
                ins_.then_inc(S("pexp"), 1)
                act.wait_ge(S("p_T"), it + 1)
                if it >= 2:
                    act.wait_ge(S("pv"), it - 1)
                act.copy(PTs[it % 2][:, 0:T + 1].rearrange("p s g t -> p s (g t)"), PS[:, 4 + 2 * (it % 2):5 + 2 * (it % 2) + T, :]).then_inc(S("p_T_sb"), 1)
                if it % 4 == 3:
                    act.wait_ge(S("pv"), it + 1)
                    act.copy(oT[:, :, T * P:(T + 1) * P], PS[:, 2:4, :].rearrange("p b (f t) -> p (b f) t", t=P)).then_inc(S("att_o_sb"), 1)
            with act.Fori(0, 4) as jj:
                for u in range(4):
                    act.wait_ge(S("ik_free"), jj * 4 + (u + 3))
                    act.copy(by_row(KTs[u % 2].rearrange("p a b -> p (a b)")[:, 0:512]), bank(4 + u % 2).rearrange("p (r n) -> p r n", r=ROW)).then_inc(S("ik_sb"), 1)
            act.wait_ge(S("dsa_pe"), PE_STEP["ik_new"])
            act.activation(Wx[0:64, 0:2048], PS[0:64, 0:4, :].rearrange("p b n -> p (b n)"), ACT.Relu, scale=IDH ** -0.5)
            act.activation(Wx[0:64, 2048:2049], PS[0:64, 6, 0:1], ACT.Relu, scale=IDH ** -0.5).then_inc(S("irelu0"), 1)
            with act.Fori(0, 4) as jj:
                for b in range(DEC):
                    act.wait_ge(S("kp_free"), jj * 8 + (b + 3))
                    act.copy(KTs[b % 2].rearrange("p q (n r) -> p q r n", r=ROW),
                             PS[:, 4 + 2 * (b % 2):6 + 2 * (b % 2), :].rearrange("p q (r n) -> p q r n", r=ROW)).then_inc(S("kp_sb"), 1)
            act.wait_ge(S("dsa_dve"), DVE_STEP["snmax"])
            act.activation(Sx[:, 0:2048], PS[:, 0:4, :].rearrange("p b n -> p (b n)"), ACT.Exp, bias=mxn[:, 3:4], scale=DH ** -0.5, accum_out=mxn[:, 0:1])
            act.activation(Sx[:, 2048:2049], PS[:, 4, 0:1], ACT.Exp, bias=mxn[:, 3:4], scale=DH ** -0.5, accum_out=mxn[:, 1:2]).then_inc(S("sexp"), 1)
            for q in range(4):
                act.wait_ge(S("sp_T"), q + 1)
                act.copy(PT[:, 4 * q:4 * q + 4, :], PS[:, 4 + q, :].rearrange("p (j c) -> p j c", c=P)).then_inc(S("sp_sb"), 1)
            act.wait_ge(S("kv_out"), 96)

        fin = arena[:, 2112:2112 + KT * TOK].rearrange("p (k t) -> p k t", k=KT)
        orow = [arena[:, 4400 + D * i:4400 + D * (i + 1)] for i in range(3)]

        def dve_final():
            dve.wait_ge(S("x_rms"), 5)
            dv(dve.reciprocal(rstd[:], rstd[:]))
            for k in range(KT):
                ins_ = dve.scalar_tensor_tensor(out=fin[:, k, :], in0=xT[:, k, :], scalar=vT[:, 32 + k:33 + k], in1=rstd[:], op0=ALU.mult, op1=ALU.mult)
            ins_.then_inc(S("dsa_dve"), 1)
            for T in range(TT):
                n = P if T < 2 else DEC
                dve.wait_ge(S("dsa_pe"), PE_STEP[f"rows{T}"])
                dve.tensor_copy(orow[T][0:n, :], PS[0:n, 2 + 2 * T:4 + 2 * T, :].rearrange("p b n -> p (b n)")).then_inc(S("dsa_dve"), 1)

        def pe_final():
            pe.wait_ge(S("dsa_dve"), DVE_STEP["final"])
            for T in range(TT):
                n = P if T < 2 else DEC
                for k in range(KT):
                    m = pe.transpose(PS[0:n, 2 + 2 * T + k // 4, (k % 4) * P:(k % 4 + 1) * P], fin[:, k, T * P:T * P + n], K["ident"])
                m.then_inc(S("dsa_pe"), 1)

        def sp_final():
            for T in range(TT):
                n = P if T < 2 else DEC
                sp.wait_ge(S("dsa_dve"), DVE_STEP[f"row{T}"])
                dst = outs["y_p"][0, T * P:(T + 1) * P, :] if T < 2 else outs["y_s"][:, 0, :]
                sp.dma_start(dst, orow[T][0:n, :]).then_inc(S("y_out"), 16)
            sp.wait_ge(S("y_out"), 48)
            sp.wait_ge(S("kv_out"), 96)

        @block.sync
        def _(sp_):
            sp_setup()
            sp_gla_small()
            sp_bias()
            sp_ada(0)
            sp_gla()
            sp_router(0)
            sp_moe(0)
            sp_ada(1)
            sp_experts_first(0)
            sp_experts(0)
            sp_dsa()
            sp_dout(0)
            sp_dout(1)
            sp_moe(1)
            sp_router(1)
            sp_experts_first(1)
            sp_experts(1)
            sp_final()

        @block.tensor
        def _(pe_):
            pe_setup()
            pe_bias(range(AH))
            pe_ada(0)
            pe_norm(0, norm_sq, 0)
            pe_gla()
            pe_route(0)
            pe_experts(0)
            pe_combine(0)
            pe_norm(2, norm_sq, 0)
            pe_dsa()
            pe_route(1)
            pe_experts(1)
            pe_combine(1)
            pe_norm(4, norm_sq, 0)
            pe_final()

        @block.vector
        def _(dve_):
            dve_setup()
            dve.sem_inc(S("setup_taken"), 1)
            dve.sem_inc(S("x_new"), 1)
            dve_bias(range(AH))
            dve_ada(0)
            dve_norm(0, 0, 0, 0)
            dve_gla()
            dve_out_proj(0)
            dve_norm(1, 0, 1, 0)
            dve_route(0)
            dve_experts(0)
            dve_combine(0)
            dve_norm(2, 1, 0, 0)
            dve.sem_inc(S("bias_free"), 1)
            dve_dsa()
            dve_out_proj(1)
            dve_norm(3, 1, 1, 0)
            dve_route(1)
            dve_experts(1)
            dve_combine(1)
            dve_final()

        @block.scalar
        def _(act_):
            act_setup()
            act_ada(0)
            act_norm(0, norm_sq, 0)
            act_gla()
            act_norm(1, norm_sq, 0)
            act_route(0)
            act_ada(1)
            act_experts(0)
            act_combine(0)
            act_norm(2, norm_sq, 0)
            act_dsa()
            act_norm(3, norm_sq, 0)
            act_route(1)
            act_experts(1)
            act_combine(1)
            act_norm(4, norm_sq, 0)

        @block.gpsimd
        def _(pool_):
            pool_bias()
            pool_gla()
            pool.wait_ge(S("out_pool"), 16)
            pool_experts(0)
            pool_pages()
            pool_experts(1)


_INS = ["x_prompt", "x_sample", "c_prompt", "c_sample", "state_gla", "cache_k", "cache_v", "cache_idx_k", "page_table",
        "rel_bias", "w_ada", "b_ada", "norm_mix", "norm_ffn", "norm_final", "gla_w_in", "gla_w_g2", "gla_b_g2",
        "gla_gnorm", "gla_w_out", "dsa_w_in", "dsa_idx_ln_g", "dsa_idx_ln_b", "dsa_w_out", "moe_w_router",
        "moe_router_bias", "moe_w_gate", "moe_w_up", "moe_w_down", "shared_w_gate", "shared_w_up", "shared_w_down"]
_OUTS = [("y_p", (1, SEQ, D)), ("y_s", (DEC, 1, D)), ("gla_p", (1, 1, GH, GDK, GDV)), ("gla_s", (1, DEC, GH, GDK, GDV)),
         ("k_p", (1, 1, SEQ, KVH, DH)), ("v_p", (1, 1, SEQ, KVH, DH)), ("ki_p", (1, 1, SEQ, IDH)),
         ("k_s", (1, DEC, 1, KVH, DH)), ("v_s", (1, DEC, 1, KVH, DH)), ("ki_s", (1, DEC, 1, IDH))]


def kernel(**inputs):
    import numpy as _np
    import concourse.bacc as _bacc
    from concourse import mybir as _mybir
    from concourse.bass_utils import run_bass_kernel_spmd as _run

    nc = _bacc.Bacc("TRN2", target_bir_lowering=False, num_devices=1)
    arrays, ins, outs = {}, {}, {}
    for name in _INS:
        a = _np.ascontiguousarray(inputs[name])
        arrays[f"in_{name}"] = a
        ins[name] = nc.dram_tensor(f"in_{name}", a.shape, _mybir.dt.from_np(a.dtype), kind="ExternalInput").ap()
    arrays["in_consts"] = constants()
    ins["consts"] = nc.dram_tensor("in_consts", (P, NCONST), F32, kind="ExternalInput").ap()
    arrays["in_onehot"] = distance_onehot()
    ins["onehot"] = nc.dram_tensor("in_onehot", (32, 384), F32, kind="ExternalInput").ap()
    for name, shape in _OUTS:
        outs[name] = nc.dram_tensor(f"out_{name}", shape, F32, kind="ExternalOutput").ap()
    build(nc, ins, outs)
    r = _run(nc, [arrays], core_ids=[0])
    return tuple(r.results[0][f"out_{name}"] for name, _ in _OUTS)
```
